# Optimizing a Trainium2 kernel written in Bass

```python
import math
import jax, jax.numpy as jnp
from jax import lax
import numpy as np

D_MODEL = 1024
BATCH = 1
SEQ = 512
DEPTH = 1

PLE_DIM = 256
SSD_WIDTH = D_MODEL // 2
ATT_WIDTH = D_MODEL - SSD_WIDTH
MIX_WIDTH = SSD_WIDTH + ATT_WIDTH
SSD_HEAD_DIM = 64
SSD_HEADS = SSD_WIDTH // SSD_HEAD_DIM
SSD_GROUPS = 2
SSD_STATE = 128
SSD_CONV = 4
SSD_CHUNK = 128
SSD_CONV_CH = SSD_WIDTH + 2 * SSD_GROUPS * SSD_STATE
SSD_NORM_EPS = 1e-5
ATT_HEAD_DIM = 64
ATT_HEADS = ATT_WIDTH // (2 * ATT_HEAD_DIM)
Q_BLOCK = 128
SUBLN_EPS = 1e-5
OFF_Z = 0
OFF_XBC = OFF_Z + SSD_WIDTH
OFF_DT = OFF_XBC + SSD_CONV_CH
OFF_Q = OFF_DT + SSD_HEADS
OFF_K = OFF_Q + ATT_WIDTH
OFF_V = OFF_K + ATT_WIDTH
IN_PROJ = OFF_V + ATT_WIDTH
N_EXPERTS = 32
TOP_K = 4
D_EXPERT = D_MODEL
SWIGLU_LIMIT = 7.0
SWIGLU_ALPHA = 1.702
EXPERT_BLOCK = 128
NORM_EPS = 1e-6

kernel_name = 'hybrid_ssd_diffattn_moe_ple'

def rms_norm(x, w, eps):
    xf = x.astype(jnp.float32)
    y = xf * lax.rsqrt(jnp.mean(xf * xf, axis=-1, keepdims=True) + eps)
    return (y * w.astype(jnp.float32)).astype(x.dtype)

def causal_depthwise_conv(u, w, b):
    k = w.shape[0]
    c = u.shape[-1]
    out = lax.conv_general_dilated(u, w[:, None, :].astype(u.dtype), window_strides=(1,),
                                   padding=((k - 1, 0),), dimension_numbers=('NWC', 'WIO', 'NWC'),
                                   feature_group_count=c)
    return out + b

def ssd_chunked(xdt, a_dt, b_mat, c_mat):
    bsz, seq, nh, hp = xdt.shape
    ng, ns = b_mat.shape[2], b_mat.shape[3]
    r = nh // ng
    nc = seq // SSD_CHUNK
    X = xdt.reshape(bsz, nc, SSD_CHUNK, ng, r, hp)
    A = a_dt.reshape(bsz, nc, SSD_CHUNK, ng, r).transpose(0, 3, 4, 1, 2)
    Bm = b_mat.reshape(bsz, nc, SSD_CHUNK, ng, ns)
    Cm = c_mat.reshape(bsz, nc, SSD_CHUNK, ng, ns)
    A_cum = jnp.cumsum(A, axis=-1)
    causal = jnp.tril(jnp.ones((SSD_CHUNK, SSD_CHUNK), dtype=bool))
    seg = A_cum[..., :, None] - A_cum[..., None, :]
    Lmat = jnp.where(causal, jnp.exp(jnp.where(causal, seg, 0.0)), 0.0)
    CB = jnp.einsum('bclgn,bcsgn->bgcls', Cm, Bm)
    y_diag = jnp.einsum('bgcls,bgrcls,bcsgrp->bclgrp', CB, Lmat, X)
    decay_states = jnp.exp(A_cum[..., -1:] - A_cum)
    states = jnp.einsum('bclgn,bgrcl,bclgrp->bcgrpn', Bm, decay_states, X)
    chunk_decay = jnp.exp(A_cum[..., -1])

    def step(h, inp):
        st, dec = inp
        return h * dec[..., None, None] + st, h

    init = jnp.zeros((bsz, ng, r, hp, ns), xdt.dtype)
    _, prev = lax.scan(step, init, (states.transpose(1, 0, 2, 3, 4, 5), chunk_decay.transpose(3, 0, 1, 2)))
    prev = prev.transpose(1, 0, 2, 3, 4, 5)
    y_off = jnp.einsum('bclgn,bcgrpn,bgrcl->bclgrp', Cm, prev, jnp.exp(A_cum))
    return (y_diag + y_off).reshape(bsz, seq, nh, hp)

def ssd_mixer(z, xbc, dt_raw, conv_w, conv_b, dt_bias, a_log, d_skip, norm_w):
    bsz, seq = z.shape[:2]
    xbc = jax.nn.silu(causal_depthwise_conv(xbc, conv_w, conv_b))
    xs = xbc[..., :SSD_WIDTH].reshape(bsz, seq, SSD_HEADS, SSD_HEAD_DIM).astype(jnp.float32)
    bm = xbc[..., SSD_WIDTH:SSD_WIDTH + SSD_GROUPS * SSD_STATE].reshape(bsz, seq, SSD_GROUPS, SSD_STATE).astype(jnp.float32)
    cm = xbc[..., SSD_WIDTH + SSD_GROUPS * SSD_STATE:].reshape(bsz, seq, SSD_GROUPS, SSD_STATE).astype(jnp.float32)
    dt = jax.nn.softplus(dt_raw.astype(jnp.float32) + dt_bias.astype(jnp.float32))
    a = -jnp.exp(a_log.astype(jnp.float32))
    y = ssd_chunked(xs * dt[..., None], a * dt, bm, cm)
    y = y + d_skip.astype(jnp.float32)[:, None] * xs
    y = y.reshape(bsz, seq, SSD_WIDTH) * jax.nn.silu(z.astype(jnp.float32))
    y = y.reshape(bsz, seq, SSD_GROUPS, SSD_WIDTH // SSD_GROUPS)
    y = y * lax.rsqrt(jnp.mean(y * y, axis=-1, keepdims=True) + SSD_NORM_EPS)
    y = y.reshape(bsz, seq, SSD_WIDTH) * norm_w.astype(jnp.float32)
    return y.astype(z.dtype)

def diff_attention(q, k, v, lam):
    seq = q.shape[1]
    scale = ATT_HEAD_DIM ** -0.5
    outs = []
    for blk in range(seq // Q_BLOCK):
        q0 = blk * Q_BLOCK
        q1 = q0 + Q_BLOCK
        s = jnp.einsum('bqhjd,bkhjd->bhjqk', q[:, q0:q1], k[:, :q1]).astype(jnp.float32) * scale
        qpos = q0 + jnp.arange(Q_BLOCK)[:, None]
        kpos = jnp.arange(q1)[None, :]
        s = jnp.where(kpos <= qpos, s, -jnp.inf)
        a = jax.nn.softmax(s, axis=-1)
        w = a[:, :, 0] - lam * a[:, :, 1]
        outs.append(jnp.einsum('bhqk,bkhe->bqhe', w.astype(v.dtype), v[:, :q1]))
    return jnp.concatenate(outs, axis=1)

def diff_attn_mixer(q, k, v, lam_q1, lam_k1, lam_q2, lam_k2, subln_w, lam_init):
    bsz, seq = q.shape[:2]
    q = q.reshape(bsz, seq, ATT_HEADS, 2, ATT_HEAD_DIM)
    k = k.reshape(bsz, seq, ATT_HEADS, 2, ATT_HEAD_DIM)
    v = v.reshape(bsz, seq, ATT_HEADS, 2 * ATT_HEAD_DIM)
    f32 = jnp.float32
    lam = (jnp.exp(jnp.sum(lam_q1.astype(f32) * lam_k1.astype(f32)))
           - jnp.exp(jnp.sum(lam_q2.astype(f32) * lam_k2.astype(f32))) + lam_init)
    o = diff_attention(q, k, v, lam)
    o = rms_norm(o, subln_w, SUBLN_EPS) * (1.0 - lam_init)
    return o.reshape(bsz, seq, ATT_WIDTH)

def moe_ffn(h, w_router, b_router, w_up, b_up, w_down, b_down):
    bsz, seq, d = h.shape
    t = h.reshape(-1, d)
    n_tok = t.shape[0]
    logits = (t @ w_router + b_router).astype(jnp.float32)
    top_val, top_idx = lax.top_k(logits, TOP_K)
    gates = jax.nn.softmax(top_val, axis=-1)
    n_assign = n_tok * TOP_K
    flat_e = top_idx.reshape(-1).astype(jnp.int32)
    flat_tok = jnp.repeat(jnp.arange(n_tok, dtype=jnp.int32), TOP_K)
    flat_g = gates.reshape(-1)
    order = jnp.argsort(flat_e, stable=True)
    se = flat_e[order]
    counts = jnp.bincount(flat_e, length=N_EXPERTS).astype(jnp.int32)
    padded = (counts + EXPERT_BLOCK - 1) // EXPERT_BLOCK * EXPERT_BLOCK
    start = jnp.cumsum(counts) - counts
    pend = jnp.cumsum(padded)
    pstart = pend - padded
    dest = pstart[se] + jnp.arange(n_assign, dtype=jnp.int32) - start[se]
    n_blocks = -(-n_assign // EXPERT_BLOCK) + N_EXPERTS
    n_rows = n_blocks * EXPERT_BLOCK
    row_tok = jnp.zeros((n_rows,), jnp.int32).at[dest].set(flat_tok[order])
    row_gate = jnp.zeros((n_rows,), jnp.float32).at[dest].set(flat_g[order])
    block_e = jnp.minimum(jnp.searchsorted(pend, jnp.arange(n_blocks, dtype=jnp.int32) * EXPERT_BLOCK, side='right'),
                          N_EXPERTS - 1).astype(jnp.int32)
    xs = t[row_tok].reshape(n_blocks, EXPERT_BLOCK, d)

    def expert_block(args):
        xb, e = args
        hu = xb @ w_up[e] + b_up[e]
        gate = jnp.minimum(hu[..., ::2], SWIGLU_LIMIT)
        up = jnp.clip(hu[..., 1::2], -SWIGLU_LIMIT, SWIGLU_LIMIT)
        act = (up + 1.0) * gate * jax.nn.sigmoid(SWIGLU_ALPHA * gate)
        return act @ w_down[e] + b_down[e]

    ys = lax.map(expert_block, (xs, block_e)).reshape(n_rows, d)
    out = jnp.zeros((n_tok, d), jnp.float32).at[row_tok].add(ys.astype(jnp.float32) * row_gate[:, None])
    return out.astype(h.dtype).reshape(bsz, seq, d)

def setup_inputs(seed: int = 0) -> dict:
    key = jax.random.key(seed)
    ks = jax.random.split(key, 32)
    f32 = jnp.float32
    nrm = lambda k, shape, s: jax.random.normal(k, shape, f32) * s
    gain = lambda k, shape: 1.0 + 0.02 * jax.random.normal(k, shape, f32)
    dt = jnp.exp(jax.random.uniform(ks[5], (DEPTH, SSD_HEADS), f32, math.log(1e-3), math.log(1e-1)))
    return {
        'x': nrm(ks[0], (BATCH, SEQ, D_MODEL), 1.0),
        'p': nrm(ks[1], (DEPTH, BATCH, SEQ, PLE_DIM), 1.0),
        'g_mix': gain(ks[2], (DEPTH, D_MODEL)),
        'w_in': nrm(ks[3], (DEPTH, D_MODEL, IN_PROJ), D_MODEL ** -0.5),
        'conv_w': nrm(ks[4], (DEPTH, SSD_CONV, SSD_CONV_CH), SSD_CONV ** -0.5),
        'conv_b': nrm(ks[6], (DEPTH, SSD_CONV_CH), 0.02),
        'dt_bias': dt + jnp.log(-jnp.expm1(-dt)),
        'a_log': jnp.log(jax.random.uniform(ks[7], (DEPTH, SSD_HEADS), f32, 1.0, 16.0)),
        'd_skip': gain(ks[8], (DEPTH, SSD_HEADS)),
        'ssd_norm_w': gain(ks[9], (DEPTH, SSD_WIDTH)),
        'lam_q1': nrm(ks[10], (DEPTH, ATT_HEAD_DIM), 0.1),
        'lam_k1': nrm(ks[11], (DEPTH, ATT_HEAD_DIM), 0.1),
        'lam_q2': nrm(ks[12], (DEPTH, ATT_HEAD_DIM), 0.1),
        'lam_k2': nrm(ks[13], (DEPTH, ATT_HEAD_DIM), 0.1),
        'subln_w': gain(ks[14], (DEPTH, 2 * ATT_HEAD_DIM)),
        'w_out': nrm(ks[15], (DEPTH, MIX_WIDTH, D_MODEL), MIX_WIDTH ** -0.5),
        'g_ffn': gain(ks[16], (DEPTH, D_MODEL)),
        'w_router': nrm(ks[17], (DEPTH, D_MODEL, N_EXPERTS), D_MODEL ** -0.5),
        'b_router': nrm(ks[18], (DEPTH, N_EXPERTS), 0.01),
        'w_up': nrm(ks[19], (DEPTH, N_EXPERTS, D_MODEL, 2 * D_EXPERT), D_MODEL ** -0.5),
        'b_up': nrm(ks[20], (DEPTH, N_EXPERTS, 2 * D_EXPERT), 0.02),
        'w_down': nrm(ks[21], (DEPTH, N_EXPERTS, D_EXPERT, D_MODEL), D_EXPERT ** -0.5),
        'b_down': nrm(ks[22], (DEPTH, N_EXPERTS, D_MODEL), 0.02),
        'g_ple': gain(ks[23], (DEPTH, D_MODEL)),
        'w_ple_gate': nrm(ks[24], (DEPTH, D_MODEL, D_MODEL), D_MODEL ** -0.5),
        'w_ple_proj': nrm(ks[25], (DEPTH, PLE_DIM, D_MODEL), PLE_DIM ** -0.5),
        'g_final': gain(ks[26], (D_MODEL,)),
    }

def reference(x, p, g_mix, w_in, conv_w, conv_b, dt_bias, a_log, d_skip, ssd_norm_w,
              lam_q1, lam_k1, lam_q2, lam_k2, subln_w, w_out, g_ffn, w_router, b_router,
              w_up, b_up, w_down, b_down, g_ple, w_ple_gate, w_ple_proj, g_final):
    for i in range(DEPTH):
        lam_init = 0.8 - 0.6 * math.exp(-0.3 * i)
        h = rms_norm(x, g_mix[i], NORM_EPS)
        proj = h @ w_in[i]
        y_ssd = ssd_mixer(proj[..., OFF_Z:OFF_XBC], proj[..., OFF_XBC:OFF_DT], proj[..., OFF_DT:OFF_Q],
                          conv_w[i], conv_b[i], dt_bias[i], a_log[i], d_skip[i], ssd_norm_w[i])
        y_att = diff_attn_mixer(proj[..., OFF_Q:OFF_K], proj[..., OFF_K:OFF_V], proj[..., OFF_V:IN_PROJ],
                                lam_q1[i], lam_k1[i], lam_q2[i], lam_k2[i], subln_w[i], lam_init)
        x = x + jnp.concatenate([y_ssd, y_att], axis=-1) @ w_out[i]
        x = x + moe_ffn(rms_norm(x, g_ffn[i], NORM_EPS), w_router[i], b_router[i],
                        w_up[i], b_up[i], w_down[i], b_down[i])
        gate = jax.nn.sigmoid(rms_norm(x, g_ple[i], NORM_EPS) @ w_ple_gate[i])
        x = x + (p[i] @ w_ple_proj[i]) * gate
    return rms_norm(x, g_final, NORM_EPS)


_drawn_inputs = setup_inputs


def setup_inputs(seed=0):
    import zlib

    import numpy as np

    out = dict(_drawn_inputs(seed))
    spreads = {}
    factors = {'d_skip': 2.949,
     'lam_q1': 8.0,
     'b_up': 6.932,
     'b_down': 7.925,
     'g_ple': 8.0,
     'g_final': 2.805}
    for name, (base, spread) in spreads.items():
        noise = np.random.default_rng([zlib.crc32(name.encode()), seed]).standard_normal(out[name].shape)
        drawn = base * np.exp(spread * noise) if base else spread * noise
        out[name] = __import__('jax').numpy.asarray(drawn.astype(out[name].dtype))
    for name, factor in factors.items():
        out[name] = (out[name] * factor).astype(out[name].dtype)
    return out
```

```python
import math
from contextlib import ExitStack

import concourse.bass as bass
from concourse import mybir

F32 = mybir.dt.float32
I32 = mybir.dt.int32
U32 = mybir.dt.uint32
ALU = mybir.AluOpType
ACT = mybir.ActivationFunctionType
AX = mybir.AxisListType.X

P = 128
BANK = 512

NORM_EPS = 1e-6
SUBLN_EPS = 1e-5
SSD_NORM_EPS = 1e-5
LAM_INIT = 0.8 - 0.6 * math.exp(-0.3 * 0)
SWIGLU_LIMIT = 7.0
SWIGLU_ALPHA = 1.702
MASKED = -1e30
N_CONSTS = 11
N_PARAMS = 8
N_LATE_PARAMS = 10
TAIL_ORDER = [(False, 0), (False, 1), (True, 0), (False, 2), (True, 1), (False, 3), (True, 2), (True, 3)]


def hybrid_ssd_diffattn_moe_ple_kernel(
    nc, x, p, g_mix, w_in, conv_w, conv_b, dt_bias, a_log, d_skip, ssd_norm_w,
    lam_q1, lam_k1, lam_q2, lam_k2, subln_w, w_out, g_ffn, w_router, b_router,
    w_up, b_up, w_down, b_down, g_ple, w_ple_gate, w_ple_proj, g_final, out,
):
    T, D = x.shape[1], x.shape[2]
    NT = T // P
    KD = D // P
    PLE = p.shape[3]
    SSD_W = ssd_norm_w.shape[1]
    NH = dt_bias.shape[1]
    HP = SSD_W // NH
    NG = 2
    HG = NH // NG
    NS = P
    CONV = conv_w.shape[1]
    CH = conv_w.shape[2]
    CT = CH // P
    XT = SSD_W // P
    ATT_W = D - SSD_W
    AH = 4
    DH = lam_q1.shape[1]
    VH = 2 * DH
    E = w_router.shape[2]
    TOPK = 4
    OFF_Z, OFF_XBC = 0, SSD_W
    OFF_DT = OFF_XBC + CH
    OFF_Q = OFF_DT + NH
    OFF_K = OFF_Q + ATT_W
    OFF_V = OFF_K + ATT_W

    B = 112
    PER_BANK = 4
    EXTRA = T * TOPK // B
    NB = E + EXTRA
    NCOL = NB + 2
    PEELED = 3
    EMPTY = 4096

    SLOT = 2048
    UP_SLOTS, DOWN_SLOTS = 8, 4
    SLOTS = UP_SLOTS + DOWN_SLOTS
    Y_BUFS = 3
    WCOL = SLOT // KD

    hn_rows = nc.dram_tensor("hn_rows", (T, D), F32).ap()
    y_rows = nc.dram_tensor("y_rows", (T * TOPK, D), F32).ap()

    x_v = x.rearrange("b (j p) d -> p (b j) d", p=P)
    out_v = out.rearrange("b (j p) d -> p (b j) d", p=P)
    hn_v = hn_rows.rearrange("(j p) d -> p j d", p=P)
    y_v = y_rows.rearrange("(j p r) d -> j p (r d)", p=P, r=TOPK)
    w_in_v = w_in.rearrange("o (k p) n -> p (o k) n", p=P)
    w_out_v = w_out.rearrange("o (k p) n -> p (o k) n", p=P)
    w_gate_v = w_ple_gate.rearrange("o (k p) n -> p (o k) n", p=P)
    w_proj_v = w_ple_proj.rearrange("o (k p) n -> p (o k) n", p=P)

    ctx = ExitStack()
    with ctx:
        def sb(name, shape, dt=F32):
            return ctx.enter_context(nc.sbuf_tensor(name, shape, dt))

        def sem(name):
            return ctx.enter_context(nc.semaphore(name))

        ring = sb("ring", [P, SLOTS, SLOT])
        xres = sb("xres", [P, NT, D])
        hT = sb("hT", [P, KD, T])
        xbcT = sb("xbcT", [P, CT, T])
        qkT = sb("qkT", [P, 2 * AH, T])
        zs = sb("zs", [P, NT, SSD_W])
        vt = sb("vt", [P, NT, ATT_W])
        work = sb("work", [P, 4608])

        ident = sb("ident", [P, P])
        upper = sb("upper", [P, P])
        strict = sb("strict", [P, P])
        ones = sb("ones", [P, P])
        attmask = sb("attmask", [P, P])
        iota = sb("iota", [P, P])
        token4_i = sb("token4_i", [P, NT], I32)
        token4 = sb("token4", [P, NT])

        gmix_t = sb("gmix_t", [P, KD])
        gffn_t = sb("gffn_t", [P, KD])
        gple_t = sb("gple_t", [P, KD])
        convw_t = sb("convw_t", [P, CONV, CT])
        convb_t = sb("convb_t", [P, CT])
        dtb = sb("dtb", [P, NH])
        alog = sb("alog", [P, NH])
        dskip = sb("dskip", [P, NH])
        normw = sb("normw", [P, SSD_W])
        subln = sb("subln", [P, VH])
        brt = sb("brt", [P, E])
        wdt = sb("wdt", [P, KD, NH])
        bup_t = sb("bup_t", [P, E * 2 * KD])
        bdn_t = sb("bdn_t", [P, E * KD])

        ssq = sb("ssq", [P, 20])
        rstd = sb("rstd", [P, 20])
        dts = sb("dts", [P, 12, NT * NH])
        lam_s = sb("lam_s", [P, 8])
        att_s = sb("att_s", [P, 2, 8])
        o_inv = sb("o_inv", [P, AH])
        gates = sb("gates", [P, NT, TOPK])
        pos_tab = sb("pos_tab", [P, NT, NCOL])
        val_tab = sb("val_tab", [P, NT, NCOL])
        block_expert = sb("block_expert", [P, NCOL], I32)
        extra_count = sb("extra_count", [P, 1], I32)
        out_idx = sb("out_idx", [P, NCOL], I32)
        gather_idx = sb("gather_idx", [P, 1], I32)
        scatter_idx = sb("scatter_idx", [P, 1], I32)

        def carve(buf, at, shape):
            n = 1
            for s in shape:
                n *= s
            v = buf[:, at:at + n]
            if len(shape) == 2:
                v = v.rearrange("p (a b) -> p a b", a=shape[0])
            if len(shape) == 3:
                v = v.rearrange("p (a b c) -> p a b c", a=shape[0], b=shape[1])
            return v

        hrow = carve(work, 0, [2, D])
        xs_tok = carve(work, 0, [SSD_W])
        xdt = carve(work, SSD_W, [SSD_W])
        xdec = carve(work, 2 * SSD_W, [SSD_W])
        b_tok = carve(work, 3 * SSD_W, [NG * NS])
        cb_mask = carve(work, 3 * SSD_W + 256, [NG, P])
        seg = carve(work, 4 * SSD_W, [NH, P])
        prevT = carve(work, 6 * SSD_W, [SSD_W])
        yrow = carve(work, 7 * SSD_W, [SSD_W])
        ysq = carve(work, 8 * SSD_W, [SSD_W])
        probs = carve(work, 0, [2, 2, T])
        wgt = carve(work, 4 * T, [2, T])
        wgtT = carve(work, 6 * T, [2, T])
        orow = carve(work, 8 * T, [ATT_W])
        logits = carve(work, 2048, [NT, E])
        top8 = carve(work, 2176, [NT, 8])
        topi_u = carve(work, 2208, [NT * 8]).bitcast(U32).rearrange("p (a b) -> p a b", a=NT)
        topi = carve(work, 2240, [NT, 8])
        chosen = carve(work, 2272, [NT, E])
        rankv = carve(work, 2400, [NT, E])
        onehot = carve(work, 2528, [NT, E])
        small = carve(work, 2656, [64])
        counts = carve(work, 2720, [E])
        extra = carve(work, 2752, [E])
        cum = carve(work, 2784, [E])
        blk_e = carve(work, 2816, [EXTRA])
        blk_b = carve(work, 2848, [EXTRA])
        sel = carve(work, 2880, [EXTRA, E])
        sel2 = carve(work, 2880 + EXTRA * E, [EXTRA, E])
        qk_flat = qkT[:, :, :].rearrange("p a b -> p (a b)")
        vt_flat = vt[:, :, :].rearrange("p a b -> p (a b)")
        zs_flat = zs[:, :, :].rearrange("p a b -> p (a b)")
        gate_s = carve(qk_flat, 0, [KD, B])
        up_s = carve(qk_flat, KD * B, [KD, B])
        sig_s = carve(qk_flat, 2 * KD * B, [KD, B])
        act_s = carve(qk_flat, 3 * KD * B, [KD, B])
        xT = carve(vt_flat, 0, [KD, B])
        yT = carve(vt_flat, KD * B, [KD, B])
        wrt = carve(zs_flat, 0, [KD, E])
        xg = zs_flat[:, 0:D]
        yg = zs_flat[:, D:2 * D]
        slot_hot = carve(work, 0, [NT, B])
        hT_flat = hT[:, :, :].rearrange("p a b -> p (a b)")
        xbc_flat = xbcT[:, :, :].rearrange("p a b -> p (a b)")
        p_rows = carve(hT_flat, 0, [NT, PLE])
        pT = carve(xbc_flat, 0, [2, T])
        gfin = xbc_flat[:, 2 * T:2 * T + D]
        w_proj_s = carve(xbc_flat, 2 * T + D, [2, D])
        pw = ring[:, 10:12, :].rearrange("p a (j n) -> p (a j) n", n=D)
        sig_t = carve(work, 2 * D, [2, D])
        squares = carve(qk_flat, 0, [D])
        lam_prod = carve(work, 4 * D, [2, DH])
        lamv = carve(work, 4 * D + 2 * DH, [4, DH])
        iota_i = work[:, 4 * D + 6 * DH:4 * D + 6 * DH + P].bitcast(I32)
        osq = xbcT[:, 0, :]
        out_row = carve(vt_flat, 0, [2, D])
        b_rows_up = zs_flat[0:E, 0:2 * D]
        b_rows_dn = vt_flat[0:E, 0:D]

        def dense(slot):
            return ring[:, slot, :].rearrange("p (k n) -> p k n", k=KD)

        ps = ctx.enter_context(nc.psum_tensor("ps", [P, 8, BANK], F32))

        x_loaded = [sem(f"x_loaded{j}") for j in range(NT)]
        gain_loaded = sem("gain_loaded")
        params_loaded = sem("params_loaded")
        late_params_loaded = sem("late_params_loaded")
        router_loaded = sem("router_loaded")
        bias_rows_loaded = sem("bias_rows_loaded")
        slot_loaded = [sem(f"slot_loaded{s}") for s in range(SLOTS)]
        consts_ready = sem("consts_ready")
        squared = sem("squared")
        scaled = sem("scaled")
        rooted = sem("rooted")
        normed = sem("normed")
        norm_turned = sem("norm_turned")
        norm_copied = sem("norm_copied")
        bias_turned = sem("bias_turned")
        bias_copied = sem("bias_copied")
        projected = sem("projected")
        conv_done = sem("conv_done")
        conv_silu = sem("conv_silu")
        proj_copied = sem("proj_copied")
        dt_projected = sem("dt_projected")
        dt_pre = sem("dt_pre")
        dt_e = sem("dt_e")
        dt_u = sem("dt_u")
        dt_l = sem("dt_l")
        adt_ready = sem("adt_ready")
        cum_ready = sem("cum_ready")
        cum_args = sem("cum_args")
        cum_exp = sem("cum_exp")
        ssd_turned = sem("ssd_turned")
        ssd_read = sem("ssd_read")
        seg_ready = sem("seg_ready")
        seg_exp = sem("seg_exp")
        decay_ready = sem("decay_ready")
        ssd_summed = sem("ssd_summed")
        state_updated = sem("state_updated")
        y_gated = sem("y_gated")
        y_squared = sem("y_squared")
        y_mean = sem("y_mean")
        y_root = sem("y_root")
        y_ssd_ready = sem("y_ssd_ready")
        mix_turned = sem("mix_turned")
        mix_copied = sem("mix_copied")
        lam_dots = sem("lam_dots")
        lam_exps = sem("lam_exps")
        scored = sem("scored")
        maxed = sem("maxed")
        expd = sem("expd")
        weighed = sem("weighed")
        w_turned = sem("w_turned")
        w_copied = sem("w_copied")
        attended = sem("attended")
        o_copied = sem("o_copied")
        o_squared = sem("o_squared")
        o_mean = sem("o_mean")
        o_root = sem("o_root")
        o_ready = sem("o_ready")
        mixed = sem("mixed")
        mixed_added = sem("mixed_added")
        hn_stored = [sem(f"hn_stored{j}") for j in range(NT)]
        routed = sem("routed")
        logits_read = sem("logits_read")
        top_shifted = sem("top_shifted")
        top_exp = sem("top_exp")
        chosen_ready = sem("chosen_ready")
        placed = sem("placed")
        tables_ready = sem("tables_ready")
        dve_step = sem("dve_step")
        act_step = sem("act_step")
        hot_ready = sem("hot_ready")
        idx_summed = sem("idx_summed")
        out_idx_ready = sem("out_idx_ready")
        gather_idx_ready = sem("gather_idx_ready")
        gather_started = sem("gather_started")
        scatter_started = sem("scatter_started")
        gathered = sem("gathered")
        x_turned = sem("x_turned")
        xT_ready = sem("xT_ready")
        up_used = sem("up_used")
        up_biased = sem("up_biased")
        gate_clamped = sem("gate_clamped")
        up_clamped = sem("up_clamped")
        sigmoided = sem("sigmoided")
        swish = sem("swish")
        act_ready = sem("act_ready")
        down_used = sem("down_used")
        yT_ready = sem("yT_ready")
        y_turned = sem("y_turned")
        y_ready = sem("y_ready")
        scatter_idx_ready = sem("scatter_idx_ready")
        scattered = sem("scattered")
        p_loaded = sem("p_loaded")
        pw_done = sem("pw_done")
        pw_copied = sem("pw_copied")
        tail_loaded = sem("tail_loaded")
        p_turned = sem("p_turned")
        p_copied = sem("p_copied")
        y_loaded = [sem(f"y_loaded{b}") for b in range(Y_BUFS)]
        y_summed = sem("y_summed")
        ple_done = sem("ple_done")
        gate_sig = sem("gate_sig")
        ple_added = sem("ple_added")
        out_ready = sem("out_ready")
        out_stored = [sem(f"out_stored{j}") for j in range(NT)]

        N_PROJ_CH = CT
        G_Z = CT
        G_QK = G_Z + NT
        G_V = G_QK + 2 * AH
        N_GROUPS = G_V + NT
        PER_CHUNK = (N_GROUPS - G_QK) // NT
        UNITS = NT * AH

        block = ctx.enter_context(nc.Block())

        @block.sync
        def _(sp):
            for j in range(NT):
                sp.dma_start(xres[:, j, :], x_v[:, j, :]).then_inc(x_loaded[j], 16)
            sp.wait_ge(gain_loaded, 16)
            sp.wait_ge(params_loaded, 16 * N_PARAMS)

            def load_dense(slot, src, col):
                sp.dma_start(dense(slot), src[:, :, col:col + WCOL]).then_inc(slot_loaded[slot], 16)

            cols = ([OFF_XBC + WCOL * i for i in range(4)] + [OFF_Z + WCOL * i for i in range(2)]
                    + [OFF_Q + WCOL * i for i in range(2)] + [OFF_K + WCOL * i for i in range(2)]
                    + [OFF_V + WCOL * i for i in range(2)])
            for s, col in enumerate(cols):
                load_dense(s, w_in_v, col)

            def load_up(e, c):
                sp.dma_start(ring[:, c, :], w_up[0, e, c * P:(c + 1) * P, :] if isinstance(e, int)
                             else w_up[0, bass.ds(e, 1), c * P:(c + 1) * P, :].rearrange("a p n -> (a p) n")
                             ).then_inc(slot_loaded[c], 16)

            def load_down(e, c):
                rows = slice(c * 2 * P, (c + 1) * 2 * P)
                src = (w_down[0, e, rows, :] if isinstance(e, int)
                       else w_down[0, bass.ds(e, 1), rows, :].rearrange("a q n -> (a q) n"))
                sp.dma_start(ring[:, UP_SLOTS + c, :].rearrange("p (f n) -> p f n", f=2),
                             src.rearrange("(f p) n -> p f n", p=P)).then_inc(slot_loaded[UP_SLOTS + c], 16)

            done = ([2 * i + 2 for i in range(4)] + [G_QK] * 2 + [G_QK + 2 * i + 2 for i in range(4)])
            for c in range(UP_SLOTS):
                sp.wait_ge(projected, done[c])
                load_up(0, c)
            for c in range(DOWN_SLOTS):
                sp.wait_ge(projected, (done + [N_GROUPS] * 2)[UP_SLOTS + c])
                load_dense(UP_SLOTS + c, w_out_v, WCOL * c)
            sp.wait_ge(mix_turned, NT)
            sp.dma_start(wrt, w_router.rearrange("o (k p) e -> p (o k) e", p=P)).then_inc(router_loaded, 16)
            for j in range(NT):
                sp.wait_ge(normed, NT + j + 1)
                sp.dma_start(hn_v[:, j, :], hrow[:, j % 2, :]).then_inc(hn_stored[j], 16)
            def load_block(i, e, before):
                for c in range(UP_SLOTS):
                    sp.wait_ge(up_used, (i - 1) * UP_SLOTS + c + 1)
                    load_up(e, c)
                for c in range(DOWN_SLOTS):
                    sp.wait_ge(down_used, (i - 1) * DOWN_SLOTS + c + 1)
                    load_down(before, c)

            for c in range(DOWN_SLOTS):
                sp.wait_ge(down_used, c + 1)
                load_down(0, c)
            sp.dma_start(p_rows, p.rearrange("o b (j p) c -> p (o b j) c", p=P)).then_inc(p_loaded, 16)
            for c in range(UP_SLOTS):
                sp.wait_ge(up_used, c + 1)
                load_up(1, c)
            sp.dma_start(w_proj_s, w_proj_v).then_inc(tail_loaded, 16)
            sp.dma_start(gfin, g_final.rearrange("(a n) -> a n", a=1).to_broadcast([P, D])).then_inc(tail_loaded, 16)
            for i in range(2, PEELED):
                load_block(i, i, i - 1)
            sp.wait_ge(tables_ready, 1)
            n = sp.value_load(extra_count[0:1, 0:1], min_val=0, max_val=EXTRA) + E
            with sp.Fori(PEELED, n) as i:
                e = sp.value_load(block_expert[0:1, bass.ds(i, 1)], min_val=0, max_val=E - 1)
                before = sp.value_load(block_expert[0:1, bass.ds(i - 1, 1)], min_val=0, max_val=E - 1)
                load_block(i, e, before)
            last = sp.value_load(block_expert[0:1, bass.ds(n - 1, 1)], min_val=0, max_val=E - 1)
            for c in range(DOWN_SLOTS):
                sp.wait_ge(down_used, (n - 1) * DOWN_SLOTS + c + 1)
                load_down(last, c)
            for c in range(4):
                sp.wait_ge(up_used, (n - 1) * UP_SLOTS + c + 1)
                load_dense(c, w_gate_v, WCOL * c)
            sp.wait_ge(down_used, (n + 1) * DOWN_SLOTS)
            sp.wait_ge(scattered, n * 16)
            for j in range(NT):
                if j >= Y_BUFS:
                    sp.wait_ge(y_summed, j - Y_BUFS + 1)
                s = 4 + 2 * (j % Y_BUFS)
                sp.dma_start(ring[:, s:s + 2, :].rearrange("p a n -> p (a n)"), y_v[j]).then_inc(y_loaded[j % Y_BUFS], 16)
            for j in range(NT):
                sp.wait_ge(out_ready, j + 1)
                sp.dma_start(out_v[:, j, :], out_row[:, j % 2, :]).then_inc(out_stored[j], 16)
            for j in range(NT):
                sp.wait_ge(out_stored[j], 16)

        @block.gpsimd
        def _(pool):
            n = 0

            def link(ins):
                nonlocal n
                n += 1
                ins.then_inc(consts_ready, 1)
                pool.wait_ge(consts_ready, n)

            link(nc.gpsimd.memset(ident[:], 0.0))
            link(nc.gpsimd.affine_select(out=ident[:], in_=ident[:], compare_op=ALU.not_equal, fill=1.0,
                                         base=0, pattern=[[-1, P]], channel_multiplier=1))
            link(nc.gpsimd.memset(ones[:], 1.0))
            link(nc.gpsimd.affine_select(out=upper[:], in_=ones[:], compare_op=ALU.is_ge, fill=0.0,
                                         base=0, pattern=[[1, P]], channel_multiplier=-1))
            link(nc.gpsimd.affine_select(out=strict[:], in_=ones[:], compare_op=ALU.is_gt, fill=0.0,
                                         base=0, pattern=[[1, P]], channel_multiplier=-1))
            link(nc.gpsimd.memset(attmask[:], 0.0))
            link(nc.gpsimd.affine_select(out=attmask[:], in_=attmask[:], compare_op=ALU.is_ge, fill=MASKED,
                                         base=0, pattern=[[-1, P]], channel_multiplier=1))
            link(nc.gpsimd.iota(iota_i, pattern=[[1, P]], base=0, channel_multiplier=0))
            link(nc.gpsimd.tensor_copy(iota[:], iota_i))
            link(nc.gpsimd.iota(token4_i[:], pattern=[[TOPK * P, NT]], base=0, channel_multiplier=TOPK))
            link(nc.gpsimd.tensor_copy(token4[:], token4_i[:]))
            assert n == N_CONSTS

            last_token = pool.alloc_register("last_token")
            pool.reg_mov(last_token, T - 1)
            last_row = pool.alloc_register("last_row")
            pool.reg_mov(last_row, T * TOPK - 1)

            def gather(i):
                pool.wait_ge(gather_idx_ready, i + 1)
                if not isinstance(i, int) or i >= 1:
                    pool.wait_ge(x_turned, i)
                pool.sem_inc(gather_started, 1)
                nc.gpsimd.indirect_dma_start(
                    xg[0:B, :], None, hn_rows, bass.IndirectOffsetOnAxis(ap=gather_idx[0:B, :], axis=0),
                    bounds_check=last_token, oob_is_err=False).then_inc(gathered, 16)

            def scatter(i):
                pool.wait_ge(y_ready, i + 1)
                pool.wait_ge(scatter_idx_ready, i + 1)
                pool.sem_inc(scatter_started, 1)
                nc.gpsimd.indirect_dma_start(
                    y_rows, bass.IndirectOffsetOnAxis(ap=scatter_idx[0:B, :], axis=0), yg[0:B, :], None,
                    bounds_check=last_row, oob_is_err=False).then_inc(scattered, 16)

            for j in range(NT):
                pool.wait_ge(hn_stored[j], 16)
            gather(0)
            gather(1)
            pool.wait_ge(tables_ready, 1)
            n_blocks = pool.value_load(extra_count[0:1, 0:1], min_val=0, max_val=EXTRA) + E
            gather(2)
            gather(3)
            scatter(0)
            gather(4)
            with pool.Fori(PEELED, n_blocks) as i:
                scatter(i - 2)
                gather(i + 2)
            scatter(n_blocks - 2)
            scatter(n_blocks - 1)
            pool.wait_ge(gathered, (n_blocks + 2) * 16)
            pool.wait_ge(scattered, n_blocks * 16)

        @block.scalar
        def _(act):
            steps = 0

            def link(ins):
                nonlocal steps
                steps += 1
                ins.then_inc(act_step, 1)
                act.wait_ge(act_step, steps)

            def row(v):
                return v.to_broadcast([P, v.shape[1]])

            with nc.allow_non_contiguous_dma(reason="small parameters by partition"):
                act.dma_start(gmix_t[:], g_mix.rearrange("o (k p) -> p (o k)", p=P)).then_inc(gain_loaded, 16)
                act.dma_start(wdt[:], w_in_v[:, :, OFF_DT:OFF_DT + NH]).then_inc(params_loaded, 16)
                act.dma_start(convb_t[:], conv_b.rearrange("o (k p) -> p (o k)", p=P)).then_inc(params_loaded, 16)
                for k in range(CONV):
                    act.dma_start(convw_t[:, k, :], conv_w[0, k].rearrange("(t p) -> p t", p=P)).then_inc(params_loaded, 16)
                act.dma_start(dtb[:], row(dt_bias)).then_inc(params_loaded, 16)
                act.dma_start(alog[:], row(a_log)).then_inc(params_loaded, 16)

            def load_late_params():
                with nc.allow_non_contiguous_dma(reason="small parameters by partition"):
                    act.dma_start(b_rows_up, b_up[0]).then_inc(bias_rows_loaded, 16)
                    act.dma_start(b_rows_dn, b_down[0]).then_inc(bias_rows_loaded, 16)
                    for dst, src in ((gffn_t, g_ffn), (gple_t, g_ple)):
                        act.dma_start(dst[:], src.rearrange("o (k p) -> p (o k)", p=P)).then_inc(late_params_loaded, 16)
                    for dst, src in ((dskip[:], d_skip), (normw[:], ssd_norm_w),
                                     (lamv[:, 0, :], lam_q1), (lamv[:, 1, :], lam_k1), (lamv[:, 2, :], lam_q2),
                                     (lamv[:, 3, :], lam_k2), (subln[:], subln_w), (brt[:], b_router)):
                        act.dma_start(dst, row(src)).then_inc(late_params_loaded, 16)

            def square_of_tile(col, j):
                if col >= 1:
                    act.wait_ge(squared, col)
                nc.scalar.activation(squares, xres[:, j, :], ACT.Square,
                                     accum_out=ssq[:, col:col + 1]).then_inc(squared, 1)

            def root_of_tile(col):
                act.wait_ge(scaled, col + 1)
                nc.scalar.activation(rstd[:, col:col + 1], ssq[:, col:col + 1], ACT.Sqrt).then_inc(rooted, 1)

            for j in range(NT):
                act.wait_ge(x_loaded[j], 16)
                square_of_tile(j, j)
            for j in range(NT):
                root_of_tile(j)
            load_late_params()
            act.wait_ge(params_loaded, 16 * N_PARAMS)
            link(nc.scalar.activation(alog[:], alog[:], ACT.Exp))
            for t in range(CT):
                act.wait_ge(conv_done, t + 1)
                nc.scalar.activation(xbcT[:, t, :], xbcT[:, t, :], ACT.Silu).then_inc(conv_silu, 1)
            act.wait_ge(dt_pre, 1)
            nc.scalar.activation(dts[:, 2, :], dts[:, 1, :], ACT.Exp).then_inc(dt_e, 1)
            act.wait_ge(dt_u, 1)
            nc.scalar.activation(dts[:, 4, :], dts[:, 3, :], ACT.Ln).then_inc(dt_l, 1)

            act.wait_ge(lam_dots, 1)
            nc.scalar.activation(lam_s[:, 2:4], lam_s[:, 0:2], ACT.Exp).then_inc(lam_exps, 1)

            def copy_group(g):
                act.wait_ge(projected, g + 1)
                bank = ps[:, g % 2, :]
                if g < G_QK:
                    ins = nc.scalar.activation(zs[:, g - G_Z, :], bank, ACT.Silu)
                elif g < G_QK + AH:
                    ins = nc.scalar.activation(qkT[:, g - G_QK, :], bank, ACT.Copy, scale=float(DH) ** -0.5)
                elif g < G_V:
                    ins = nc.scalar.activation(qkT[:, g - G_QK, :], bank, ACT.Copy)
                else:
                    ins = nc.scalar.activation(vt[:, g - G_V, :], bank, ACT.Copy)
                ins.then_inc(proj_copied, 1)

            for g in range(G_Z, G_QK):
                copy_group(g)
            act.wait_ge(cum_args, 1)
            nc.scalar.activation(dts[:, 8:11, :], dts[:, 8:11, :], ACT.Exp).then_inc(cum_exp, 1)

            g = G_QK
            for c in range(NT):
                act.wait_ge(seg_ready, c + 1)
                nc.scalar.activation(seg, seg, ACT.Exp).then_inc(seg_exp, 1)
                for _ in range(PER_CHUNK):
                    copy_group(g)
                    g += 1
                act.wait_ge(y_gated, c + 1)
                half = SSD_W // NG
                if c >= 1:
                    act.wait_ge(y_root, c)
                for q in range(NG):
                    ins = nc.scalar.activation(ysq[:, q * half:(q + 1) * half], yrow[:, q * half:(q + 1) * half],
                                               ACT.Square, accum_out=ssq[:, 16 + q:17 + q])
                    ins.then_inc(y_squared, 1)
                act.wait_ge(y_mean, c + 1)
                nc.scalar.activation(rstd[:, 16:16 + NG], ssq[:, 16:16 + NG], ACT.Sqrt).then_inc(y_root, 1)

            for c in range(NT):
                act.wait_ge(mix_turned, c + 1)
                nc.scalar.activation(hT[:, 0:XT, c * P:(c + 1) * P], ps[:, 6 + c % 2, :].rearrange("p (k t) -> p k t", k=XT),
                                     ACT.Copy).then_inc(mix_copied, 1)

            def exp_unit(u):
                nk = (u // AH + 1) * P
                for j in range(2):
                    s = 2 * u + j
                    act.wait_ge(maxed, s + 1)
                    if u >= 2:
                        act.wait_ge(weighed, u - 1)
                    nc.scalar.activation(probs[:, u % 2, j, 0:nk], ps[:, (u % 2) * 2 + j, 0:nk], ACT.Exp,
                                         bias=att_s[:, u % 2, j:j + 1],
                                         accum_out=att_s[:, u % 2, 2 + j:3 + j]).then_inc(expd, 1)

            def copy_w(u):
                nk = (u // AH + 1) * P
                act.wait_ge(w_turned, u + 1)
                if u >= 2:
                    act.wait_ge(attended, u - 1)
                nc.scalar.activation(wgtT[:, u % 2, 0:nk], ps[:, 4 + u % 2, 0:nk], ACT.Copy).then_inc(w_copied, 1)

            def square_o(b):
                act.wait_ge(o_copied, b + 1)
                if b >= 1:
                    act.wait_ge(o_squared, AH * b)
                for h in range(AH):
                    nc.scalar.activation(osq[:, h * VH:(h + 1) * VH],
                                         orow[:, h * VH:(h + 1) * VH], ACT.Square,
                                         accum_out=lam_s[:, 4 + h:5 + h]).then_inc(o_squared, 1)
                act.wait_ge(o_mean, b + 1)
                nc.scalar.activation(rstd[:, 16:16 + AH], lam_s[:, 4:4 + AH], ACT.Sqrt).then_inc(o_root, 1)

            def copy_o(b):
                act.wait_ge(mix_turned, NT + b + 1)
                nc.scalar.activation(hT[:, XT:KD, b * P:(b + 1) * P], ps[:, 6 + b % 2, :].rearrange("p (k t) -> p k t", k=AH),
                                     ACT.Copy).then_inc(mix_copied, 1)

            exp_unit(0)
            for u in range(UNITS):
                if u + 1 < UNITS:
                    exp_unit(u + 1)
                copy_w(u)
                if u % AH == 0 and u:
                    square_o(u // AH - 1)
                if u % AH == 2 and u > AH:
                    copy_o(u // AH - 1)
            square_o(NT - 1)
            copy_o(NT - 1)

            for j in range(NT):
                act.wait_ge(mixed_added, j + 1)
                square_of_tile(NT + j, j)
                root_of_tile(NT + j)
            act.wait_ge(top_shifted, 1)
            nc.scalar.activation(gates[:, :, :], gates[:, :, :], ACT.Exp).then_inc(top_exp, 1)

            def sigmoid_of(i):
                act.wait_ge(gate_clamped, i + 1)
                nc.scalar.activation(sig_s, gate_s, ACT.Sigmoid, scale=SWIGLU_ALPHA).then_inc(sigmoided, 1)

            def copy_y(i):
                act.wait_ge(y_turned, i + 1)
                if not isinstance(i, int) or i >= 1:
                    act.wait_ge(scattered, i * 16)
                nc.scalar.activation(yg[0:B, :].rearrange("p (a n) -> p a n", a=2), ps[0:B, 6:8, :],
                                     ACT.Copy).then_inc(y_ready, 1)

            act.wait_ge(tables_ready, 1)
            n_blocks = act.value_load(extra_count[0:1, 0:1], min_val=0, max_val=EXTRA) + E
            sigmoid_of(0)
            sigmoid_of(1)
            copy_y(0)
            sigmoid_of(2)
            with act.Fori(PEELED, n_blocks) as i:
                copy_y(i - 2)
                sigmoid_of(i)
            copy_y(n_blocks - 2)
            copy_y(n_blocks - 1)

            for j in range(NT):
                act.wait_ge(pw_done, j + 1)
                b = 2 * (j % 2)
                nc.scalar.activation(pw[:, j, :].rearrange("p (a n) -> p a n", a=2), ps[:, b:b + 2, :], ACT.Copy).then_inc(pw_copied, 1)
            for s, (final, j) in enumerate(TAIL_ORDER):
                if final:
                    act.wait_ge(ple_done, j + 1)
                    if j >= 2:
                        act.wait_ge(ple_added, j - 1)
                    b = 2 * (j % 2)
                    nc.scalar.activation(sig_t[:, j % 2, :].rearrange("p (a n) -> p a n", a=2), ps[:, b:b + 2, :],
                                         ACT.Sigmoid).then_inc(gate_sig, 1)
                    act.wait_ge(ple_added, j + 1)
                else:
                    act.wait_ge(y_summed, j + 1)
                square_of_tile(2 * NT + s, j)
                root_of_tile(2 * NT + s)

        @block.tensor
        def _(pe):
            mm = nc.tensor.matmul

            def turn_rows(stage, j):
                s = stage * NT + j
                pe.wait_ge(normed, s + 1)
                if s % NT >= 2:
                    pe.wait_ge(norm_copied, s - 1)
                for k in range(KD):
                    last = nc.tensor.transpose(ps[:, 4 + 2 * (j % 2) + k // 4, (k % 4) * P:(k % 4 + 1) * P],
                                               hrow[:, j % 2, k * P:(k + 1) * P], ident[:])
                last.then_inc(norm_turned, 1)

            pe.wait_ge(consts_ready, N_CONSTS)
            for j in range(NT):
                turn_rows(0, j)

            def project(g):
                if g >= 2:
                    if g - 2 < G_Z:
                        pe.wait_ge(conv_done, g - 1)
                    else:
                        pe.wait_ge(proj_copied, g - 1 - G_Z)
                bank = ps[:, g % 2, :]
                if g < G_Z or G_QK <= g < G_V:
                    t = g if g < G_Z else g - G_QK + 12
                    slot = t // 2
                    w = dense(slot)
                    if t % 2 == 0:
                        pe.wait_ge(slot_loaded[slot], 16)
                    for k in range(KD):
                        last = mm(bank, w[:, k, (t % 2) * P:(t % 2 + 1) * P], hT[:, k, :], start=(k == 0), stop=(k == KD - 1))
                else:
                    first, j = (4, g - G_Z) if g < G_QK else (10, g - G_V)
                    if j == 0:
                        pe.wait_ge(slot_loaded[first], 16)
                        pe.wait_ge(slot_loaded[first + 1], 16)
                    for s in range(2):
                        w = dense(first + s)
                        for k in range(KD):
                            last = mm(ps[:, g % 2, s * WCOL:(s + 1) * WCOL], hT[:, k, j * P:(j + 1) * P], w[:, k, :],
                                      start=(k == 0), stop=(k == KD - 1))
                last.then_inc(projected, 1)

            pe.wait_ge(norm_copied, NT)
            for g in range(CT):
                project(g)
            pe.wait_ge(bias_rows_loaded, 32)
            for s in range(2):
                for t in range(KD):
                    q = s * KD + t
                    nc.tensor.transpose(ps[:, 2, q * E:(q + 1) * E], b_rows_up[:, 2 * P * t + s:2 * P * (t + 1):2], ident[0:E, 0:E])
            for t in range(KD):
                last = nc.tensor.transpose(ps[:, 3, t * E:(t + 1) * E], b_rows_dn[:, t * P:(t + 1) * P], ident[0:E, 0:E])
            last.then_inc(bias_turned, 1)
            pe.wait_ge(bias_copied, 2)
            pe.wait_ge(params_loaded, 16 * N_PARAMS)
            for j in range(NT):
                for k in range(KD):
                    last = mm(ps[:, 2, j * NH:(j + 1) * NH], hT[:, k, j * P:(j + 1) * P], wdt[:, k, :],
                              start=(k == 0), stop=(k == KD - 1))
            last.then_inc(dt_projected, 1)
            for g in range(G_Z, G_QK):
                project(g)
            pe.wait_ge(adt_ready, 1)
            adt = dts[:, 6, :]
            mm(ps[:, 3, 0:NT * NH], upper[:], adt, start=True, stop=True)
            mm(ps[:, 3, NT * NH:2 * NT * NH], ones[:], adt, start=True, stop=True).then_inc(cum_ready, 1)

            def ssd_turn(c):
                tok = slice(c * P, (c + 1) * P)
                if c == 0:
                    pe.wait_ge(conv_silu, CT)
                    pe.wait_ge(cum_args, 1)
                else:
                    pe.wait_ge(ssd_read, c)
                    pe.wait_ge(seg_ready, c)
                    pe.wait_ge(state_updated, c)
                for t in range(XT):
                    nc.tensor.transpose(ps[:, 2, t * P:(t + 1) * P], xbcT[:, t, tok], ident[:])
                for q in range(NG):
                    nc.tensor.transpose(ps[:, 3, q * P:(q + 1) * P], xbcT[:, XT + q, tok], ident[:])
                for q in range(NG):
                    mm(ps[:, 3, (NG + q) * P:(NG + q + 1) * P], xbcT[:, XT + q, tok], xbcT[:, XT + NG + q, tok],
                       start=True, stop=True)
                for h in range(NH):
                    last = mm(ps[:, 4 + h // HG, (h % HG) * P:(h % HG + 1) * P],
                              dts[:, 6, c * NH + h:c * NH + h + 1].to_broadcast([P, P]), upper[:], start=True, stop=True)
                last.then_inc(ssd_turned, 1)

            def ssd_sum(c):
                tok = slice(c * P, (c + 1) * P)
                pe.wait_ge(decay_ready, c + 1)
                if c >= 1:
                    pe.wait_ge(y_gated, c)
                for h in range(NH):
                    mm(ps[:, 6, h * HP:(h + 1) * HP], seg[:, h, :], xdt[:, h * HP:(h + 1) * HP], start=True, stop=True)
                if c >= 1:
                    for q in range(NG):
                        mm(ps[:, 7, q * HG * HP:(q + 1) * HG * HP], xbcT[:, XT + NG + q, tok],
                           prevT[:, q * HG * HP:(q + 1) * HG * HP], start=True, stop=True)
                for q in range(NG):
                    last = mm(ps[:, 2, q * HG * HP:(q + 1) * HG * HP], b_tok[:, q * NS:(q + 1) * NS],
                              xdec[:, q * HG * HP:(q + 1) * HG * HP], start=True, stop=True)
                last.then_inc(ssd_summed, 1)

            g = G_QK
            for c in range(NT):
                ssd_turn(c)
                for _ in range(PER_CHUNK):
                    project(g)
                    g += 1
                ssd_sum(c)

            for c in range(NT):
                pe.wait_ge(y_ssd_ready, c + 1)
                if c < 2:
                    pe.wait_ge(y_gated, NT)
                else:
                    pe.wait_ge(mix_copied, c - 1)
                for t in range(XT):
                    last = nc.tensor.transpose(ps[:, 6 + c % 2, t * P:(t + 1) * P], zs[:, c, t * P:(t + 1) * P], ident[:])
                last.then_inc(mix_turned, 1)

            pe.wait_ge(proj_copied, N_GROUPS - G_Z)

            def score(u):
                b, h = u // AH, u % AH
                nk = (b + 1) * P
                for j in range(2):
                    if u >= 2:
                        pe.wait_ge(expd, 2 * (u - 2) + j + 1)
                    half = slice(j * DH, (j + 1) * DH)
                    mm(ps[:, (u % 2) * 2 + j, 0:nk], qkT[half, h, b * P:(b + 1) * P], qkT[half, AH + h, 0:nk],
                       start=True, stop=True).then_inc(scored, 1)

            def turn_w(u):
                b = u // AH
                pe.wait_ge(weighed, u + 1)
                if u >= 2:
                    pe.wait_ge(w_copied, u - 1)
                for k in range(b + 1):
                    last = nc.tensor.transpose(ps[:, 4 + u % 2, k * P:(k + 1) * P], wgt[:, u % 2, k * P:(k + 1) * P], ident[:])
                last.then_inc(w_turned, 1)

            def attend(u):
                b, h = u // AH, u % AH
                pe.wait_ge(w_copied, u + 1)
                if h == 0:
                    pe.wait_ge(mix_copied, NT if b < 2 else NT + b - 1)
                for k in range(b + 1):
                    last = mm(ps[:, 6 + b % 2, h * VH:(h + 1) * VH], wgtT[:, u % 2, k * P:(k + 1) * P],
                              vt[:, k, h * VH:(h + 1) * VH], start=(k == 0), stop=(k == b))
                last.then_inc(attended, 1)

            def turn_o(b):
                pe.wait_ge(o_ready, b + 1)
                for h in range(AH):
                    last = nc.tensor.transpose(ps[:, 6 + b % 2, h * P:(h + 1) * P], orow[:, h * VH:(h + 1) * VH], ident[:])
                last.then_inc(mix_turned, 1)

            score(0)
            score(1)
            for u in range(UNITS):
                if u + 2 < UNITS:
                    score(u + 2)
                turn_w(u)
                attend(u)
                if u % AH == 1 and u > AH:
                    turn_o(u // AH - 1)
            turn_o(NT - 1)

            pe.wait_ge(mix_copied, 2 * NT)
            for c in range(DOWN_SLOTS):
                pe.wait_ge(slot_loaded[UP_SLOTS + c], 32)
            for j in range(NT):
                if j >= 2:
                    pe.wait_ge(mixed_added, j - 1)
                for c in range(DOWN_SLOTS):
                    w = dense(UP_SLOTS + c)
                    for k in range(KD):
                        last = mm(ps[:, 2 * (j % 2) + c // 2, (c % 2) * WCOL:(c % 2 + 1) * WCOL],
                                  hT[:, k, j * P:(j + 1) * P], w[:, k, :], start=(k == 0), stop=(k == KD - 1))
                    if j == NT - 1:
                        last.then_inc(down_used, 1)
                if j < NT - 1:
                    last.then_inc(mixed, 1)
                if j >= 1:
                    turn_rows(1, j - 1)
            turn_rows(1, NT - 1)

            pe.wait_ge(norm_copied, 2 * NT)
            pe.wait_ge(mixed_added, NT)
            pe.wait_ge(router_loaded, 16)
            for j in range(NT):
                for k in range(KD):
                    last = mm(ps[:, 0, j * E:(j + 1) * E], xbcT[:, k, j * P:(j + 1) * P], wrt[:, k, :],
                              start=(k == 0), stop=(k == KD - 1))
            last.then_inc(routed, 1)
            pe.wait_ge(p_loaded, 16)
            for j in range(NT):
                for k in range(2):
                    last = nc.tensor.transpose(ps[:, 2 + k, j * P:(j + 1) * P], p_rows[:, j, k * P:(k + 1) * P], ident[:])
            last.then_inc(p_turned, 1)
            pe.wait_ge(chosen_ready, 1)
            for j in range(NT):
                for i in range(j + 1):
                    mm(ps[:, 1, j * E:(j + 1) * E], (strict if i == j else ones)[:], chosen[:, i, :],
                       start=(i == 0), stop=(i == j))
            for i in range(NT):
                last = mm(ps[:, 1, NT * E:(NT + 1) * E], ones[:], chosen[:, i, :], start=(i == 0), stop=(i == NT - 1))
            last.then_inc(placed, 1)

            def sum_idx(i):
                pe.wait_ge(hot_ready, i + 1)
                if not isinstance(i, int) or i >= 1:
                    pe.wait_ge(out_idx_ready, i)
                if not isinstance(i, int) or i >= 2:
                    pe.wait_ge(xT_ready, i)
                for j in range(NT):
                    last = mm(ps[0:B, 6, PER_BANK * B:PER_BANK * B + 1], slot_hot[:, j, :],
                              val_tab[:, j, bass.ds(i, 1)], start=(j == 0), stop=(j == NT - 1))
                last.then_inc(idx_summed, 1)

            def turn_x(i):
                pe.wait_ge(gathered, 16 * (i + 1))
                pe.wait_ge(out_idx_ready, 2 if isinstance(i, int) and i == 0 else i + 1)
                if not isinstance(i, int) or i >= 3:
                    pe.wait_ge(y_ready, i - 2)
                for k in range(KD):
                    last = nc.tensor.transpose(ps[:, 6 + k // PER_BANK, (k % PER_BANK) * B:(k % PER_BANK + 1) * B],
                                               xg[0:B, k * P:(k + 1) * P], ident[0:B, 0:B])
                last.then_inc(x_turned, 1)

            def up_chunk(i, k):
                if k == 0:
                    pe.wait_ge(xT_ready, i + 1)
                    if not isinstance(i, int) or i >= 1:
                        pe.wait_ge(up_biased, 2 * i)
                pe.wait_ge(slot_loaded[k], 16 * (i + 2))
                w = ring[:, k, :]
                for s in range(2):
                    for t in range(KD):
                        last = mm(ps[:, 2 * s + t // PER_BANK, (t % PER_BANK) * B:(t % PER_BANK + 1) * B],
                                  w[:, 2 * P * t + s:2 * P * (t + 1):2], xT[:, k, :],
                                  start=(k == 0 and t % PER_BANK == 0), stop=(k == KD - 1), skip_group_check=True)
                last.then_inc(up_used, 1)

            def down(i):
                pe.wait_ge(act_ready, i + 1)
                if not isinstance(i, int) or i >= 1:
                    pe.wait_ge(yT_ready, i)
                for c in range(DOWN_SLOTS):
                    pe.wait_ge(slot_loaded[UP_SLOTS + c], 16 * (i + 3))
                    w = ring[:, UP_SLOTS + c, :].rearrange("p (f n) -> p f n", f=2)
                    for f in range(2):
                        for t in range(KD):
                            last = mm(ps[:, 4 + t // PER_BANK, (t % PER_BANK) * B:(t % PER_BANK + 1) * B],
                                      w[:, f, t * P:(t + 1) * P], act_s[:, 2 * c + f, :],
                                      start=(c == 0 and f == 0 and t % PER_BANK == 0),
                                      stop=(c == DOWN_SLOTS - 1 and f == 1), skip_group_check=True)
                    last.then_inc(down_used, 1)

            def turn_y(i):
                pe.wait_ge(yT_ready, i + 1)
                pe.wait_ge(xT_ready, i + 3)
                pe.wait_ge(out_idx_ready, i + 4)
                if not isinstance(i, int) or i >= 1:
                    pe.wait_ge(y_ready, i)
                for k in range(KD):
                    last = nc.tensor.transpose(ps[0:B, 6 + k // 4, (k % 4) * P:(k % 4 + 1) * P], yT[:, k, :], ident[:])
                last.then_inc(y_turned, 1)

            def expert_step(i):
                static = isinstance(i, int)
                for k in range(KD // 2):
                    up_chunk(i, k)
                if not static or i >= 2:
                    turn_y(i - 2)
                for k in range(KD // 2, KD):
                    up_chunk(i, k)
                turn_x(i + 1)
                if not static or i >= 1:
                    down(i - 1)
                sum_idx(i + 2)

            sum_idx(0)
            sum_idx(1)
            turn_x(0)
            for i in range(PEELED):
                expert_step(i)
            pe.wait_ge(tables_ready, 1)
            n_blocks = pe.value_load(extra_count[0:1, 0:1], min_val=0, max_val=EXTRA) + E
            with pe.Fori(PEELED, n_blocks) as i:
                expert_step(i)
            turn_y(n_blocks - 2)
            down(n_blocks - 1)

            def project_p(j):
                if j >= 2:
                    pe.wait_ge(pw_copied, j - 1)
                for h in range(2):
                    for k in range(2):
                        last = mm(ps[:, 2 * (j % 2) + h, :], pT[:, k, j * P:(j + 1) * P], w_proj_s[:, k, h * BANK:(h + 1) * BANK],
                                  start=(k == 0), stop=(k == 1))
                last.then_inc(pw_done, 1)

            def project_gate(j):
                pe.wait_ge(norm_copied, 2 * NT + j + 1)
                if j >= 2:
                    pe.wait_ge(gate_sig, j - 1)
                else:
                    pe.wait_ge(pw_copied, NT)
                for c in range(4):
                    w = dense(c)
                    for k in range(KD):
                        last = mm(ps[:, 2 * (j % 2) + c // 2, (c % 2) * WCOL:(c % 2 + 1) * WCOL], hT[:, k, j * P:(j + 1) * P],
                                  w[:, k, :], start=(k == 0), stop=(k == KD - 1))
                last.then_inc(ple_done, 1)

            pe.wait_ge(up_biased, 2 * n_blocks)
            pe.wait_ge(tail_loaded, 32)
            pe.wait_ge(p_copied, 1)
            project_p(0)
            pe.wait_ge(yT_ready, n_blocks)
            pe.wait_ge(y_ready, n_blocks - 1)
            for k in range(KD):
                last = nc.tensor.transpose(ps[0:B, 6 + k // 4, (k % 4) * P:(k % 4 + 1) * P], yT[:, k, :], ident[:])
            last.then_inc(y_turned, 1)
            for j in range(1, NT):
                project_p(j)
            pe.wait_ge(y_ready, n_blocks)
            for c in range(4):
                pe.wait_ge(slot_loaded[c], 16 * (n_blocks + 2))
            turn_rows(2, 0)
            project_gate(0)
            for j in range(1, NT):
                turn_rows(2, j)
                project_gate(j)

        @block.vector
        def _(dve):
            v = nc.vector
            steps = 0

            def link(ins):
                nonlocal steps
                steps += 1
                ins.then_inc(dve_step, 1)
                dve.wait_ge(dve_step, steps)

            def heads(table):
                return table.unsqueeze(2).to_broadcast([P, NH, HP])

            def by_head(a):
                return a.rearrange("p (h e) -> p h e", h=NH)

            def rms(col, n, eps):
                dve.wait_ge(squared, col + 1)
                v.tensor_scalar(ssq[:, col:col + 1], ssq[:, col:col + 1], 1.0 / n, eps, ALU.mult, ALU.add).then_inc(scaled, 1)
                dve.wait_ge(rooted, col + 1)
                link(v.reciprocal(rstd[:, col:col + 1], rstd[:, col:col + 1]))

            def norm_rows(stage, j, col=None):
                s = stage * NT + j
                col = s if col is None else col
                rms(col, D, NORM_EPS)
                if j >= 2:
                    dve.wait_ge(norm_turned, s - 1)
                if stage == 1 and j >= 2:
                    dve.wait_ge(hn_stored[j - 2], 16)
                v.tensor_scalar(hrow[:, j % 2, :], xres[:, j, :], rstd[:, col:col + 1], None, ALU.mult).then_inc(normed, 1)

            def norm_copy(stage, j, dst, gain):
                s = stage * NT + j
                dve.wait_ge(norm_turned, s + 1)
                b = 4 + 2 * (j % 2)
                v.tensor_tensor(dst[:, :, j * P:(j + 1) * P],
                                ps[:, b:b + 2, :].rearrange("p a (k t) -> p (a k) t", k=4),
                                gain[:].unsqueeze(2).to_broadcast([P, KD, P]), ALU.mult).then_inc(norm_copied, 1)

            dve.wait_ge(gain_loaded, 16)
            norm_rows(0, 0)
            for j in range(NT):
                if j + 1 < NT:
                    norm_rows(0, j + 1)
                norm_copy(0, j, hT, gmix_t)

            dve.wait_ge(params_loaded, 16 * N_PARAMS)
            for t in range(CT):
                dve.wait_ge(projected, t + 1)
                u = ps[:, t % 2, :]
                link(v.tensor_scalar(xbcT[:, t, :], u, convw_t[:, CONV - 1, t:t + 1], convb_t[:, t:t + 1], ALU.mult, ALU.add))
                for k in range(CONV - 1):
                    back = CONV - 1 - k
                    ins = v.scalar_tensor_tensor(xbcT[:, t, back:T], u[:, 0:T - back], convw_t[:, k, t:t + 1],
                                                 xbcT[:, t, back:T], ALU.mult, ALU.add)
                    if k < CONV - 2:
                        link(ins)
                ins.then_inc(conv_done, 1)

            dve.wait_ge(bias_turned, 1)
            v.tensor_copy(bup_t[:].rearrange("p (e q) -> p q e", e=E),
                          ps[:, 2, :].rearrange("p (q e) -> p q e", e=E)).then_inc(bias_copied, 1)
            v.tensor_copy(bdn_t[:].rearrange("p (e q) -> p q e", e=E),
                          ps[:, 3, 0:KD * E].rearrange("p (q e) -> p q e", e=E)).then_inc(bias_copied, 1)

            NHT = NT * NH
            d = [dts[:, i, :] for i in range(12)]
            dve.wait_ge(dt_projected, 1)
            link(v.tensor_tensor(d[0].rearrange("p (j h) -> p j h", h=NH),
                                 ps[:, 2, 0:NHT].rearrange("p (j h) -> p j h", h=NH),
                                 dtb[:].unsqueeze(1).to_broadcast([P, NT, NH]), ALU.add))
            link(v.tensor_scalar(d[2], d[0], -1.0, None, ALU.mult))
            v.tensor_tensor(d[1], d[0], d[2], ALU.min).then_inc(dt_pre, 1)
            dve.wait_ge(dt_e, 1)
            v.tensor_scalar(d[3], d[2], 1.0, None, ALU.add).then_inc(dt_u, 1)
            dve.wait_ge(dt_u, 1)
            link(v.tensor_scalar(d[5], d[3], -1.0, None, ALU.add))
            link(v.tensor_scalar(d[7], d[5], 0.0, None, ALU.is_equal))
            link(v.tensor_tensor(d[5], d[5], d[7], ALU.add))
            link(v.reciprocal(d[5], d[5]))
            link(v.tensor_tensor(d[5], d[5], d[2], ALU.mult))
            dve.wait_ge(dt_l, 1)
            link(v.tensor_tensor(d[4], d[4], d[7], ALU.add))
            link(v.tensor_tensor(d[4], d[4], d[5], ALU.mult))
            link(v.tensor_scalar(d[0], d[0], 0.0, None, ALU.max))
            link(v.tensor_tensor(d[0], d[0], d[4], ALU.add))
            link(v.tensor_scalar(alog[:], alog[:], -1.0, None, ALU.mult))
            v.tensor_tensor(d[6].rearrange("p (j h) -> p j h", h=NH), d[0].rearrange("p (j h) -> p j h", h=NH),
                            alog[:].unsqueeze(1).to_broadcast([P, NT, NH]), ALU.mult).then_inc(adt_ready, 1)
            dve.wait_ge(late_params_loaded, 16 * N_LATE_PARAMS)
            for i in range(2):
                ins = v.tensor_tensor_reduce(out=lam_prod[:, i, :], in0=lamv[:, 2 * i, :], in1=lamv[:, 2 * i + 1, :],
                                             scale=1.0, scalar=0.0, op0=ALU.mult, op1=ALU.add,
                                             accum_out=lam_s[:, i:i + 1])
                if i == 0:
                    link(ins)
            ins.then_inc(lam_dots, 1)
            dve.wait_ge(lam_exps, 1)
            link(v.tensor_tensor(lam_s[:, 0:1], lam_s[:, 2:3], lam_s[:, 3:4], ALU.subtract))
            link(v.tensor_scalar(lam_s[:, 0:1], lam_s[:, 0:1], LAM_INIT, None, ALU.add))
            link(v.tensor_scalar(subln[:], subln[:], 1.0 - LAM_INIT, None, ALU.mult))

            dve.wait_ge(cum_ready, 1)
            link(v.tensor_copy(dts[:, 8, :], ps[:, 3, 0:NHT]))
            link(v.tensor_copy(dts[:, 10, :], ps[:, 3, NHT:2 * NHT]))
            link(v.tensor_scalar(dts[:, 11, :], d[8], -1.0, None, ALU.mult))
            v.tensor_tensor(dts[:, 9, :], d[10], d[8], ALU.subtract).then_inc(cum_args, 1)
            dve.wait_ge(cum_exp, 1)

            def hcol(i, c):
                return dts[:, i, c * NH:(c + 1) * NH]

            half = SSD_W // NG
            for c in range(NT):
                dve.wait_ge(ssd_turned, c + 1)
                link(v.tensor_copy(xs_tok, ps[:, 2, :]))
                link(v.tensor_copy(b_tok, ps[:, 3, 0:NG * NS]))
                v.tensor_tensor(cb_mask, ps[:, 3, NG * NS:].rearrange("p (q l) -> p q l", q=NG),
                                upper[:].unsqueeze(1).to_broadcast([P, NG, P]), ALU.mult).then_inc(ssd_read, 1)
                dve.wait_ge(ssd_read, c + 1)
                for h in range(NH):
                    ins = v.tensor_scalar(seg[:, h, :], ps[:, 4 + h // HG, (h % HG) * P:(h % HG + 1) * P],
                                          dts[:, 11, c * NH + h:c * NH + h + 1], 0.0, ALU.add, ALU.min)
                    if h < NH - 1:
                        link(ins)
                ins.then_inc(seg_ready, 1)
                link(v.tensor_tensor(by_head(xdt), by_head(xs_tok), heads(hcol(0, c)), ALU.mult))
                link(v.tensor_tensor(by_head(xdec), by_head(xdt), heads(hcol(9, c)), ALU.mult))
                link(v.tensor_tensor(by_head(xs_tok), by_head(xs_tok), heads(dskip[:]), ALU.mult))
                dve.wait_ge(seg_exp, c + 1)
                for q in range(NG):
                    ins = v.tensor_tensor(seg[:, q * HG:(q + 1) * HG, :], seg[:, q * HG:(q + 1) * HG, :],
                                          cb_mask[:, q:q + 1, :].to_broadcast([P, HG, P]), ALU.mult)
                    if q < NG - 1:
                        link(ins)
                ins.then_inc(decay_ready, 1)
                dve.wait_ge(ssd_summed, c + 1)
                dve.wait_ge(proj_copied, NT)
                if c >= 1:
                    link(v.tensor_tensor(by_head(yrow), by_head(ps[:, 7, :]), heads(hcol(8, c)), ALU.mult))
                    link(v.tensor_tensor(yrow, yrow, xs_tok, ALU.add))
                    link(v.tensor_tensor(yrow, ps[:, 6, :], yrow, ALU.add))
                else:
                    link(v.tensor_tensor(yrow, ps[:, 6, :], xs_tok, ALU.add))
                v.tensor_tensor(yrow, yrow, zs[:, c, :], ALU.mult).then_inc(y_gated, 1)
                if c == 0:
                    v.tensor_copy(prevT, ps[:, 2, :]).then_inc(state_updated, 1)
                else:
                    link(v.tensor_tensor(by_head(prevT), by_head(prevT), heads(hcol(10, c)), ALU.mult))
                    v.tensor_tensor(prevT, ps[:, 2, :], prevT, ALU.add).then_inc(state_updated, 1)
                dve.wait_ge(state_updated, c + 1)
                dve.wait_ge(y_squared, NG * (c + 1))
                v.tensor_scalar(ssq[:, 16:16 + NG], ssq[:, 16:16 + NG], 1.0 / half, SSD_NORM_EPS, ALU.mult, ALU.add).then_inc(y_mean, 1)
                dve.wait_ge(y_root, c + 1)
                link(v.reciprocal(att_s[:, 0, 0:NG], rstd[:, 16:16 + NG]))
                for q in range(NG):
                    cols = slice(q * half, (q + 1) * half)
                    ins = v.scalar_tensor_tensor(zs[:, c, cols], yrow[:, cols], att_s[:, 0, q:q + 1], normw[:, cols],
                                                 ALU.mult, ALU.mult)
                    if q < NG - 1:
                        link(ins)
                ins.then_inc(y_ssd_ready, 1)
                dve.wait_ge(y_ssd_ready, c + 1)

            def max_unit(u):
                b = u // AH
                nk = (b + 1) * P
                for j in range(2):
                    dve.wait_ge(scored, 2 * u + j + 1)
                    s = ps[:, (u % 2) * 2 + j, :]
                    link(v.tensor_tensor(s[:, b * P:nk], s[:, b * P:nk], attmask[:], ALU.add))
                    v.tensor_reduce(out=att_s[:, u % 2, j:j + 1], in_=s[:, 0:nk], axis=AX, op=ALU.max,
                                    negate=True).then_inc(maxed, 1)

            def weigh(u):
                nk = (u // AH + 1) * P
                a = att_s[:, u % 2, :]
                dve.wait_ge(expd, 2 * u + 2)
                link(v.reciprocal(a[:, 4:6], a[:, 2:4]))
                link(v.tensor_tensor(a[:, 5:6], a[:, 5:6], lam_s[:, 0:1], ALU.mult))
                if u >= 2:
                    dve.wait_ge(w_turned, u - 1)
                link(v.tensor_scalar(wgt[:, u % 2, 0:nk], probs[:, u % 2, 1, 0:nk], a[:, 5:6], None, ALU.mult))
                v.scalar_tensor_tensor(wgt[:, u % 2, 0:nk], probs[:, u % 2, 0, 0:nk], a[:, 4:5], wgt[:, u % 2, 0:nk],
                                       ALU.mult, ALU.subtract).then_inc(weighed, 1)

            def norm_o(b):
                dve.wait_ge(attended, AH * (b + 1))
                if b >= 1:
                    dve.wait_ge(mix_turned, NT + b)
                v.tensor_copy(orow, ps[:, 6 + b % 2, :]).then_inc(o_copied, 1)
                dve.wait_ge(o_squared, AH * (b + 1))
                v.tensor_scalar(lam_s[:, 4:4 + AH], lam_s[:, 4:4 + AH], 1.0 / VH, SUBLN_EPS, ALU.mult, ALU.add).then_inc(o_mean, 1)
                dve.wait_ge(o_root, b + 1)
                link(v.reciprocal(o_inv[:], rstd[:, 16:16 + AH]))
                for h in range(AH):
                    cols = slice(h * VH, (h + 1) * VH)
                    ins = v.scalar_tensor_tensor(orow[:, cols], orow[:, cols], o_inv[:, h:h + 1], subln[:], ALU.mult, ALU.mult)
                    if h < AH - 1:
                        link(ins)
                ins.then_inc(o_ready, 1)

            max_unit(0)
            for u in range(UNITS):
                if u + 1 < UNITS:
                    max_unit(u + 1)
                weigh(u)
                if u % AH == 0 and u:
                    norm_o(u // AH - 1)
            norm_o(NT - 1)

            for j in range(NT):
                if j < NT - 1:
                    dve.wait_ge(mixed, j + 1)
                else:
                    dve.wait_ge(down_used, DOWN_SLOTS)
                xj = xres[:, j, :].rearrange("p (a n) -> p a n", a=2)
                v.tensor_tensor(xj, ps[:, 2 * (j % 2):2 * (j % 2) + 2, :], xj, ALU.add).then_inc(mixed_added, 1)
                norm_rows(1, j)
                if j >= 1:
                    norm_copy(1, j - 1, xbcT, gffn_t)
            norm_copy(1, NT - 1, xbcT, gffn_t)

            dve.wait_ge(routed, 1)
            v.tensor_tensor(logits, ps[:, 0, 0:NT * E].rearrange("p (j e) -> p j e", e=E),
                            brt[:].unsqueeze(1).to_broadcast([P, NT, E]), ALU.add).then_inc(logits_read, 1)
            dve.wait_ge(logits_read, 1)
            for j in range(NT):
                link(v.max(top8[:, j, :], logits[:, j, :]))
            for j in range(NT):
                link(v.max_index(topi_u[:, j, :], top8[:, j, :], logits[:, j, :]))
            v.tensor_tensor(gates[:], top8[:, :, 0:TOPK], top8[:, :, 0:1].to_broadcast([P, NT, TOPK]),
                            ALU.subtract).then_inc(top_shifted, 1)
            link(v.tensor_copy(topi, topi_u))
            for r in range(TOPK):
                dst = chosen if r == 0 else onehot
                link(v.tensor_tensor(dst, iota[:, 0:E].unsqueeze(1).to_broadcast([P, NT, E]),
                                     topi[:, :, r:r + 1].to_broadcast([P, NT, E]), ALU.is_equal))
                if r == 1:
                    link(v.tensor_scalar(rankv, onehot, float(r), None, ALU.mult))
                elif r > 1:
                    link(v.scalar_tensor_tensor(rankv, onehot, float(r), rankv, ALU.mult, ALU.add))
                if r:
                    ins = v.tensor_tensor(chosen, chosen, onehot, ALU.add)
                    if r < TOPK - 1:
                        link(ins)
            ins.then_inc(chosen_ready, 1)
            link(v.tensor_tensor(rankv, rankv, token4[:].unsqueeze(2).to_broadcast([P, NT, E]), ALU.add))
            link(v.tensor_scalar(val_tab[:, :, 0:E], rankv, -float(EMPTY), None, ALU.add))
            dve.wait_ge(placed, 1)
            link(v.tensor_copy(counts, ps[:, 1, NT * E:(NT + 1) * E]))
            link(v.tensor_copy(onehot, ps[:, 1, 0:NT * E].rearrange("p (j e) -> p j e", e=E)))
            link(v.tensor_scalar(onehot, onehot, 1.0, None, ALU.add))
            link(v.tensor_tensor(onehot, onehot, chosen, ALU.mult))
            link(v.tensor_scalar(pos_tab[:, :, 0:E], onehot, -1.0, None, ALU.add))

            def hot(i):
                if not isinstance(i, int) or i >= 1:
                    dve.wait_ge(idx_summed, i)
                for j in range(NT):
                    ins = v.tensor_scalar(slot_hot[:, j, :], iota[:, 0:B], pos_tab[:, j, bass.ds(i, 1)], None, ALU.is_equal)
                ins.then_inc(hot_ready, 1)

            def indices(i):
                dve.wait_ge(idx_summed, i + 1)
                v.tensor_scalar(out_idx[0:B, bass.ds(i, 1)], ps[0:B, 6, PER_BANK * B:PER_BANK * B + 1],
                                float(EMPTY), None, ALU.add).then_inc(out_idx_ready, 1)
                dve.wait_ge(out_idx_ready, i + 1)
                if not isinstance(i, int) or i >= 1:
                    dve.wait_ge(gathered, 16 * i)
                v.tensor_scalar(gather_idx[0:B, :], out_idx[0:B, bass.ds(i, 1)], 2, None,
                                ALU.arith_shift_right).then_inc(gather_idx_ready, 1)

            dve.wait_ge(norm_turned, 2 * NT)
            for j in range(NT):
                dve.wait_ge(hn_stored[j], 16)
            link(v.memset(xg, 0.0))
            hot(0)
            indices(0)
            hot(1)
            indices(1)
            dve.wait_ge(p_turned, 1)
            v.tensor_copy(pT, ps[:, 2:4, :]).then_inc(p_copied, 1)

            def copy_x(i):
                dve.wait_ge(x_turned, i + 1)
                for a in range(2):
                    ks = slice(a * PER_BANK, (a + 1) * PER_BANK)
                    ins = v.tensor_tensor(xT[:, ks, :], ps[:, 6 + a, 0:PER_BANK * B].rearrange("p (k n) -> p k n", n=B),
                                          gffn_t[:, ks].unsqueeze(2).to_broadcast([P, PER_BANK, B]), ALU.mult)
                ins.then_inc(xT_ready, 1)

            def add_bias(i, e):
                dve.wait_ge(up_used, UP_SLOTS * (i + 1))
                for s, dst in enumerate((gate_s, up_s)):
                    for a in range(2):
                        ks = slice(a * PER_BANK, (a + 1) * PER_BANK)
                        at = e * (2 * KD) + s * KD + a * PER_BANK
                        ins = v.tensor_tensor(dst[:, ks, :], ps[:, 2 * s + a, 0:PER_BANK * B].rearrange("p (k n) -> p k n", n=B),
                                              bup_t[:, bass.ds(at, PER_BANK)].unsqueeze(2).to_broadcast([P, PER_BANK, B]), ALU.add)
                    ins.then_inc(up_biased, 1)

            def activate(i):
                dve.wait_ge(up_biased, 2 * (i + 1))
                v.tensor_scalar(gate_s, gate_s, SWIGLU_LIMIT, None, ALU.min).then_inc(gate_clamped, 1)
                v.tensor_scalar(up_s, up_s, -SWIGLU_LIMIT, SWIGLU_LIMIT, ALU.max, ALU.min).then_inc(up_clamped, 1)
                dve.wait_ge(gate_clamped, i + 1)
                dve.wait_ge(up_clamped, i + 1)
                v.scalar_tensor_tensor(up_s, up_s, 1.0, gate_s, ALU.add, ALU.mult).then_inc(swish, 1)

            def finish_act(i):
                dve.wait_ge(swish, i + 1)
                dve.wait_ge(sigmoided, i + 1)
                if not isinstance(i, int) or i >= 1:
                    dve.wait_ge(down_used, DOWN_SLOTS * (i + 1))
                v.tensor_tensor(act_s, up_s, sig_s, ALU.mult).then_inc(act_ready, 1)

            def copy_yT(i, e):
                dve.wait_ge(down_used, DOWN_SLOTS * (i + 2))
                if not isinstance(i, int) or i >= 1:
                    dve.wait_ge(y_turned, i)
                for a in range(2):
                    ks = slice(a * PER_BANK, (a + 1) * PER_BANK)
                    at = e * KD + a * PER_BANK
                    ins = v.tensor_tensor(yT[:, ks, :], ps[:, 4 + a, 0:PER_BANK * B].rearrange("p (k n) -> p k n", n=B),
                                          bdn_t[:, bass.ds(at, PER_BANK)].unsqueeze(2).to_broadcast([P, PER_BANK, B]), ALU.add)
                ins.then_inc(yT_ready, 1)

            def place_scatter(i):
                if not isinstance(i, int) or i >= 1:
                    dve.wait_ge(scattered, 16 * i)
                v.tensor_copy(scatter_idx[0:B, :], out_idx[0:B, bass.ds(i, 1)]).then_inc(scatter_idx_ready, 1)

            def expert_step(i, e, before2):
                if not isinstance(i, int) or i >= 2:
                    copy_yT(i - 2, before2)
                    place_scatter(i - 2)
                hot(i + 2)
                add_bias(i, e)
                copy_x(i + 1)
                activate(i)
                finish_act(i)
                indices(i + 2)

            copy_x(0)
            link(v.tensor_scalar(extra, counts, float(B), None, ALU.is_gt))
            for m in range(2, -(-T // B)):
                link(v.tensor_scalar(cum, counts, float(m * B), None, ALU.is_gt))
                link(v.tensor_tensor(extra, extra, cum, ALU.add))
            link(v.tensor_copy(cum, extra))
            for s in (1, 2, 4, 8, 16):
                link(v.tensor_copy(counts, cum))
                link(v.tensor_tensor(cum[:, s:E], counts[:, s:E], counts[:, 0:E - s], ALU.add))
            wide = [P, EXTRA, E]
            link(v.tensor_tensor(sel, cum.unsqueeze(1).to_broadcast(wide), iota[:, 0:EXTRA].unsqueeze(2).to_broadcast(wide), ALU.is_le))
            link(v.tensor_reduce(out=blk_e, in_=sel, axis=AX, op=ALU.add))
            link(v.tensor_tensor(sel, sel, extra.unsqueeze(1).to_broadcast(wide), ALU.mult))
            link(v.tensor_reduce(out=blk_b, in_=sel, axis=AX, op=ALU.add))
            link(v.tensor_tensor(blk_b, iota[:, 0:EXTRA], blk_b, ALU.subtract))
            link(v.tensor_scalar(blk_b, blk_b, 1.0, float(B), ALU.add, ALU.mult))
            link(v.tensor_tensor(sel, iota[:, 0:E].unsqueeze(1).to_broadcast(wide), blk_e.unsqueeze(2).to_broadcast(wide), ALU.is_equal))
            for j in range(NT):
                for src, dst in ((pos_tab, pos_tab), (val_tab, val_tab)):
                    link(v.tensor_tensor(sel2, sel, src[:, j, 0:E].unsqueeze(1).to_broadcast(wide), ALU.mult))
                    link(v.tensor_reduce(out=dst[:, j, E:NB], in_=sel2, axis=AX, op=ALU.add))
                link(v.tensor_tensor(pos_tab[:, j, E:NB], pos_tab[:, j, E:NB], blk_b, ALU.subtract))
            link(v.memset(pos_tab[:, :, NB:NCOL], -1.0))
            link(v.memset(val_tab[:, :, NB:NCOL], 0.0))
            link(v.tensor_copy(block_expert[:, 0:E], iota[:, 0:E]))
            link(v.tensor_scalar(blk_e, blk_e, float(E - 1), None, ALU.min))
            link(v.tensor_copy(block_expert[:, E:NB], blk_e))
            v.tensor_copy(extra_count[:], cum[:, E - 1:E]).then_inc(tables_ready, 1)
            dve.wait_ge(tables_ready, 1)

            dve.wait_ge(top_exp, 1)
            link(v.tensor_reduce(out=small[:, 0:NT], in_=gates[:], axis=AX, op=ALU.add))
            link(v.reciprocal(small[:, 0:NT], small[:, 0:NT]))
            link(v.tensor_tensor(gates[:], gates[:], small[:, 0:NT].unsqueeze(2).to_broadcast([P, NT, TOPK]), ALU.mult))
            for i in range(PEELED):
                expert_step(i, i, i - 2)
            n_blocks = dve.value_load(extra_count[0:1, 0:1], min_val=0, max_val=EXTRA) + E
            with dve.Fori(PEELED, n_blocks) as i:
                e = dve.value_load(block_expert[0:1, bass.ds(i, 1)], min_val=0, max_val=E - 1)
                before2 = dve.value_load(block_expert[0:1, bass.ds(i - 2, 1)], min_val=0, max_val=E - 1)
                expert_step(i, e, before2)
            for back in (2, 1):
                e = dve.value_load(block_expert[0:1, bass.ds(n_blocks - back, 1)], min_val=0, max_val=E - 1)
                copy_yT(n_blocks - back, e)
                place_scatter(n_blocks - back)

            def sum_experts(s, j):
                b = j % Y_BUFS
                dve.wait_ge(y_loaded[b], 16 * (j // Y_BUFS + 1))
                ys = ring[:, 4 + 2 * b:6 + 2 * b, :].rearrange("p a (r d) -> p (a r) d", d=D)
                for r in range(TOPK):
                    ins = v.scalar_tensor_tensor(xres[:, j, :], ys[:, r, :], gates[:, j, r:r + 1], xres[:, j, :], ALU.mult, ALU.add)
                    if r < TOPK - 1:
                        link(ins)
                ins.then_inc(y_summed, 1)
                norm_rows(2, j, s)
                norm_copy(2, j, hT, gple_t)

            def add_ple(j):
                dve.wait_ge(gate_sig, j + 1)
                link(v.tensor_tensor(sig_t[:, j % 2, :], pw[:, j, :], sig_t[:, j % 2, :], ALU.mult))
                v.tensor_tensor(xres[:, j, :], xres[:, j, :], sig_t[:, j % 2, :], ALU.add).then_inc(ple_added, 1)

            def finish_tile(s, j):
                rms(s, D, NORM_EPS)
                if j >= 2:
                    dve.wait_ge(out_stored[j - 2], 16)
                v.scalar_tensor_tensor(out_row[:, j % 2, :], xres[:, j, :], rstd[:, s:s + 1], gfin, ALU.mult, ALU.mult).then_inc(out_ready, 1)

            for s, (final, j) in enumerate(TAIL_ORDER):
                if final:
                    add_ple(j)
                    finish_tile(2 * NT + s, j)
                else:
                    sum_experts(2 * NT + s, j)


_INS = ['x', 'p', 'g_mix', 'w_in', 'conv_w', 'conv_b', 'dt_bias', 'a_log', 'd_skip', 'ssd_norm_w',
        'lam_q1', 'lam_k1', 'lam_q2', 'lam_k2', 'subln_w', 'w_out', 'g_ffn', 'w_router', 'b_router',
        'w_up', 'b_up', 'w_down', 'b_down', 'g_ple', 'w_ple_gate', 'w_ple_proj', 'g_final']


def kernel(**inputs):
    import numpy as _np
    import concourse.bacc as _bacc
    from concourse import mybir as _mybir
    from concourse.bass_utils import run_bass_kernel_spmd as _run

    nc = _bacc.Bacc("TRN2", target_bir_lowering=False, num_devices=1)
    arrays, args = {}, []
    for name in _INS:
        a = _np.ascontiguousarray(inputs[name])
        arrays[f"in_{name}_dram"] = a
        args.append(nc.dram_tensor(f"in_{name}_dram", a.shape, _mybir.dt.from_np(a.dtype), kind="ExternalInput").ap())
    shape = tuple(inputs["x"].shape)
    args.append(nc.dram_tensor("out_0_dram", shape, _mybir.dt.float32, kind="ExternalOutput").ap())
    hybrid_ssd_diffattn_moe_ple_kernel(nc, *args)
    r = _run(nc, [arrays], core_ids=[0])
    return r.results[0]["out_0_dram"]
```

```python
import math
from contextlib import ExitStack

import concourse.bass as bass
from concourse import mybir

F32 = mybir.dt.float32
F32R = mybir.dt.float32r
I32 = mybir.dt.int32
U32 = mybir.dt.uint32
ALU = mybir.AluOpType
ACT = mybir.ActivationFunctionType
AX = mybir.AxisListType.X

P = 128
BANK = 512

NORM_EPS = 1e-6
SUBLN_EPS = 1e-5
SSD_NORM_EPS = 1e-5
LAM_INIT = 0.8 - 0.6 * math.exp(-0.3 * 0)
SWIGLU_LIMIT = 7.0
SWIGLU_ALPHA = 1.702
MASKED = -1e30
N_CONSTS = 13
N_PARAMS = 8
N_LATE_PARAMS = 9
TAIL_ORDER = [(False, 0), (False, 1), (True, 0), (False, 2), (True, 1), (False, 3), (True, 2), (True, 3)]


def hybrid_ssd_diffattn_moe_ple_kernel(
    nc, x, p, g_mix, w_in, conv_w, conv_b, dt_bias, a_log, d_skip, ssd_norm_w,
    lam_q1, lam_k1, lam_q2, lam_k2, subln_w, w_out, g_ffn, w_router, b_router,
    w_up, b_up, w_down, b_down, g_ple, w_ple_gate, w_ple_proj, g_final, out,
):
    T, D = x.shape[1], x.shape[2]
    NT = T // P
    KD = D // P
    PLE = p.shape[3]
    SSD_W = ssd_norm_w.shape[1]
    NH = dt_bias.shape[1]
    HP = SSD_W // NH
    NG = 2
    HG = NH // NG
    NS = P
    CONV = conv_w.shape[1]
    CH = conv_w.shape[2]
    CT = CH // P
    XT = SSD_W // P
    ATT_W = D - SSD_W
    AH = 4
    DH = lam_q1.shape[1]
    VH = 2 * DH
    E = w_router.shape[2]
    TOPK = 4
    OFF_Z, OFF_XBC = 0, SSD_W
    OFF_DT = OFF_XBC + CH
    OFF_Q = OFF_DT + NH
    OFF_K = OFF_Q + ATT_W
    OFF_V = OFF_K + ATT_W

    B = P
    EXTRA = T * TOPK // B
    NB = E + EXTRA
    NCOL = NB + 2
    PEELED = 3
    EMPTY = 4096

    UP_CHUNKS, DOWN_CHUNKS = KD, KD // 2
    UP_WHOLE, DOWN_WHOLE = (3, 7), (0,)
    UP_SPLIT = [k for k in range(UP_CHUNKS) if k not in UP_WHOLE]
    DOWN_SPLIT = [c for c in range(DOWN_CHUNKS) if c not in DOWN_WHOLE]
    SPLITS = UP_SPLIT + DOWN_SPLIT
    PARTS = 3
    assert len(SPLITS) % PARTS == 0 and len(DOWN_SPLIT) == PARTS

    SLOT = 2048
    SLOTS = 12
    RING = 6
    OUT_SLOT = 8
    Y_BUFS = 3
    WCOL = SLOT // KD

    hn_rows = nc.dram_tensor("hn_rows", (T, D), F32).ap()
    y_rows = nc.dram_tensor("y_rows", (T * TOPK, D), F32).ap()

    x_v = x.rearrange("b (j p) d -> p (b j) d", p=P)
    out_v = out.rearrange("b (j p) d -> p (b j) d", p=P)
    hn_v = hn_rows.rearrange("(j p) d -> p j d", p=P)
    y_v = y_rows.rearrange("(j p r) d -> j p (r d)", p=P, r=TOPK)
    w_in_v = w_in.rearrange("o (k p) n -> p (o k) n", p=P)
    w_out_v = w_out.rearrange("o (k p) n -> p (o k) n", p=P)
    w_gate_v = w_ple_gate.rearrange("o (k p) n -> p (o k) n", p=P)
    w_proj_v = w_ple_proj.rearrange("o (k p) n -> p (o k) n", p=P)

    ctx = ExitStack()
    with ctx:
        place = {}

        def sb(name, shape, dt=F32):
            place[name] = -(-nc.sbuf_base // 32) * 32
            return ctx.enter_context(nc.sbuf_tensor(name, shape, dt))

        def sem(name):
            return ctx.enter_context(nc.semaphore(name))

        ring = sb("ring", [P, SLOTS, SLOT])
        xres = sb("xres", [P, NT, D])
        hT = sb("hT", [P, KD, T])
        xbcT = sb("xbcT", [P, CT, T])
        qkT = sb("qkT", [P, 2 * AH, T])
        zs = sb("zs", [P, NT, SSD_W])
        vt = sb("vt", [P, NT, ATT_W])
        work = sb("work", [P, 4608])

        ident = sb("ident", [P, P])
        upper = sb("upper", [P, P])
        strict = sb("strict", [P, P])
        ones = sb("ones", [P, P])
        attmask = sb("attmask", [P, P])
        iota = sb("iota", [P, P])
        token4_i = sb("token4_i", [P, NT], I32)
        token4 = sb("token4", [P, NT])

        gmix_t = sb("gmix_t", [P, KD])
        gple_t = sb("gple_t", [P, KD])
        convw_t = sb("convw_t", [P, CONV, CT])
        convb_t = sb("convb_t", [P, CT])
        dtb = sb("dtb", [P, NH])
        alog = sb("alog", [P, NH])
        dskip = sb("dskip", [P, NH])
        normw = sb("normw", [P, SSD_W])
        subln = sb("subln", [P, VH])
        brt = sb("brt", [P, E])
        wdt = sb("wdt", [P, KD, NH])
        expert_of = sb("expert_of", [P, 1])
        expert_tmp = sb("expert_tmp", [P, 1])
        expert_i = sb("expert_i", [P, 1], I32)

        ssq = sb("ssq", [P, 20])
        rstd = sb("rstd", [P, 20])
        dts = sb("dts", [P, 12, NT * NH])
        lam_s = sb("lam_s", [P, 8])
        att_s = sb("att_s", [P, 2, 8])
        o_inv = sb("o_inv", [P, AH])
        gates = sb("gates", [P, NT, TOPK])
        pos_tab = sb("pos_tab", [P, NT, NCOL])
        val_tab = sb("val_tab", [P, NT, NCOL])
        block_expert_f = sb("block_expert_f", [P, NCOL])
        block_expert = sb("block_expert", [P, NCOL], I32)
        extra_count = sb("extra_count", [P, 1], I32)
        out_idx = sb("out_idx", [P, NCOL], I32)
        gather_idx = sb("gather_idx", [P, 1], I32)
        scatter_idx = sb("scatter_idx", [P, 1], I32)

        def over(name, host, at, cols):
            return nc.alloc_sbuf_tensor_at(name, [P, cols], F32R, offset=place[host] + 4 * at)

        w_hi = [over(f"w_hi{b}", "ring", (RING + 2 * b) * SLOT, SLOT) for b in range(PARTS)]
        w_lo = [over(f"w_lo{b}", "ring", (RING + 2 * b + 1) * SLOT, SLOT) for b in range(PARTS)]
        xT_hi, xT_lo, aT_hi, aT_lo = [over(name, "hT", q * D, D).ap().rearrange("p (k n) -> p k n", n=B)
                                      for q, name in enumerate(("xT_hi", "xT_lo", "aT_hi", "aT_lo"))]
        bias_tab = over("bias_tab", "xbcT", 0, 3 * D)
        up_hot = sb("up_hot", [2 * E, B], F32R)
        down_hot = sb("down_hot", [2 * E, B], F32R)

        def carve(buf, at, shape):
            n = 1
            for s in shape:
                n *= s
            v = buf[:, at:at + n]
            if len(shape) == 2:
                v = v.rearrange("p (a b) -> p a b", a=shape[0])
            if len(shape) == 3:
                v = v.rearrange("p (a b c) -> p a b c", a=shape[0], b=shape[1])
            return v

        hrow = carve(work, 0, [2, D])
        xs_tok = carve(work, 0, [SSD_W])
        xdt = carve(work, SSD_W, [SSD_W])
        xdec = carve(work, 2 * SSD_W, [SSD_W])
        b_tok = carve(work, 3 * SSD_W, [NG * NS])
        cb_mask = carve(work, 3 * SSD_W + 256, [NG, P])
        seg = carve(work, 4 * SSD_W, [NH, P])
        prevT = carve(work, 6 * SSD_W, [SSD_W])
        yrow = carve(work, 7 * SSD_W, [SSD_W])
        ysq = carve(work, 8 * SSD_W, [SSD_W])
        probs = carve(work, 0, [2, 2, T])
        wgt = carve(work, 4 * T, [2, T])
        wgtT = carve(work, 6 * T, [2, T])
        orow = carve(work, 8 * T, [ATT_W])
        logits = carve(work, 2048, [NT, E])
        top8 = carve(work, 2176, [NT, 8])
        topi_u = carve(work, 2208, [NT * 8]).bitcast(U32).rearrange("p (a b) -> p a b", a=NT)
        topi = carve(work, 2240, [NT, 8])
        chosen = carve(work, 2272, [NT, E])
        rankv = carve(work, 2400, [NT, E])
        onehot = carve(work, 2528, [NT, E])
        small = carve(work, 2656, [64])
        counts = carve(work, 2720, [E])
        extra = carve(work, 2752, [E])
        cum = carve(work, 2784, [E])
        blk_e = carve(work, 2816, [EXTRA])
        blk_b = carve(work, 2848, [EXTRA])
        sel = carve(work, 2880, [EXTRA, E])
        sel2 = carve(work, 2880 + EXTRA * E, [EXTRA, E])
        qk_flat = qkT[:, :, :].rearrange("p a b -> p (a b)")
        vt_flat = vt[:, :, :].rearrange("p a b -> p (a b)")
        zs_flat = zs[:, :, :].rearrange("p a b -> p (a b)")
        gate_s, up_s, sig_s = [carve(qk_flat, q * D, [D]) for q in range(3)]
        bias_rows = qk_flat[:, D:4 * D]
        x_whole = carve(vt_flat, 0, [len(UP_WHOLE), B])
        a_whole = carve(vt_flat, 2 * B, [2 * len(DOWN_WHOLE), B])
        gfin = vt_flat[:, D:2 * D]
        wrt = carve(zs_flat, 0, [KD, E])
        gffn = zs_flat[:, KD * E:KD * E + D]
        xg = zs_flat[:, 0:D]
        yg = zs_flat[:, D:2 * D]
        slot_hot = carve(work, 0, [NT, B])
        hT_flat = hT[:, :, :].rearrange("p a b -> p (a b)")
        xbc_flat = xbcT[:, :, :].rearrange("p a b -> p (a b)")
        p_rows = carve(hT_flat, 3 * D, [NT, PLE])
        pT = carve(xbc_flat, 3 * D, [2, T])
        w_proj_s = carve(work, 2 * D, [2, D])
        pw = ring[:, 10:12, :].rearrange("p a (j n) -> p (a j) n", n=D)
        sig_t = carve(qk_flat, D, [2, D])
        squares = carve(qk_flat, 0, [D])
        lam_prod = carve(work, 4 * D, [2, DH])
        lamv = carve(work, 4 * D + 2 * DH, [4, DH])
        iota_i = work[:, 4 * D + 6 * DH:4 * D + 6 * DH + P].bitcast(I32)
        osq = xbcT[:, 0, :]
        out_row = carve(zs_flat, 0, [2, D])

        def dense(slot):
            return ring[:, slot, :].rearrange("p (k n) -> p k n", k=KD)

        ps = ctx.enter_context(nc.psum_tensor("ps", [P, 8, BANK], F32))

        x_loaded = [sem(f"x_loaded{j}") for j in range(NT)]
        gain_loaded = sem("gain_loaded")
        params_loaded = sem("params_loaded")
        late_params_loaded = sem("late_params_loaded")
        router_loaded = sem("router_loaded")
        bias_rows_loaded = sem("bias_rows_loaded")
        gffn_loaded = sem("gffn_loaded")
        slot_loaded = [sem(f"slot_loaded{s}") for s in range(SLOTS)]
        up_loaded = [sem(f"up_loaded{k}") for k in range(UP_CHUNKS)]
        down_loaded = [sem(f"down_loaded{c}") for c in range(DOWN_CHUNKS)]
        consts_ready = sem("consts_ready")
        squared = sem("squared")
        scaled = sem("scaled")
        rooted = sem("rooted")
        normed = sem("normed")
        norm_turned = sem("norm_turned")
        norm_copied = sem("norm_copied")
        bias_hi = sem("bias_hi")
        bias_ready = sem("bias_ready")
        projected = sem("projected")
        conv_done = sem("conv_done")
        conv_silu = sem("conv_silu")
        proj_copied = sem("proj_copied")
        dt_projected = sem("dt_projected")
        dt_pre = sem("dt_pre")
        dt_e = sem("dt_e")
        dt_u = sem("dt_u")
        dt_l = sem("dt_l")
        adt_ready = sem("adt_ready")
        cum_ready = sem("cum_ready")
        cum_args = sem("cum_args")
        cum_exp = sem("cum_exp")
        ssd_turned = sem("ssd_turned")
        ssd_read = sem("ssd_read")
        seg_ready = sem("seg_ready")
        seg_exp = sem("seg_exp")
        decay_ready = sem("decay_ready")
        ssd_summed = sem("ssd_summed")
        state_updated = sem("state_updated")
        y_gated = sem("y_gated")
        y_squared = sem("y_squared")
        y_mean = sem("y_mean")
        y_root = sem("y_root")
        y_ssd_ready = sem("y_ssd_ready")
        mix_turned = sem("mix_turned")
        mix_copied = sem("mix_copied")
        lam_dots = sem("lam_dots")
        lam_exps = sem("lam_exps")
        scored = sem("scored")
        maxed = sem("maxed")
        expd = sem("expd")
        weighed = sem("weighed")
        w_turned = sem("w_turned")
        w_copied = sem("w_copied")
        attended = sem("attended")
        o_copied = sem("o_copied")
        o_squared = sem("o_squared")
        o_mean = sem("o_mean")
        o_root = sem("o_root")
        o_ready = sem("o_ready")
        mixed = sem("mixed")
        mixed_added = sem("mixed_added")
        hn_stored = [sem(f"hn_stored{j}") for j in range(NT)]
        routed = sem("routed")
        logits_read = sem("logits_read")
        top_shifted = sem("top_shifted")
        top_exp = sem("top_exp")
        chosen_ready = sem("chosen_ready")
        placed = sem("placed")
        tables_ready = sem("tables_ready")
        dve_step = sem("dve_step")
        act_step = sem("act_step")
        hot_ready = sem("hot_ready")
        idx_summed = sem("idx_summed")
        out_idx_ready = sem("out_idx_ready")
        gather_idx_ready = sem("gather_idx_ready")
        gather_started = sem("gather_started")
        scatter_started = sem("scatter_started")
        gathered = sem("gathered")
        x_turned = sem("x_turned")
        xT_hi_ready = sem("xT_hi_ready")
        xT_ready = sem("xT_ready")
        up_hot_ready = sem("up_hot_ready")
        down_hot_ready = sem("down_hot_ready")
        up_hi = sem("up_hi")
        up_lo = sem("up_lo")
        down_hi = sem("down_hi")
        down_lo = sem("down_lo")
        up_used = sem("up_used")
        down_used = sem("down_used")
        gate_clamped = sem("gate_clamped")
        up_clamped = sem("up_clamped")
        sigmoided = sem("sigmoided")
        swish = sem("swish")
        act_ready = sem("act_ready")
        a_turned = sem("a_turned")
        aT_hi_ready = sem("aT_hi_ready")
        aT_ready = sem("aT_ready")
        y_ready = sem("y_ready")
        scatter_idx_ready = sem("scatter_idx_ready")
        scattered = sem("scattered")
        p_loaded = sem("p_loaded")
        pw_done = sem("pw_done")
        pw_copied = sem("pw_copied")
        tail_loaded = sem("tail_loaded")
        p_turned = sem("p_turned")
        p_copied = sem("p_copied")
        y_loaded = [sem(f"y_loaded{b}") for b in range(Y_BUFS)]
        y_summed = sem("y_summed")
        ple_done = sem("ple_done")
        gate_sig = sem("gate_sig")
        ple_added = sem("ple_added")
        out_ready = sem("out_ready")
        out_stored = [sem(f"out_stored{j}") for j in range(NT)]

        N_PROJ_CH = CT
        G_Z = CT
        G_QK = G_Z + NT
        G_V = G_QK + 2 * AH
        N_GROUPS = G_V + NT
        PER_CHUNK = (N_GROUPS - G_QK) // NT
        UNITS = NT * AH

        def wait_up_free(eng, i, k):
            if k in UP_WHOLE:
                eng.wait_ge(up_used, i * UP_CHUNKS + k + 1)
            else:
                eng.wait_ge(up_lo, i * len(UP_SPLIT) + UP_SPLIT.index(k) + 1)

        def wait_down_free(eng, i, c):
            if c in DOWN_WHOLE:
                eng.wait_ge(down_used, i * DOWN_CHUNKS + c + 1)
            else:
                eng.wait_ge(down_lo, i * len(DOWN_SPLIT) + DOWN_SPLIT.index(c) + 1)

        def is_static(i, least):
            return isinstance(i, int) and i < least

        block = ctx.enter_context(nc.Block())

        @block.sync
        def _(sp):
            for j in range(NT):
                sp.dma_start(xres[:, j, :], x_v[:, j, :]).then_inc(x_loaded[j], 16)
            sp.wait_ge(gain_loaded, 16)
            sp.wait_ge(params_loaded, 16 * N_PARAMS)

            def load_dense(slot, src, col):
                sp.dma_start(dense(slot), src[:, :, col:col + WCOL]).then_inc(slot_loaded[slot], 16)

            cols = ([OFF_XBC + WCOL * i for i in range(4)] + [OFF_Z + WCOL * i for i in range(2)]
                    + [OFF_Q + WCOL * i for i in range(2)] + [OFF_K + WCOL * i for i in range(2)]
                    + [OFF_V + WCOL * i for i in range(2)])
            for s, col in enumerate(cols):
                load_dense(s, w_in_v, col)

            def load_up(e, k):
                sp.dma_start(ring[:, k % RING, :], w_up[0, e, k * P:(k + 1) * P, :] if isinstance(e, int)
                             else w_up[0, bass.ds(e, 1), k * P:(k + 1) * P, :].rearrange("a p n -> (a p) n")
                             ).then_inc(up_loaded[k], 16)

            def load_down(e, c):
                rows = slice(c * 2 * P, (c + 1) * 2 * P)
                src = (w_down[0, e, rows, :] if isinstance(e, int)
                       else w_down[0, bass.ds(e, 1), rows, :].rearrange("a q n -> (a q) n"))
                sp.dma_start(ring[:, 2 + c, :].rearrange("p (f n) -> p f n", f=2),
                             src.rearrange("(f p) n -> p f n", p=P)).then_inc(down_loaded[c], 16)

            done = ([2 * i + 2 for i in range(4)] + [G_QK] * 2 + [G_QK + 2 * i + 2 for i in range(4)] + [N_GROUPS] * 2)
            for k in range(RING):
                sp.wait_ge(projected, done[k])
                load_up(0, k)
            for c in range(4):
                sp.wait_ge(projected, done[OUT_SLOT + c])
                load_dense(OUT_SLOT + c, w_out_v, WCOL * c)
            sp.wait_ge(mix_turned, NT)
            sp.dma_start(wrt, w_router.rearrange("o (k p) e -> p (o k) e", p=P)).then_inc(router_loaded, 16)
            sp.dma_start(gffn, g_ffn.to_broadcast([P, D])).then_inc(gffn_loaded, 16)
            sp.wait_ge(attended, UNITS)
            for q in range(2):
                rows = slice(q * E, (q + 1) * E)
                sp.dma_start(bias_rows[rows, 0:2 * D], b_up[0]).then_inc(bias_rows_loaded, 16)
                sp.dma_start(bias_rows[rows, 2 * D:3 * D], b_down[0]).then_inc(bias_rows_loaded, 16)
            sp.dma_start(gfin, g_final.rearrange("(a n) -> a n", a=1).to_broadcast([P, D])).then_inc(tail_loaded, 16)
            for j in range(NT):
                sp.wait_ge(normed, NT + j + 1)
                sp.dma_start(hn_v[:, j, :], hrow[:, j % 2, :]).then_inc(hn_stored[j], 16)
            sp.wait_ge(mixed, NT)
            sp.dma_start(p_rows, p.rearrange("o b (j p) c -> p (o b j) c", p=P)).then_inc(p_loaded, 16)

            def load_block(i, e, before):
                for k in range(UP_CHUNKS):
                    if k >= RING:
                        wait_up_free(sp, i, k - RING)
                    elif k + RING < UP_CHUNKS:
                        wait_up_free(sp, i - 1, k + RING)
                    elif is_static(i, 2):
                        wait_up_free(sp, 0, k)
                    else:
                        wait_down_free(sp, i - 2, k - 2)
                    load_up(e, k)
                for c in range(DOWN_CHUNKS):
                    wait_up_free(sp, i, 2 + c)
                    load_down(before, c)

            for k in range(RING, UP_CHUNKS):
                wait_up_free(sp, 0, k - RING)
                load_up(0, k)
            for i in range(1, PEELED):
                load_block(i, i, i - 1)
            sp.wait_ge(tables_ready, 1)
            sp.dma_start(w_proj_s, w_proj_v).then_inc(tail_loaded, 16)
            n = sp.value_load(extra_count[0:1, 0:1], min_val=0, max_val=EXTRA) + E
            with sp.Fori(PEELED, n) as i:
                e = sp.value_load(block_expert[0:1, bass.ds(i, 1)], min_val=0, max_val=E - 1)
                before = sp.value_load(block_expert[0:1, bass.ds(i - 1, 1)], min_val=0, max_val=E - 1)
                load_block(i, e, before)
            last = sp.value_load(block_expert[0:1, bass.ds(n - 1, 1)], min_val=0, max_val=E - 1)
            for c in range(DOWN_CHUNKS):
                wait_down_free(sp, n - 2, c)
                load_down(last, c)
            for c in range(4):
                if c < 2:
                    wait_up_free(sp, n - 1, RING + c)
                else:
                    wait_down_free(sp, n - 1, c - 2)
                load_dense(c, w_gate_v, WCOL * c)
            sp.wait_ge(scattered, n * 16)
            for j in range(NT):
                if j >= Y_BUFS:
                    sp.wait_ge(y_summed, j - Y_BUFS + 1)
                s = 4 + 2 * (j % Y_BUFS)
                sp.dma_start(ring[:, s:s + 2, :].rearrange("p a n -> p (a n)"), y_v[j]).then_inc(y_loaded[j % Y_BUFS], 16)
            for j in range(NT):
                sp.wait_ge(out_ready, j + 1)
                sp.dma_start(out_v[:, j, :], out_row[:, j % 2, :]).then_inc(out_stored[j], 16)
            for j in range(NT):
                sp.wait_ge(out_stored[j], 16)

        @block.gpsimd
        def _(pool):
            n = 0

            def link(ins):
                nonlocal n
                n += 1
                ins.then_inc(consts_ready, 1)
                pool.wait_ge(consts_ready, n)

            link(nc.gpsimd.memset(ident[:], 0.0))
            link(nc.gpsimd.affine_select(out=ident[:], in_=ident[:], compare_op=ALU.not_equal, fill=1.0,
                                         base=0, pattern=[[-1, P]], channel_multiplier=1))
            link(nc.gpsimd.memset(ones[:], 1.0))
            link(nc.gpsimd.affine_select(out=upper[:], in_=ones[:], compare_op=ALU.is_ge, fill=0.0,
                                         base=0, pattern=[[1, P]], channel_multiplier=-1))
            link(nc.gpsimd.affine_select(out=strict[:], in_=ones[:], compare_op=ALU.is_gt, fill=0.0,
                                         base=0, pattern=[[1, P]], channel_multiplier=-1))
            link(nc.gpsimd.memset(attmask[:], 0.0))
            link(nc.gpsimd.affine_select(out=attmask[:], in_=attmask[:], compare_op=ALU.is_ge, fill=MASKED,
                                         base=0, pattern=[[-1, P]], channel_multiplier=1))
            link(nc.gpsimd.iota(iota_i, pattern=[[1, P]], base=0, channel_multiplier=0))
            link(nc.gpsimd.tensor_copy(iota[:], iota_i))
            link(nc.gpsimd.iota(token4_i[:], pattern=[[TOPK * P, NT]], base=0, channel_multiplier=TOPK))
            link(nc.gpsimd.tensor_copy(token4[:], token4_i[:]))
            link(nc.gpsimd.iota(expert_i[:], pattern=[[0, 1]], base=0, channel_multiplier=1))
            link(nc.gpsimd.tensor_copy(expert_of[:], expert_i[:]))
            assert n == N_CONSTS

            last_token = pool.alloc_register("last_token")
            pool.reg_mov(last_token, T - 1)
            last_row = pool.alloc_register("last_row")
            pool.reg_mov(last_row, T * TOPK - 1)

            def gather(i):
                pool.wait_ge(gather_idx_ready, i + 1)
                if not isinstance(i, int) or i >= 1:
                    pool.wait_ge(x_turned, i)
                pool.sem_inc(gather_started, 1)
                nc.gpsimd.indirect_dma_start(
                    xg[0:B, :], None, hn_rows, bass.IndirectOffsetOnAxis(ap=gather_idx[0:B, :], axis=0),
                    bounds_check=last_token, oob_is_err=False).then_inc(gathered, 16)

            def scatter(i):
                pool.wait_ge(y_ready, i + 1)
                pool.wait_ge(scatter_idx_ready, i + 1)
                pool.sem_inc(scatter_started, 1)
                nc.gpsimd.indirect_dma_start(
                    y_rows, bass.IndirectOffsetOnAxis(ap=scatter_idx[0:B, :], axis=0), yg[0:B, :], None,
                    bounds_check=last_row, oob_is_err=False).then_inc(scattered, 16)

            for j in range(NT):
                pool.wait_ge(hn_stored[j], 16)
            gather(0)
            gather(1)
            pool.wait_ge(tables_ready, 1)
            n_blocks = pool.value_load(extra_count[0:1, 0:1], min_val=0, max_val=EXTRA) + E
            gather(2)
            gather(3)
            scatter(0)
            with pool.Fori(PEELED, n_blocks) as i:
                gather(i + 1)
                scatter(i - 2)
            scatter(n_blocks - 2)
            scatter(n_blocks - 1)
            pool.wait_ge(gathered, (n_blocks + 1) * 16)
            pool.wait_ge(scattered, n_blocks * 16)

        @block.scalar
        def _(act):
            steps = 0

            def link(ins):
                nonlocal steps
                steps += 1
                ins.then_inc(act_step, 1)
                act.wait_ge(act_step, steps)

            def row(v):
                return v.to_broadcast([P, v.shape[1]])

            with nc.allow_non_contiguous_dma(reason="small parameters by partition"):
                act.dma_start(gmix_t[:], g_mix.rearrange("o (k p) -> p (o k)", p=P)).then_inc(gain_loaded, 16)
                act.dma_start(wdt[:], w_in_v[:, :, OFF_DT:OFF_DT + NH]).then_inc(params_loaded, 16)
                act.dma_start(convb_t[:], conv_b.rearrange("o (k p) -> p (o k)", p=P)).then_inc(params_loaded, 16)
                for k in range(CONV):
                    act.dma_start(convw_t[:, k, :], conv_w[0, k].rearrange("(t p) -> p t", p=P)).then_inc(params_loaded, 16)
                act.dma_start(dtb[:], row(dt_bias)).then_inc(params_loaded, 16)
                act.dma_start(alog[:], row(a_log)).then_inc(params_loaded, 16)

            def load_late_params():
                with nc.allow_non_contiguous_dma(reason="small parameters by partition"):
                    act.dma_start(gple_t[:], g_ple.rearrange("o (k p) -> p (o k)", p=P)).then_inc(late_params_loaded, 16)
                    for dst, src in ((dskip[:], d_skip), (normw[:], ssd_norm_w),
                                     (lamv[:, 0, :], lam_q1), (lamv[:, 1, :], lam_k1), (lamv[:, 2, :], lam_q2),
                                     (lamv[:, 3, :], lam_k2), (subln[:], subln_w), (brt[:], b_router)):
                        act.dma_start(dst, row(src)).then_inc(late_params_loaded, 16)

            def square_of_tile(col, j):
                if col >= 1:
                    act.wait_ge(squared, col)
                nc.scalar.activation(squares, xres[:, j, :], ACT.Square,
                                     accum_out=ssq[:, col:col + 1]).then_inc(squared, 1)

            def root_of_tile(col):
                act.wait_ge(scaled, col + 1)
                nc.scalar.activation(rstd[:, col:col + 1], ssq[:, col:col + 1], ACT.Sqrt).then_inc(rooted, 1)

            for j in range(NT):
                act.wait_ge(x_loaded[j], 16)
                square_of_tile(j, j)
            for j in range(NT):
                root_of_tile(j)
            load_late_params()
            act.wait_ge(params_loaded, 16 * N_PARAMS)
            link(nc.scalar.activation(alog[:], alog[:], ACT.Exp))
            for t in range(CT):
                act.wait_ge(conv_done, t + 1)
                nc.scalar.activation(xbcT[:, t, :], xbcT[:, t, :], ACT.Silu).then_inc(conv_silu, 1)
            act.wait_ge(dt_pre, 1)
            nc.scalar.activation(dts[:, 2, :], dts[:, 1, :], ACT.Exp).then_inc(dt_e, 1)
            act.wait_ge(dt_u, 1)
            nc.scalar.activation(dts[:, 4, :], dts[:, 3, :], ACT.Ln).then_inc(dt_l, 1)

            act.wait_ge(lam_dots, 1)
            nc.scalar.activation(lam_s[:, 2:4], lam_s[:, 0:2], ACT.Exp).then_inc(lam_exps, 1)

            def copy_group(g):
                act.wait_ge(projected, g + 1)
                bank = ps[:, g % 2, :]
                if g < G_QK:
                    ins = nc.scalar.activation(zs[:, g - G_Z, :], bank, ACT.Silu)
                elif g < G_QK + AH:
                    ins = nc.scalar.activation(qkT[:, g - G_QK, :], bank, ACT.Copy, scale=float(DH) ** -0.5)
                elif g < G_V:
                    ins = nc.scalar.activation(qkT[:, g - G_QK, :], bank, ACT.Copy)
                else:
                    ins = nc.scalar.activation(vt[:, g - G_V, :], bank, ACT.Copy)
                ins.then_inc(proj_copied, 1)

            for g in range(G_Z, G_QK):
                copy_group(g)
            act.wait_ge(cum_args, 1)
            nc.scalar.activation(dts[:, 8:11, :], dts[:, 8:11, :], ACT.Exp).then_inc(cum_exp, 1)

            g = G_QK
            for c in range(NT):
                act.wait_ge(seg_ready, c + 1)
                nc.scalar.activation(seg, seg, ACT.Exp).then_inc(seg_exp, 1)
                for _ in range(PER_CHUNK):
                    copy_group(g)
                    g += 1
                act.wait_ge(y_gated, c + 1)
                half = SSD_W // NG
                if c >= 1:
                    act.wait_ge(y_root, c)
                for q in range(NG):
                    ins = nc.scalar.activation(ysq[:, q * half:(q + 1) * half], yrow[:, q * half:(q + 1) * half],
                                               ACT.Square, accum_out=ssq[:, 16 + q:17 + q])
                    ins.then_inc(y_squared, 1)
                act.wait_ge(y_mean, c + 1)
                nc.scalar.activation(rstd[:, 16:16 + NG], ssq[:, 16:16 + NG], ACT.Sqrt).then_inc(y_root, 1)

            for c in range(NT):
                act.wait_ge(mix_turned, c + 1)
                nc.scalar.activation(hT[:, 0:XT, c * P:(c + 1) * P], ps[:, 6 + c % 2, :].rearrange("p (k t) -> p k t", k=XT),
                                     ACT.Copy).then_inc(mix_copied, 1)

            def exp_unit(u):
                nk = (u // AH + 1) * P
                for j in range(2):
                    s = 2 * u + j
                    act.wait_ge(maxed, s + 1)
                    if u >= 2:
                        act.wait_ge(weighed, u - 1)
                    nc.scalar.activation(probs[:, u % 2, j, 0:nk], ps[:, (u % 2) * 2 + j, 0:nk], ACT.Exp,
                                         bias=att_s[:, u % 2, j:j + 1],
                                         accum_out=att_s[:, u % 2, 2 + j:3 + j]).then_inc(expd, 1)

            def copy_w(u):
                nk = (u // AH + 1) * P
                act.wait_ge(w_turned, u + 1)
                if u >= 2:
                    act.wait_ge(attended, u - 1)
                nc.scalar.activation(wgtT[:, u % 2, 0:nk], ps[:, 4 + u % 2, 0:nk], ACT.Copy).then_inc(w_copied, 1)

            def square_o(b):
                act.wait_ge(o_copied, b + 1)
                if b >= 1:
                    act.wait_ge(o_squared, AH * b)
                for h in range(AH):
                    nc.scalar.activation(osq[:, h * VH:(h + 1) * VH],
                                         orow[:, h * VH:(h + 1) * VH], ACT.Square,
                                         accum_out=lam_s[:, 4 + h:5 + h]).then_inc(o_squared, 1)
                act.wait_ge(o_mean, b + 1)
                nc.scalar.activation(rstd[:, 16:16 + AH], lam_s[:, 4:4 + AH], ACT.Sqrt).then_inc(o_root, 1)

            def copy_o(b):
                act.wait_ge(mix_turned, NT + b + 1)
                nc.scalar.activation(hT[:, XT:KD, b * P:(b + 1) * P], ps[:, 6 + b % 2, :].rearrange("p (k t) -> p k t", k=AH),
                                     ACT.Copy).then_inc(mix_copied, 1)

            exp_unit(0)
            for u in range(UNITS):
                if u + 1 < UNITS:
                    exp_unit(u + 1)
                copy_w(u)
                if u % AH == 0 and u:
                    square_o(u // AH - 1)
                if u % AH == 2 and u > AH:
                    copy_o(u // AH - 1)
            square_o(NT - 1)
            copy_o(NT - 1)

            for j in range(NT):
                act.wait_ge(mixed_added, j + 1)
                square_of_tile(NT + j, j)
                root_of_tile(NT + j)
            act.wait_ge(top_shifted, 1)
            nc.scalar.activation(gates[:, :, :], gates[:, :, :], ACT.Exp).then_inc(top_exp, 1)

            def split_hi(i, q, after_loop=False):
                chunk, b = SPLITS[q], q % PARTS
                is_up = q < len(UP_SPLIT)
                if q >= PARTS:
                    if after_loop:
                        act.wait_ge(down_used, (i - 2) * DOWN_CHUNKS + chunk + 1)
                    else:
                        act.wait_ge(up_used, i * UP_CHUNKS + SPLITS[q - PARTS] + 1)
                elif is_static(i, 1):
                    if q == 0:
                        act.wait_ge(mixed, NT)
                elif is_static(i, 2):
                    act.wait_ge(up_used, UP_SPLIT[len(UP_SPLIT) - PARTS + q] + 1)
                else:
                    act.wait_ge(down_used, (i - 2) * DOWN_CHUNKS + DOWN_SPLIT[q] + 1)
                if is_up:
                    act.wait_ge(up_loaded[chunk], 16 * (i + 1))
                    nc.scalar.activation(w_hi[b][:], ring[:, chunk % RING, :], ACT.Copy).then_inc(up_hi, 1)
                else:
                    act.wait_ge(down_loaded[chunk], 16 * i)
                    nc.scalar.activation(w_hi[b][:], ring[:, 2 + chunk, :], ACT.Copy).then_inc(down_hi, 1)

            def sigmoid_of(i):
                act.wait_ge(gate_clamped, i + 1)
                nc.scalar.activation(sig_s, gate_s, ACT.Sigmoid, scale=SWIGLU_ALPHA).then_inc(sigmoided, 1)

            def copy_y(i):
                act.wait_ge(down_used, (i + 1) * DOWN_CHUNKS)
                if not isinstance(i, int) or i >= 1:
                    act.wait_ge(scattered, i * 16)
                nc.scalar.activation(yg.rearrange("p (a n) -> p a n", a=2), ps[:, 4:6, :], ACT.Copy).then_inc(y_ready, 1)

            turned = ps[:, 6:8, :].rearrange("p a (k n) -> p (a k) n", n=B)

            def copy_x(i):
                act.wait_ge(x_turned, i + 1)
                nc.scalar.activation(x_whole, turned[:, UP_WHOLE[0]:KD:UP_WHOLE[1] - UP_WHOLE[0], :], ACT.Copy).then_inc(xT_hi_ready, 1)
                nc.scalar.activation(xT_hi, turned, ACT.Copy).then_inc(xT_hi_ready, 1)

            def copy_a(i):
                act.wait_ge(a_turned, i + 1)
                nc.scalar.activation(a_whole, turned[:, 0:2 * len(DOWN_WHOLE), :], ACT.Copy).then_inc(aT_hi_ready, 1)
                nc.scalar.activation(aT_hi, turned, ACT.Copy).then_inc(aT_hi_ready, 1)

            def expert_step(i):
                for q in range(PARTS):
                    if not is_static(i, 1):
                        split_hi(i, q)
                if not is_static(i, 2):
                    copy_y(i - 2)
                for q in range(PARTS, len(UP_SPLIT)):
                    split_hi(i, q)
                if not is_static(i, 1):
                    copy_a(i - 1)
                    for q in range(len(UP_SPLIT), len(SPLITS)):
                        split_hi(i, q)
                sigmoid_of(i)
                copy_x(i + 1)

            act.wait_ge(bias_rows_loaded, 64)
            nc.scalar.activation(bias_tab[0:2 * E, :], bias_rows[0:2 * E, :], ACT.Copy).then_inc(bias_hi, 1)
            for q in range(PARTS):
                split_hi(0, q)
            copy_x(0)
            for i in range(PEELED):
                expert_step(i)
            act.wait_ge(tables_ready, 1)
            n_blocks = act.value_load(extra_count[0:1, 0:1], min_val=0, max_val=EXTRA) + E
            with act.Fori(PEELED, n_blocks) as i:
                expert_step(i)
            copy_y(n_blocks - 2)
            copy_a(n_blocks - 1)
            for q in range(len(UP_SPLIT), len(SPLITS)):
                split_hi(n_blocks, q, after_loop=True)
            copy_y(n_blocks - 1)

            for j in range(NT):
                act.wait_ge(pw_done, j + 1)
                b = 2 * (j % 2)
                nc.scalar.activation(pw[:, j, :].rearrange("p (a n) -> p a n", a=2), ps[:, b:b + 2, :], ACT.Copy).then_inc(pw_copied, 1)
            for s, (final, j) in enumerate(TAIL_ORDER):
                if final:
                    act.wait_ge(ple_done, j + 1)
                    if j >= 2:
                        act.wait_ge(ple_added, j - 1)
                    b = 2 * (j % 2)
                    nc.scalar.activation(sig_t[:, j % 2, :].rearrange("p (a n) -> p a n", a=2), ps[:, b:b + 2, :],
                                         ACT.Sigmoid).then_inc(gate_sig, 1)
                    act.wait_ge(ple_added, j + 1)
                else:
                    act.wait_ge(y_summed, j + 1)
                square_of_tile(2 * NT + s, j)
                root_of_tile(2 * NT + s)

        @block.tensor
        def _(pe):
            mm = nc.tensor.matmul

            def turn_rows(stage, j):
                s = stage * NT + j
                pe.wait_ge(normed, s + 1)
                if s % NT >= 2:
                    pe.wait_ge(norm_copied, s - 1)
                for k in range(KD):
                    last = nc.tensor.transpose(ps[:, 4 + 2 * (j % 2) + k // 4, (k % 4) * P:(k % 4 + 1) * P],
                                               hrow[:, j % 2, k * P:(k + 1) * P], ident[:])
                last.then_inc(norm_turned, 1)

            pe.wait_ge(consts_ready, N_CONSTS)
            for j in range(NT):
                turn_rows(0, j)

            def project(g):
                if g >= 2:
                    if g - 2 < G_Z:
                        pe.wait_ge(conv_done, g - 1)
                    else:
                        pe.wait_ge(proj_copied, g - 1 - G_Z)
                bank = ps[:, g % 2, :]
                if g < G_Z or G_QK <= g < G_V:
                    t = g if g < G_Z else g - G_QK + 12
                    slot = t // 2
                    w = dense(slot)
                    if t % 2 == 0:
                        pe.wait_ge(slot_loaded[slot], 16)
                    for k in range(KD):
                        last = mm(bank, w[:, k, (t % 2) * P:(t % 2 + 1) * P], hT[:, k, :], start=(k == 0), stop=(k == KD - 1))
                else:
                    first, j = (4, g - G_Z) if g < G_QK else (10, g - G_V)
                    if j == 0:
                        pe.wait_ge(slot_loaded[first], 16)
                        pe.wait_ge(slot_loaded[first + 1], 16)
                    for s in range(2):
                        w = dense(first + s)
                        for k in range(KD):
                            last = mm(ps[:, g % 2, s * WCOL:(s + 1) * WCOL], hT[:, k, j * P:(j + 1) * P], w[:, k, :],
                                      start=(k == 0), stop=(k == KD - 1))
                last.then_inc(projected, 1)

            pe.wait_ge(norm_copied, NT)
            for g in range(CT):
                project(g)
            pe.wait_ge(params_loaded, 16 * N_PARAMS)
            for j in range(NT):
                for k in range(KD):
                    last = mm(ps[:, 2, j * NH:(j + 1) * NH], hT[:, k, j * P:(j + 1) * P], wdt[:, k, :],
                              start=(k == 0), stop=(k == KD - 1))
            last.then_inc(dt_projected, 1)
            for g in range(G_Z, G_QK):
                project(g)
            pe.wait_ge(adt_ready, 1)
            adt = dts[:, 6, :]
            mm(ps[:, 3, 0:NT * NH], upper[:], adt, start=True, stop=True)
            mm(ps[:, 3, NT * NH:2 * NT * NH], ones[:], adt, start=True, stop=True).then_inc(cum_ready, 1)

            def ssd_turn(c):
                tok = slice(c * P, (c + 1) * P)
                if c == 0:
                    pe.wait_ge(conv_silu, CT)
                    pe.wait_ge(cum_args, 1)
                else:
                    pe.wait_ge(ssd_read, c)
                    pe.wait_ge(seg_ready, c)
                    pe.wait_ge(state_updated, c)
                for t in range(XT):
                    nc.tensor.transpose(ps[:, 2, t * P:(t + 1) * P], xbcT[:, t, tok], ident[:])
                for q in range(NG):
                    nc.tensor.transpose(ps[:, 3, q * P:(q + 1) * P], xbcT[:, XT + q, tok], ident[:])
                for q in range(NG):
                    mm(ps[:, 3, (NG + q) * P:(NG + q + 1) * P], xbcT[:, XT + q, tok], xbcT[:, XT + NG + q, tok],
                       start=True, stop=True)
                for h in range(NH):
                    last = mm(ps[:, 4 + h // HG, (h % HG) * P:(h % HG + 1) * P],
                              dts[:, 6, c * NH + h:c * NH + h + 1].to_broadcast([P, P]), upper[:], start=True, stop=True)
                last.then_inc(ssd_turned, 1)

            def ssd_sum(c):
                tok = slice(c * P, (c + 1) * P)
                pe.wait_ge(decay_ready, c + 1)
                if c >= 1:
                    pe.wait_ge(y_gated, c)
                for h in range(NH):
                    mm(ps[:, 6, h * HP:(h + 1) * HP], seg[:, h, :], xdt[:, h * HP:(h + 1) * HP], start=True, stop=True)
                if c >= 1:
                    for q in range(NG):
                        mm(ps[:, 7, q * HG * HP:(q + 1) * HG * HP], xbcT[:, XT + NG + q, tok],
                           prevT[:, q * HG * HP:(q + 1) * HG * HP], start=True, stop=True)
                for q in range(NG):
                    last = mm(ps[:, 2, q * HG * HP:(q + 1) * HG * HP], b_tok[:, q * NS:(q + 1) * NS],
                              xdec[:, q * HG * HP:(q + 1) * HG * HP], start=True, stop=True)
                last.then_inc(ssd_summed, 1)

            g = G_QK
            for c in range(NT):
                ssd_turn(c)
                for _ in range(PER_CHUNK):
                    project(g)
                    g += 1
                ssd_sum(c)

            for c in range(NT):
                pe.wait_ge(y_ssd_ready, c + 1)
                if c < 2:
                    pe.wait_ge(y_gated, NT)
                else:
                    pe.wait_ge(mix_copied, c - 1)
                for t in range(XT):
                    last = nc.tensor.transpose(ps[:, 6 + c % 2, t * P:(t + 1) * P], zs[:, c, t * P:(t + 1) * P], ident[:])
                last.then_inc(mix_turned, 1)

            pe.wait_ge(proj_copied, N_GROUPS - G_Z)

            def score(u):
                b, h = u // AH, u % AH
                nk = (b + 1) * P
                for j in range(2):
                    if u >= 2:
                        pe.wait_ge(expd, 2 * (u - 2) + j + 1)
                    half = slice(j * DH, (j + 1) * DH)
                    mm(ps[:, (u % 2) * 2 + j, 0:nk], qkT[half, h, b * P:(b + 1) * P], qkT[half, AH + h, 0:nk],
                       start=True, stop=True).then_inc(scored, 1)

            def turn_w(u):
                b = u // AH
                pe.wait_ge(weighed, u + 1)
                if u >= 2:
                    pe.wait_ge(w_copied, u - 1)
                for k in range(b + 1):
                    last = nc.tensor.transpose(ps[:, 4 + u % 2, k * P:(k + 1) * P], wgt[:, u % 2, k * P:(k + 1) * P], ident[:])
                last.then_inc(w_turned, 1)

            def attend(u):
                b, h = u // AH, u % AH
                pe.wait_ge(w_copied, u + 1)
                if h == 0:
                    pe.wait_ge(mix_copied, NT if b < 2 else NT + b - 1)
                for k in range(b + 1):
                    last = mm(ps[:, 6 + b % 2, h * VH:(h + 1) * VH], wgtT[:, u % 2, k * P:(k + 1) * P],
                              vt[:, k, h * VH:(h + 1) * VH], start=(k == 0), stop=(k == b))
                last.then_inc(attended, 1)

            def turn_o(b):
                pe.wait_ge(o_ready, b + 1)
                for h in range(AH):
                    last = nc.tensor.transpose(ps[:, 6 + b % 2, h * P:(h + 1) * P], orow[:, h * VH:(h + 1) * VH], ident[:])
                last.then_inc(mix_turned, 1)

            score(0)
            score(1)
            for u in range(UNITS):
                if u + 2 < UNITS:
                    score(u + 2)
                turn_w(u)
                attend(u)
                if u % AH == 1 and u > AH:
                    turn_o(u // AH - 1)
            turn_o(NT - 1)

            pe.wait_ge(mix_copied, 2 * NT)
            for c in range(4):
                pe.wait_ge(slot_loaded[OUT_SLOT + c], 32)
            for j in range(NT):
                if j >= 2:
                    pe.wait_ge(mixed_added, j - 1)
                for c in range(4):
                    w = dense(OUT_SLOT + c)
                    for k in range(KD):
                        last = mm(ps[:, 2 * (j % 2) + c // 2, (c % 2) * WCOL:(c % 2 + 1) * WCOL],
                                  hT[:, k, j * P:(j + 1) * P], w[:, k, :], start=(k == 0), stop=(k == KD - 1))
                last.then_inc(mixed, 1)
                if j >= 1:
                    turn_rows(1, j - 1)
            turn_rows(1, NT - 1)

            pe.wait_ge(norm_copied, 2 * NT)
            pe.wait_ge(mixed_added, NT)
            pe.wait_ge(router_loaded, 16)
            for j in range(NT):
                for k in range(KD):
                    last = mm(ps[:, 0, j * E:(j + 1) * E], xbcT[:, k, j * P:(j + 1) * P], wrt[:, k, :],
                              start=(k == 0), stop=(k == KD - 1))
            last.then_inc(routed, 1)
            pe.wait_ge(p_loaded, 16)
            for j in range(NT):
                for k in range(2):
                    last = nc.tensor.transpose(ps[:, 2 + k, j * P:(j + 1) * P], p_rows[:, j, k * P:(k + 1) * P], ident[:])
            last.then_inc(p_turned, 1)
            pe.wait_ge(chosen_ready, 1)
            for j in range(NT):
                for i in range(j + 1):
                    mm(ps[:, 1, j * E:(j + 1) * E], (strict if i == j else ones)[:], chosen[:, i, :],
                       start=(i == 0), stop=(i == j))
            for i in range(NT):
                last = mm(ps[:, 1, NT * E:(NT + 1) * E], ones[:], chosen[:, i, :], start=(i == 0), stop=(i == NT - 1))
            last.then_inc(placed, 1)

            def sum_idx(i):
                pe.wait_ge(hot_ready, i + 1)
                if not is_static(i, 1):
                    pe.wait_ge(out_idx_ready, i)
                if not is_static(i, 2):
                    pe.wait_ge(xT_ready, i)
                for j in range(NT):
                    last = mm(ps[:, 6, 0:1], slot_hot[:, j, :], val_tab[:, j, bass.ds(i, 1)], start=(j == 0), stop=(j == NT - 1))
                last.then_inc(idx_summed, 1)

            def turn_rows_of(rows, done):
                for k in range(KD):
                    last = nc.tensor.transpose(ps[:, 6 + k // 4, (k % 4) * B:(k % 4 + 1) * B], rows[:, k * P:(k + 1) * P], ident[:])
                last.then_inc(done, 1)

            def turn_x(i):
                pe.wait_ge(gathered, 16 * (i + 1))
                pe.wait_ge(out_idx_ready, 2 if is_static(i, 1) else i + 1)
                if not is_static(i, 2):
                    pe.wait_ge(aT_ready, i - 1)
                turn_rows_of(xg, x_turned)

            def turn_a(i):
                pe.wait_ge(act_ready, i + 1)
                pe.wait_ge(xT_ready, i + 2)
                pe.wait_ge(out_idx_ready, i + 3)
                turn_rows_of(up_s, a_turned)

            def products(banks, hi, lo, w, b, stop):
                for part, (x_part, w_part) in enumerate(((hi, w_hi[b]), (lo, w_hi[b]), (hi, w_lo[b]))):
                    for a, bank in enumerate(banks):
                        last = mm(ps[:, bank, :], x_part, w_part[:, w + a * BANK:w + (a + 1) * BANK],
                                  start=False, stop=(stop and part == 2))
                return last

            def up_chunk(i, k):
                if k == 0:
                    pe.wait_ge(xT_ready, i + 1)
                    pe.wait_ge(up_hot_ready, i + 1)
                    if is_static(i, 1):
                        pe.wait_ge(bias_ready, 1)
                    else:
                        pe.wait_ge(gate_clamped, i)
                        pe.wait_ge(up_clamped, i)
                    for a in range(4):
                        mm(ps[:, a, :], up_hot[:], bias_tab[0:2 * E, a * BANK:(a + 1) * BANK], start=True, stop=False)
                if k in UP_WHOLE:
                    pe.wait_ge(up_loaded[k], 16 * (i + 1))
                    for a in range(4):
                        last = mm(ps[:, a, :], x_whole[:, UP_WHOLE.index(k), :], ring[:, k % RING, a * BANK:(a + 1) * BANK],
                                  start=False, stop=(k == KD - 1))
                else:
                    q = UP_SPLIT.index(k)
                    pe.wait_ge(up_lo, i * len(UP_SPLIT) + q + 1)
                    last = products(range(4), xT_hi[:, k, :], xT_lo[:, k, :], 0, q % PARTS, k == KD - 1)
                last.then_inc(up_used, 1)

            def down(i):
                pe.wait_ge(aT_ready, i + 1)
                pe.wait_ge(down_hot_ready, i + 1)
                if not is_static(i, 1):
                    pe.wait_ge(y_ready, i)
                for a in range(2):
                    mm(ps[:, 4 + a, :], down_hot[:], bias_tab[0:2 * E, 2 * D + a * BANK:2 * D + (a + 1) * BANK], start=True, stop=False)
                for c in range(DOWN_CHUNKS):
                    if c in DOWN_WHOLE:
                        pe.wait_ge(down_loaded[c], 16 * (i + 1))
                    else:
                        q = DOWN_SPLIT.index(c)
                        pe.wait_ge(down_lo, i * len(DOWN_SPLIT) + q + 1)
                    for f in range(2):
                        if c in DOWN_WHOLE:
                            for a in range(2):
                                last = mm(ps[:, 4 + a, :], a_whole[:, 2 * DOWN_WHOLE.index(c) + f, :],
                                          ring[:, 2 + c, f * D + a * BANK:f * D + (a + 1) * BANK], start=False, stop=False)
                        else:
                            last = products((4, 5), aT_hi[:, 2 * c + f, :], aT_lo[:, 2 * c + f, :], f * D, q,
                                            c == DOWN_CHUNKS - 1 and f == 1)
                    last.then_inc(down_used, 1)

            def expert_step(i):
                for k in range(KD // 2):
                    up_chunk(i, k)
                if not is_static(i, 1):
                    turn_a(i - 1)
                for k in range(KD // 2, KD):
                    up_chunk(i, k)
                turn_x(i + 1)
                if not is_static(i, 1):
                    down(i - 1)
                sum_idx(i + 2)

            sum_idx(0)
            sum_idx(1)
            turn_x(0)
            for i in range(PEELED):
                expert_step(i)
            pe.wait_ge(tables_ready, 1)
            n_blocks = pe.value_load(extra_count[0:1, 0:1], min_val=0, max_val=EXTRA) + E
            with pe.Fori(PEELED, n_blocks) as i:
                expert_step(i)
            turn_a(n_blocks - 1)
            down(n_blocks - 1)

            def project_p(j):
                if j >= 2:
                    pe.wait_ge(pw_copied, j - 1)
                for h in range(2):
                    for k in range(2):
                        last = mm(ps[:, 2 * (j % 2) + h, :], pT[:, k, j * P:(j + 1) * P], w_proj_s[:, k, h * BANK:(h + 1) * BANK],
                                  start=(k == 0), stop=(k == 1))
                last.then_inc(pw_done, 1)

            def project_gate(j):
                pe.wait_ge(norm_copied, 2 * NT + j + 1)
                if j >= 2:
                    pe.wait_ge(gate_sig, j - 1)
                else:
                    pe.wait_ge(pw_copied, NT)
                for c in range(4):
                    w = dense(c)
                    for k in range(KD):
                        last = mm(ps[:, 2 * (j % 2) + c // 2, (c % 2) * WCOL:(c % 2 + 1) * WCOL], hT[:, k, j * P:(j + 1) * P],
                                  w[:, k, :], start=(k == 0), stop=(k == KD - 1))
                last.then_inc(ple_done, 1)

            pe.wait_ge(tail_loaded, 32)
            pe.wait_ge(p_copied, 1)
            for j in range(NT):
                project_p(j)
            for c in range(4):
                pe.wait_ge(slot_loaded[c], 32)
            turn_rows(2, 0)
            project_gate(0)
            for j in range(1, NT):
                turn_rows(2, j)
                project_gate(j)

        @block.vector
        def _(dve):
            v = nc.vector
            steps = 0

            def link(ins):
                nonlocal steps
                steps += 1
                ins.then_inc(dve_step, 1)
                dve.wait_ge(dve_step, steps)

            def heads(table):
                return table.unsqueeze(2).to_broadcast([P, NH, HP])

            def by_head(a):
                return a.rearrange("p (h e) -> p h e", h=NH)

            def rms(col, n, eps):
                dve.wait_ge(squared, col + 1)
                v.tensor_scalar(ssq[:, col:col + 1], ssq[:, col:col + 1], 1.0 / n, eps, ALU.mult, ALU.add).then_inc(scaled, 1)
                dve.wait_ge(rooted, col + 1)
                link(v.reciprocal(rstd[:, col:col + 1], rstd[:, col:col + 1]))

            def norm_rows(stage, j, col=None):
                s = stage * NT + j
                col = s if col is None else col
                rms(col, D, NORM_EPS)
                if j >= 2:
                    dve.wait_ge(norm_turned, s - 1)
                if stage == 1 and j >= 2:
                    dve.wait_ge(hn_stored[j - 2], 16)
                if stage == 1:
                    ins = v.scalar_tensor_tensor(hrow[:, j % 2, :], xres[:, j, :], rstd[:, col:col + 1], gffn, ALU.mult, ALU.mult)
                else:
                    ins = v.tensor_scalar(hrow[:, j % 2, :], xres[:, j, :], rstd[:, col:col + 1], None, ALU.mult)
                ins.then_inc(normed, 1)

            def norm_copy(stage, j, dst, gain):
                s = stage * NT + j
                dve.wait_ge(norm_turned, s + 1)
                b = 4 + 2 * (j % 2)
                src = ps[:, b:b + 2, :].rearrange("p a (k t) -> p (a k) t", k=4)
                if gain is None:
                    ins = v.tensor_copy(dst[:, :, j * P:(j + 1) * P], src)
                else:
                    ins = v.tensor_tensor(dst[:, :, j * P:(j + 1) * P], src,
                                          gain[:].unsqueeze(2).to_broadcast([P, KD, P]), ALU.mult)
                ins.then_inc(norm_copied, 1)

            dve.wait_ge(gain_loaded, 16)
            norm_rows(0, 0)
            for j in range(NT):
                if j + 1 < NT:
                    norm_rows(0, j + 1)
                norm_copy(0, j, hT, gmix_t)

            dve.wait_ge(params_loaded, 16 * N_PARAMS)
            for t in range(CT):
                dve.wait_ge(projected, t + 1)
                u = ps[:, t % 2, :]
                link(v.tensor_scalar(xbcT[:, t, :], u, convw_t[:, CONV - 1, t:t + 1], convb_t[:, t:t + 1], ALU.mult, ALU.add))
                for k in range(CONV - 1):
                    back = CONV - 1 - k
                    ins = v.scalar_tensor_tensor(xbcT[:, t, back:T], u[:, 0:T - back], convw_t[:, k, t:t + 1],
                                                 xbcT[:, t, back:T], ALU.mult, ALU.add)
                    if k < CONV - 2:
                        link(ins)
                ins.then_inc(conv_done, 1)

            NHT = NT * NH
            d = [dts[:, i, :] for i in range(12)]
            dve.wait_ge(dt_projected, 1)
            link(v.tensor_tensor(d[0].rearrange("p (j h) -> p j h", h=NH),
                                 ps[:, 2, 0:NHT].rearrange("p (j h) -> p j h", h=NH),
                                 dtb[:].unsqueeze(1).to_broadcast([P, NT, NH]), ALU.add))
            link(v.tensor_scalar(d[2], d[0], -1.0, None, ALU.mult))
            v.tensor_tensor(d[1], d[0], d[2], ALU.min).then_inc(dt_pre, 1)
            dve.wait_ge(dt_e, 1)
            v.tensor_scalar(d[3], d[2], 1.0, None, ALU.add).then_inc(dt_u, 1)
            dve.wait_ge(dt_u, 1)
            link(v.tensor_scalar(d[5], d[3], -1.0, None, ALU.add))
            link(v.tensor_scalar(d[7], d[5], 0.0, None, ALU.is_equal))
            link(v.tensor_tensor(d[5], d[5], d[7], ALU.add))
            link(v.reciprocal(d[5], d[5]))
            link(v.tensor_tensor(d[5], d[5], d[2], ALU.mult))
            dve.wait_ge(dt_l, 1)
            link(v.tensor_tensor(d[4], d[4], d[7], ALU.add))
            link(v.tensor_tensor(d[4], d[4], d[5], ALU.mult))
            link(v.tensor_scalar(d[0], d[0], 0.0, None, ALU.max))
            link(v.tensor_tensor(d[0], d[0], d[4], ALU.add))
            link(v.tensor_scalar(alog[:], alog[:], -1.0, None, ALU.mult))
            v.tensor_tensor(d[6].rearrange("p (j h) -> p j h", h=NH), d[0].rearrange("p (j h) -> p j h", h=NH),
                            alog[:].unsqueeze(1).to_broadcast([P, NT, NH]), ALU.mult).then_inc(adt_ready, 1)
            dve.wait_ge(late_params_loaded, 16 * N_LATE_PARAMS)
            for i in range(2):
                ins = v.tensor_tensor_reduce(out=lam_prod[:, i, :], in0=lamv[:, 2 * i, :], in1=lamv[:, 2 * i + 1, :],
                                             scale=1.0, scalar=0.0, op0=ALU.mult, op1=ALU.add,
                                             accum_out=lam_s[:, i:i + 1])
                if i == 0:
                    link(ins)
            ins.then_inc(lam_dots, 1)
            dve.wait_ge(lam_exps, 1)
            link(v.tensor_tensor(lam_s[:, 0:1], lam_s[:, 2:3], lam_s[:, 3:4], ALU.subtract))
            link(v.tensor_scalar(lam_s[:, 0:1], lam_s[:, 0:1], LAM_INIT, None, ALU.add))
            link(v.tensor_scalar(subln[:], subln[:], 1.0 - LAM_INIT, None, ALU.mult))

            dve.wait_ge(cum_ready, 1)
            link(v.tensor_copy(dts[:, 8, :], ps[:, 3, 0:NHT]))
            link(v.tensor_copy(dts[:, 10, :], ps[:, 3, NHT:2 * NHT]))
            link(v.tensor_scalar(dts[:, 11, :], d[8], -1.0, None, ALU.mult))
            v.tensor_tensor(dts[:, 9, :], d[10], d[8], ALU.subtract).then_inc(cum_args, 1)
            dve.wait_ge(cum_exp, 1)

            def hcol(i, c):
                return dts[:, i, c * NH:(c + 1) * NH]

            half = SSD_W // NG
            for c in range(NT):
                dve.wait_ge(ssd_turned, c + 1)
                link(v.tensor_copy(xs_tok, ps[:, 2, :]))
                link(v.tensor_copy(b_tok, ps[:, 3, 0:NG * NS]))
                v.tensor_tensor(cb_mask, ps[:, 3, NG * NS:].rearrange("p (q l) -> p q l", q=NG),
                                upper[:].unsqueeze(1).to_broadcast([P, NG, P]), ALU.mult).then_inc(ssd_read, 1)
                dve.wait_ge(ssd_read, c + 1)
                for h in range(NH):
                    ins = v.tensor_scalar(seg[:, h, :], ps[:, 4 + h // HG, (h % HG) * P:(h % HG + 1) * P],
                                          dts[:, 11, c * NH + h:c * NH + h + 1], 0.0, ALU.add, ALU.min)
                    if h < NH - 1:
                        link(ins)
                ins.then_inc(seg_ready, 1)
                link(v.tensor_tensor(by_head(xdt), by_head(xs_tok), heads(hcol(0, c)), ALU.mult))
                link(v.tensor_tensor(by_head(xdec), by_head(xdt), heads(hcol(9, c)), ALU.mult))
                link(v.tensor_tensor(by_head(xs_tok), by_head(xs_tok), heads(dskip[:]), ALU.mult))
                dve.wait_ge(seg_exp, c + 1)
                for q in range(NG):
                    ins = v.tensor_tensor(seg[:, q * HG:(q + 1) * HG, :], seg[:, q * HG:(q + 1) * HG, :],
                                          cb_mask[:, q:q + 1, :].to_broadcast([P, HG, P]), ALU.mult)
                    if q < NG - 1:
                        link(ins)
                ins.then_inc(decay_ready, 1)
                dve.wait_ge(ssd_summed, c + 1)
                dve.wait_ge(proj_copied, NT)
                if c >= 1:
                    link(v.tensor_tensor(by_head(yrow), by_head(ps[:, 7, :]), heads(hcol(8, c)), ALU.mult))
                    link(v.tensor_tensor(yrow, yrow, xs_tok, ALU.add))
                    link(v.tensor_tensor(yrow, ps[:, 6, :], yrow, ALU.add))
                else:
                    link(v.tensor_tensor(yrow, ps[:, 6, :], xs_tok, ALU.add))
                v.tensor_tensor(yrow, yrow, zs[:, c, :], ALU.mult).then_inc(y_gated, 1)
                if c == 0:
                    v.tensor_copy(prevT, ps[:, 2, :]).then_inc(state_updated, 1)
                else:
                    link(v.tensor_tensor(by_head(prevT), by_head(prevT), heads(hcol(10, c)), ALU.mult))
                    v.tensor_tensor(prevT, ps[:, 2, :], prevT, ALU.add).then_inc(state_updated, 1)
                dve.wait_ge(state_updated, c + 1)
                dve.wait_ge(y_squared, NG * (c + 1))
                v.tensor_scalar(ssq[:, 16:16 + NG], ssq[:, 16:16 + NG], 1.0 / half, SSD_NORM_EPS, ALU.mult, ALU.add).then_inc(y_mean, 1)
                dve.wait_ge(y_root, c + 1)
                link(v.reciprocal(att_s[:, 0, 0:NG], rstd[:, 16:16 + NG]))
                for q in range(NG):
                    cols = slice(q * half, (q + 1) * half)
                    ins = v.scalar_tensor_tensor(zs[:, c, cols], yrow[:, cols], att_s[:, 0, q:q + 1], normw[:, cols],
                                                 ALU.mult, ALU.mult)
                    if q < NG - 1:
                        link(ins)
                ins.then_inc(y_ssd_ready, 1)
                dve.wait_ge(y_ssd_ready, c + 1)

            def max_unit(u):
                b = u // AH
                nk = (b + 1) * P
                for j in range(2):
                    dve.wait_ge(scored, 2 * u + j + 1)
                    s = ps[:, (u % 2) * 2 + j, :]
                    link(v.tensor_tensor(s[:, b * P:nk], s[:, b * P:nk], attmask[:], ALU.add))
                    v.tensor_reduce(out=att_s[:, u % 2, j:j + 1], in_=s[:, 0:nk], axis=AX, op=ALU.max,
                                    negate=True).then_inc(maxed, 1)

            def weigh(u):
                nk = (u // AH + 1) * P
                a = att_s[:, u % 2, :]
                dve.wait_ge(expd, 2 * u + 2)
                link(v.reciprocal(a[:, 4:6], a[:, 2:4]))
                link(v.tensor_tensor(a[:, 5:6], a[:, 5:6], lam_s[:, 0:1], ALU.mult))
                if u >= 2:
                    dve.wait_ge(w_turned, u - 1)
                link(v.tensor_scalar(wgt[:, u % 2, 0:nk], probs[:, u % 2, 1, 0:nk], a[:, 5:6], None, ALU.mult))
                v.scalar_tensor_tensor(wgt[:, u % 2, 0:nk], probs[:, u % 2, 0, 0:nk], a[:, 4:5], wgt[:, u % 2, 0:nk],
                                       ALU.mult, ALU.subtract).then_inc(weighed, 1)

            def norm_o(b):
                dve.wait_ge(attended, AH * (b + 1))
                if b >= 1:
                    dve.wait_ge(mix_turned, NT + b)
                v.tensor_copy(orow, ps[:, 6 + b % 2, :]).then_inc(o_copied, 1)
                dve.wait_ge(o_squared, AH * (b + 1))
                v.tensor_scalar(lam_s[:, 4:4 + AH], lam_s[:, 4:4 + AH], 1.0 / VH, SUBLN_EPS, ALU.mult, ALU.add).then_inc(o_mean, 1)
                dve.wait_ge(o_root, b + 1)
                link(v.reciprocal(o_inv[:], rstd[:, 16:16 + AH]))
                for h in range(AH):
                    cols = slice(h * VH, (h + 1) * VH)
                    ins = v.scalar_tensor_tensor(orow[:, cols], orow[:, cols], o_inv[:, h:h + 1], subln[:], ALU.mult, ALU.mult)
                    if h < AH - 1:
                        link(ins)
                ins.then_inc(o_ready, 1)

            max_unit(0)
            for u in range(UNITS):
                if u + 1 < UNITS:
                    max_unit(u + 1)
                weigh(u)
                if u % AH == 0 and u:
                    norm_o(u // AH - 1)
            norm_o(NT - 1)

            dve.wait_ge(gffn_loaded, 16)
            for j in range(NT):
                dve.wait_ge(mixed, j + 1)
                xj = xres[:, j, :].rearrange("p (a n) -> p a n", a=2)
                v.tensor_tensor(xj, ps[:, 2 * (j % 2):2 * (j % 2) + 2, :], xj, ALU.add).then_inc(mixed_added, 1)
                norm_rows(1, j)
                if j >= 1:
                    norm_copy(1, j - 1, xbcT, None)
            norm_copy(1, NT - 1, xbcT, None)

            dve.wait_ge(routed, 1)
            v.tensor_tensor(logits, ps[:, 0, 0:NT * E].rearrange("p (j e) -> p j e", e=E),
                            brt[:].unsqueeze(1).to_broadcast([P, NT, E]), ALU.add).then_inc(logits_read, 1)
            dve.wait_ge(logits_read, 1)
            for j in range(NT):
                link(v.max(top8[:, j, :], logits[:, j, :]))
            for j in range(NT):
                link(v.max_index(topi_u[:, j, :], top8[:, j, :], logits[:, j, :]))
            v.tensor_tensor(gates[:], top8[:, :, 0:TOPK], top8[:, :, 0:1].to_broadcast([P, NT, TOPK]),
                            ALU.subtract).then_inc(top_shifted, 1)
            link(v.tensor_copy(topi, topi_u))
            for r in range(TOPK):
                dst = chosen if r == 0 else onehot
                link(v.tensor_tensor(dst, iota[:, 0:E].unsqueeze(1).to_broadcast([P, NT, E]),
                                     topi[:, :, r:r + 1].to_broadcast([P, NT, E]), ALU.is_equal))
                if r == 1:
                    link(v.tensor_scalar(rankv, onehot, float(r), None, ALU.mult))
                elif r > 1:
                    link(v.scalar_tensor_tensor(rankv, onehot, float(r), rankv, ALU.mult, ALU.add))
                if r:
                    ins = v.tensor_tensor(chosen, chosen, onehot, ALU.add)
                    if r < TOPK - 1:
                        link(ins)
            ins.then_inc(chosen_ready, 1)
            link(v.tensor_tensor(rankv, rankv, token4[:].unsqueeze(2).to_broadcast([P, NT, E]), ALU.add))
            link(v.tensor_scalar(val_tab[:, :, 0:E], rankv, -float(EMPTY), None, ALU.add))
            dve.wait_ge(placed, 1)
            link(v.tensor_copy(counts, ps[:, 1, NT * E:(NT + 1) * E]))
            link(v.tensor_copy(onehot, ps[:, 1, 0:NT * E].rearrange("p (j e) -> p j e", e=E)))
            link(v.tensor_scalar(onehot, onehot, 1.0, None, ALU.add))
            link(v.tensor_tensor(onehot, onehot, chosen, ALU.mult))
            link(v.tensor_scalar(pos_tab[:, :, 0:E], onehot, -1.0, None, ALU.add))

            def hot(i):
                if not isinstance(i, int) or i >= 1:
                    dve.wait_ge(idx_summed, i)
                for j in range(NT):
                    ins = v.tensor_scalar(slot_hot[:, j, :], iota[:, 0:B], pos_tab[:, j, bass.ds(i, 1)], None, ALU.is_equal)
                ins.then_inc(hot_ready, 1)

            def indices(i):
                dve.wait_ge(idx_summed, i + 1)
                v.tensor_scalar(out_idx[0:B, bass.ds(i, 1)], ps[0:B, 6, 0:1],
                                float(EMPTY), None, ALU.add).then_inc(out_idx_ready, 1)
                dve.wait_ge(out_idx_ready, i + 1)
                if not isinstance(i, int) or i >= 1:
                    dve.wait_ge(gathered, 16 * i)
                v.tensor_scalar(gather_idx[0:B, :], out_idx[0:B, bass.ds(i, 1)], 2, None,
                                ALU.arith_shift_right).then_inc(gather_idx_ready, 1)

            dve.wait_ge(norm_turned, 2 * NT)
            for j in range(NT):
                dve.wait_ge(hn_stored[j], 16)
            link(v.memset(xg, 0.0))
            hot(0)
            indices(0)
            hot(1)
            indices(1)
            dve.wait_ge(p_turned, 1)
            v.tensor_copy(pT, ps[:, 2:4, :]).then_inc(p_copied, 1)

            turned = ps[:, 6:8, :].rearrange("p a (k n) -> p (a k) n", n=B)

            def copy_x(i):
                dve.wait_ge(xT_hi_ready, 2 * (i + 1))
                v.tensor_tensor(xT_lo, turned, xT_hi, ALU.subtract).then_inc(xT_ready, 1)

            def copy_a(i):
                dve.wait_ge(aT_hi_ready, 2 * (i + 1))
                v.tensor_tensor(aT_lo, turned, aT_hi, ALU.subtract).then_inc(aT_ready, 1)

            def split_lo(i, q):
                chunk, b = SPLITS[q], q % PARTS
                if q < len(UP_SPLIT):
                    dve.wait_ge(up_hi, i * len(UP_SPLIT) + q + 1)
                    v.tensor_tensor(w_lo[b][:], ring[:, chunk % RING, :], w_hi[b][:], ALU.subtract).then_inc(up_lo, 1)
                else:
                    q -= len(UP_SPLIT)
                    dve.wait_ge(down_hi, (i - 1) * len(DOWN_SPLIT) + q + 1)
                    v.tensor_tensor(w_lo[b][:], ring[:, 2 + chunk, :], w_hi[b][:], ALU.subtract).then_inc(down_lo, 1)

            def mark_expert(i, dst, done):
                expert = float(i) if isinstance(i, int) else block_expert_f[0:2 * E, bass.ds(i, 1)]
                v.tensor_scalar(dst[:], expert_of[0:2 * E, :].to_broadcast([2 * E, B]), expert, None, ALU.is_equal).then_inc(done, 1)

            def up_expert(i):
                if not is_static(i, 1):
                    dve.wait_ge(up_used, (i - 1) * UP_CHUNKS + 1)
                mark_expert(i, up_hot, up_hot_ready)

            def down_expert(i):
                if not is_static(i, 1):
                    dve.wait_ge(down_used, (i - 1) * DOWN_CHUNKS + 1)
                mark_expert(i, down_hot, down_hot_ready)

            def clamp(i):
                dve.wait_ge(up_used, UP_CHUNKS * (i + 1))
                four = [g_or_u.rearrange("p (a n) -> p a n", a=4) for g_or_u in (gate_s, up_s)]
                v.tensor_scalar(four[0], ps[:, 0:4, 0:BANK:2], SWIGLU_LIMIT, None, ALU.min).then_inc(gate_clamped, 1)
                v.tensor_scalar(four[1], ps[:, 0:4, 1:BANK:2], -SWIGLU_LIMIT, SWIGLU_LIMIT, ALU.max, ALU.min).then_inc(up_clamped, 1)

            def activate(i):
                dve.wait_ge(gate_clamped, i + 1)
                dve.wait_ge(up_clamped, i + 1)
                v.scalar_tensor_tensor(up_s, up_s, 1.0, gate_s, ALU.add, ALU.mult).then_inc(swish, 1)
                dve.wait_ge(swish, i + 1)
                dve.wait_ge(sigmoided, i + 1)
                v.tensor_tensor(up_s, up_s, sig_s, ALU.mult).then_inc(act_ready, 1)

            def place_scatter(i):
                if not is_static(i, 1):
                    dve.wait_ge(scattered, 16 * i)
                v.tensor_copy(scatter_idx[:], out_idx[:, bass.ds(i, 1)]).then_inc(scatter_idx_ready, 1)

            def expert_step(i):
                if not is_static(i, 1):
                    for q in range(PARTS):
                        split_lo(i, q)
                    indices(i + 1)
                hot(i + 2)
                if not is_static(i, 2):
                    place_scatter(i - 2)
                if not is_static(i, 1):
                    down_expert(i - 1)
                for q in range(PARTS, len(UP_SPLIT)):
                    split_lo(i, q)
                if not is_static(i, 1):
                    copy_a(i - 1)
                    for q in range(len(UP_SPLIT), len(SPLITS)):
                        split_lo(i, q)
                clamp(i)
                copy_x(i + 1)
                up_expert(i + 1)
                activate(i)

            link(v.tensor_scalar(expert_tmp[:], expert_of[:], float(E), -float(E), ALU.is_ge, ALU.mult))
            link(v.tensor_tensor(expert_of[:], expert_of[:], expert_tmp[:], ALU.add))
            up_expert(0)
            dve.wait_ge(bias_hi, 1)
            v.tensor_tensor(bias_tab[E:2 * E, :], bias_rows[E:2 * E, :], bias_tab[E:2 * E, :], ALU.subtract).then_inc(bias_ready, 1)
            for q in range(PARTS):
                split_lo(0, q)
            copy_x(0)
            expert_step(0)
            dve.wait_ge(top_exp, 1)
            link(v.tensor_reduce(out=small[:, 0:NT], in_=gates[:], axis=AX, op=ALU.add))
            link(v.reciprocal(small[:, 0:NT], small[:, 0:NT]))
            link(v.tensor_tensor(gates[:], gates[:], small[:, 0:NT].unsqueeze(2).to_broadcast([P, NT, TOPK]), ALU.mult))
            link(v.tensor_scalar(extra, counts, float(B), None, ALU.is_gt))
            for m in range(2, -(-T // B)):
                link(v.tensor_scalar(cum, counts, float(m * B), None, ALU.is_gt))
                link(v.tensor_tensor(extra, extra, cum, ALU.add))
            link(v.tensor_copy(cum, extra))
            for s in (1, 2, 4, 8, 16):
                link(v.tensor_copy(counts, cum))
                link(v.tensor_tensor(cum[:, s:E], counts[:, s:E], counts[:, 0:E - s], ALU.add))
            wide = [P, EXTRA, E]
            link(v.tensor_tensor(sel, cum.unsqueeze(1).to_broadcast(wide), iota[:, 0:EXTRA].unsqueeze(2).to_broadcast(wide), ALU.is_le))
            link(v.tensor_reduce(out=blk_e, in_=sel, axis=AX, op=ALU.add))
            link(v.tensor_tensor(sel, sel, extra.unsqueeze(1).to_broadcast(wide), ALU.mult))
            link(v.tensor_reduce(out=blk_b, in_=sel, axis=AX, op=ALU.add))
            link(v.tensor_tensor(blk_b, iota[:, 0:EXTRA], blk_b, ALU.subtract))
            link(v.tensor_scalar(blk_b, blk_b, 1.0, float(B), ALU.add, ALU.mult))
            link(v.tensor_tensor(sel, iota[:, 0:E].unsqueeze(1).to_broadcast(wide), blk_e.unsqueeze(2).to_broadcast(wide), ALU.is_equal))
            for j in range(NT):
                for src, dst in ((pos_tab, pos_tab), (val_tab, val_tab)):
                    link(v.tensor_tensor(sel2, sel, src[:, j, 0:E].unsqueeze(1).to_broadcast(wide), ALU.mult))
                    link(v.tensor_reduce(out=dst[:, j, E:NB], in_=sel2, axis=AX, op=ALU.add))
                link(v.tensor_tensor(pos_tab[:, j, E:NB], pos_tab[:, j, E:NB], blk_b, ALU.subtract))
            link(v.memset(pos_tab[:, :, NB:NCOL], -1.0))
            link(v.memset(val_tab[:, :, NB:NCOL], 0.0))
            link(v.tensor_copy(block_expert[:, 0:E], iota[:, 0:E]))
            link(v.tensor_scalar(blk_e, blk_e, float(E - 1), None, ALU.min))
            link(v.tensor_copy(block_expert[:, E:NB], blk_e))
            link(v.tensor_copy(block_expert_f[:, 0:E], iota[:, 0:E]))
            link(v.tensor_copy(block_expert_f[:, E:NB], blk_e))
            link(v.memset(block_expert_f[:, NB:NCOL], 0.0))
            v.tensor_copy(extra_count[:], cum[:, E - 1:E]).then_inc(tables_ready, 1)
            dve.wait_ge(tables_ready, 1)

            for i in range(1, PEELED):
                expert_step(i)
            n_blocks = dve.value_load(extra_count[0:1, 0:1], min_val=0, max_val=EXTRA) + E
            with dve.Fori(PEELED, n_blocks) as i:
                expert_step(i)
            indices(n_blocks + 1)
            place_scatter(n_blocks - 2)
            down_expert(n_blocks - 1)
            copy_a(n_blocks - 1)
            for q in range(len(UP_SPLIT), len(SPLITS)):
                split_lo(n_blocks, q)
            place_scatter(n_blocks - 1)
            dve.wait_ge(gathered, 16 * (n_blocks + 1))

            def sum_experts(s, j):
                b = j % Y_BUFS
                dve.wait_ge(y_loaded[b], 16 * (j // Y_BUFS + 1))
                ys = ring[:, 4 + 2 * b:6 + 2 * b, :].rearrange("p a (r d) -> p (a r) d", d=D)
                for r in range(TOPK):
                    ins = v.scalar_tensor_tensor(xres[:, j, :], ys[:, r, :], gates[:, j, r:r + 1], xres[:, j, :], ALU.mult, ALU.add)
                    if r < TOPK - 1:
                        link(ins)
                ins.then_inc(y_summed, 1)
                norm_rows(2, j, s)
                norm_copy(2, j, hT, gple_t)

            def add_ple(j):
                dve.wait_ge(gate_sig, j + 1)
                link(v.tensor_tensor(sig_t[:, j % 2, :], pw[:, j, :], sig_t[:, j % 2, :], ALU.mult))
                v.tensor_tensor(xres[:, j, :], xres[:, j, :], sig_t[:, j % 2, :], ALU.add).then_inc(ple_added, 1)

            def finish_tile(s, j):
                rms(s, D, NORM_EPS)
                if j >= 2:
                    dve.wait_ge(out_stored[j - 2], 16)
                v.scalar_tensor_tensor(out_row[:, j % 2, :], xres[:, j, :], rstd[:, s:s + 1], gfin, ALU.mult, ALU.mult).then_inc(out_ready, 1)

            for s, (final, j) in enumerate(TAIL_ORDER):
                if final:
                    add_ple(j)
                    finish_tile(2 * NT + s, j)
                else:
                    sum_experts(2 * NT + s, j)


_INS = ['x', 'p', 'g_mix', 'w_in', 'conv_w', 'conv_b', 'dt_bias', 'a_log', 'd_skip', 'ssd_norm_w',
        'lam_q1', 'lam_k1', 'lam_q2', 'lam_k2', 'subln_w', 'w_out', 'g_ffn', 'w_router', 'b_router',
        'w_up', 'b_up', 'w_down', 'b_down', 'g_ple', 'w_ple_gate', 'w_ple_proj', 'g_final']


def kernel(**inputs):
    import numpy as _np
    import concourse.bacc as _bacc
    from concourse import mybir as _mybir
    from concourse.bass_utils import run_bass_kernel_spmd as _run

    nc = _bacc.Bacc("TRN2", target_bir_lowering=False, num_devices=1)
    arrays, args = {}, []
    for name in _INS:
        a = _np.ascontiguousarray(inputs[name])
        arrays[f"in_{name}_dram"] = a
        args.append(nc.dram_tensor(f"in_{name}_dram", a.shape, _mybir.dt.from_np(a.dtype), kind="ExternalInput").ap())
    shape = tuple(inputs["x"].shape)
    args.append(nc.dram_tensor("out_0_dram", shape, _mybir.dt.float32, kind="ExternalOutput").ap())
    hybrid_ssd_diffattn_moe_ple_kernel(nc, *args)
    r = _run(nc, [arrays], core_ids=[0])
    return r.results[0]["out_0_dram"]
```

```python
import math
from contextlib import ExitStack

import concourse.bass as bass
from concourse import mybir

F32 = mybir.dt.float32
F32R = mybir.dt.float32r
I32 = mybir.dt.int32
U32 = mybir.dt.uint32
ALU = mybir.AluOpType
ACT = mybir.ActivationFunctionType
AX = mybir.AxisListType.X

P = 128
BANK = 512

NORM_EPS = 1e-6
SUBLN_EPS = 1e-5
SSD_NORM_EPS = 1e-5
LAM_INIT = 0.8 - 0.6 * math.exp(-0.3 * 0)
SWIGLU_LIMIT = 7.0
SWIGLU_ALPHA = 1.702
MASKED = -1e30
N_CONSTS = 13
N_PARAMS = 8
N_LATE_PARAMS = 8
X2_NORM = (0, 1, 2, 4)
X3_NORM = (3, 5, 6, 7)


def hybrid_ssd_diffattn_moe_ple_kernel(
    nc, x, p, g_mix, w_in, conv_w, conv_b, dt_bias, a_log, d_skip, ssd_norm_w,
    lam_q1, lam_k1, lam_q2, lam_k2, subln_w, w_out, g_ffn, w_router, b_router,
    w_up, b_up, w_down, b_down, g_ple, w_ple_gate, w_ple_proj, g_final, out,
):
    T, D = x.shape[1], x.shape[2]
    NT = T // P
    KD = D // P
    PLE = p.shape[3]
    SSD_W = ssd_norm_w.shape[1]
    NH = dt_bias.shape[1]
    HP = SSD_W // NH
    NG = 2
    HG = NH // NG
    NS = P
    CONV = conv_w.shape[1]
    CH = conv_w.shape[2]
    CT = CH // P
    XT = SSD_W // P
    ATT_W = D - SSD_W
    AH = 4
    DH = lam_q1.shape[1]
    VH = 2 * DH
    E = w_router.shape[2]
    TOPK = 4
    OFF_Z, OFF_XBC = 0, SSD_W
    OFF_DT = OFF_XBC + CH
    OFF_Q = OFF_DT + NH
    OFF_K = OFF_Q + ATT_W
    OFF_V = OFF_K + ATT_W

    B = P
    EXTRA = T * TOPK // B
    NB = E + EXTRA
    NCOL = NB + 2
    PEELED = 3
    EMPTY = 4096

    UP_CHUNKS, DOWN_CHUNKS = KD, KD // 2
    UP_WHOLE, DOWN_WHOLE = (0, 4), (0,)
    UP_SPLIT = [k for k in range(UP_CHUNKS) if k not in UP_WHOLE]
    DOWN_SPLIT = [c for c in range(DOWN_CHUNKS) if c not in DOWN_WHOLE]
    SPLITS = UP_SPLIT + DOWN_SPLIT
    PARTS = 3
    assert len(SPLITS) % PARTS == 0 and len(DOWN_SPLIT) == PARTS

    SLOT = 2048
    SLOTS = 12
    RING = 6
    IN_CHUNKS, IN_RING = 12, 4
    IN_PARTS = 3
    OUT_SLOT = 8
    Y_BUFS = 2
    WCOL = SLOT // KD

    hn_rows = nc.dram_tensor("hn_rows", (T, D), F32).ap()
    y_rows = nc.dram_tensor("y_rows", (T * TOPK, D), F32).ap()

    x_v = x.rearrange("b (j p) d -> p (b j) d", p=P)
    out_v = out.rearrange("b (j p) d -> p (b j) d", p=P)
    hn_v = hn_rows.rearrange("(j p) d -> p j d", p=P)
    y_v = y_rows.rearrange("(j p r) d -> j p (r d)", p=P, r=TOPK)
    w_in_v = w_in.rearrange("o (k p) n -> p (o k) n", p=P)
    w_out_v = w_out.rearrange("o (k p) n -> p (o k) n", p=P)
    w_gate_v = w_ple_gate.rearrange("o (k p) n -> p (o k) n", p=P)
    w_proj_v = w_ple_proj.rearrange("o (k p) n -> p (o k) n", p=P)

    ctx = ExitStack()
    with ctx:
        place = {}

        def sb(name, shape, dt=F32):
            place[name] = -(-nc.sbuf_base // 32) * 32
            return ctx.enter_context(nc.sbuf_tensor(name, shape, dt))

        def sem(name):
            return ctx.enter_context(nc.semaphore(name))

        ring = sb("ring", [P, SLOTS, SLOT])
        xres = sb("xres", [P, NT, D])
        hT = sb("hT", [P, KD, T])
        xbcT = sb("xbcT", [P, CT, T])
        qkT = sb("qkT", [P, 2 * AH, T])
        zs = sb("zs", [P, NT, SSD_W])
        vt = sb("vt", [P, NT, ATT_W])
        work = sb("work", [P, 4608])

        ident = sb("ident", [P, P])
        upper = sb("upper", [P, P])
        strict = sb("strict", [P, P])
        ones = sb("ones", [P, P])
        attmask = sb("attmask", [P, P])
        iota = sb("iota", [P, P])
        token4_i = sb("token4_i", [P, NT], I32)
        token4 = sb("token4", [P, NT])

        convw_t = sb("convw_t", [P, CONV, CT])
        convb_t = sb("convb_t", [P, CT])
        dtb = sb("dtb", [P, NH])
        alog = sb("alog", [P, NH])
        dskip = sb("dskip", [P, NH])
        normw = sb("normw", [P, SSD_W])
        subln = sb("subln", [P, VH])
        brt = sb("brt", [P, E])
        wdt = sb("wdt", [P, KD, NH])
        wdt_hi = sb("wdt_hi", [P, KD, NH], F32R)
        wdt_lo = sb("wdt_lo", [P, KD, NH], F32R)
        expert_of = sb("expert_of", [P, 1])
        expert_tmp = sb("expert_tmp", [P, 1])
        expert_i = sb("expert_i", [P, 1], I32)

        ssq = sb("ssq", [P, 20])
        rstd = sb("rstd", [P, 20])
        dts = sb("dts", [P, 12, NT * NH])
        lam_s = sb("lam_s", [P, 8])
        att_s = sb("att_s", [P, 2, 8])
        o_sum = sb("o_sum", [P, NT * AH])
        o_inv = sb("o_inv", [P, NT * AH])
        gates = sb("gates", [P, NT, TOPK])
        pos_tab = sb("pos_tab", [P, NT, NCOL])
        val_tab = sb("val_tab", [P, NT, NCOL])
        block_expert_f = sb("block_expert_f", [P, NCOL])
        block_expert = sb("block_expert", [P, NCOL], I32)
        extra_count = sb("extra_count", [P, 1], I32)
        out_idx = sb("out_idx", [P, NCOL], I32)
        gather_idx = sb("gather_idx", [P, 1], I32)
        scatter_idx = sb("scatter_idx", [P, 1], I32)

        def over(name, host, at, cols):
            return nc.alloc_sbuf_tensor_at(name, [P, cols], F32R, offset=place[host] + 4 * at)

        w_hi = [over(f"w_hi{b}", "ring", (RING + 2 * b) * SLOT, SLOT) for b in range(PARTS)]
        w_lo = [over(f"w_lo{b}", "ring", (RING + 2 * b + 1) * SLOT, SLOT) for b in range(PARTS)]
        xT_hi, xT_lo, aT_hi, aT_lo = [over(name, "xbcT", q * D, D).ap().rearrange("p (k n) -> p k n", n=B)
                                      for q, name in enumerate(("xT_hi", "xT_lo", "aT_hi", "aT_lo"))]
        in_hi = [over(f"in_hi{b}", "ring", (IN_RING + 2 * b) * SLOT, SLOT) for b in range(IN_PARTS)]
        in_lo = [over(f"in_lo{b}", "ring", (IN_RING + 2 * b + 1) * SLOT, SLOT) for b in range(IN_PARTS)]
        h_hi = over("h_hi", "hT", 0, KD * T).ap().rearrange("p (k t) -> p k t", k=KD)
        h_lo = over("h_lo", "ring", (IN_RING + 2 * IN_PARTS) * SLOT, KD * T).ap().rearrange("p (k t) -> p k t", k=KD)
        gate_lo = [over(f"gate_lo{c}", "ring", c * SLOT, SLOT) for c in range(4)]
        gate_hi = [w_hi[1], w_lo[1], w_hi[2], w_lo[2]]
        gT = [(xT_hi, xT_lo), (aT_hi, aT_lo)]
        bias_tab = over("bias_tab", "hT", 0, 3 * D)
        up_hot = sb("up_hot", [2 * E, B], F32R)
        down_hot = sb("down_hot", [2 * E, B], F32R)

        def carve(buf, at, shape):
            n = 1
            for s in shape:
                n *= s
            v = buf[:, at:at + n]
            if len(shape) == 2:
                v = v.rearrange("p (a b) -> p a b", a=shape[0])
            if len(shape) == 3:
                v = v.rearrange("p (a b c) -> p a b c", a=shape[0], b=shape[1])
            return v

        hrow = carve(work, 0, [2, D])
        gmix = carve(work, 2 * D, [D])
        dt_rows = work[0:NH, 3 * D:3 * D + T]
        xs_tok = carve(work, 0, [SSD_W])
        xdt = carve(work, SSD_W, [SSD_W])
        xdec = carve(work, 2 * SSD_W, [SSD_W])
        b_tok = carve(work, 3 * SSD_W, [NG * NS])
        cb_mask = carve(work, 3 * SSD_W + 256, [NG, P])
        seg = carve(work, 4 * SSD_W, [NH, P])
        prevT = carve(work, 6 * SSD_W, [SSD_W])
        yrow = carve(work, 7 * SSD_W, [SSD_W])
        ysq = carve(work, 8 * SSD_W, [SSD_W])
        probs = carve(work, 0, [2, 2, T])
        wgt = carve(work, 4 * T, [2, T])
        wgtT = carve(work, 6 * T, [2, T])
        logits = carve(work, 2048, [NT, E])
        logit_rows = work[0:E, 4 * D:4 * D + T]
        earlier = carve(work, 2880, [NT + 1, E])
        top8 = carve(work, 2176, [NT, 8])
        topi_u = carve(work, 2208, [NT * 8]).bitcast(U32).rearrange("p (a b) -> p a b", a=NT)
        topi = carve(work, 2240, [NT, 8])
        chosen = carve(work, 2272, [NT, E])
        rankv = carve(work, 2400, [NT, E])
        onehot = carve(work, 2528, [NT, E])
        small = carve(work, 2656, [64])
        counts = carve(work, 2720, [E])
        extra = carve(work, 2752, [E])
        cum = carve(work, 2784, [E])
        blk_e = carve(work, 2816, [EXTRA])
        blk_b = carve(work, 2848, [EXTRA])
        sel = carve(work, 2880, [EXTRA, E])
        sel2 = carve(work, 2880 + EXTRA * E, [EXTRA, E])
        qk_flat = qkT[:, :, :].rearrange("p a b -> p (a b)")
        vt_flat = vt[:, :, :].rearrange("p a b -> p (a b)")
        zs_flat = zs[:, :, :].rearrange("p a b -> p (a b)")
        gate_s, up_s, sig_s = [carve(qk_flat, q * D, [D]) for q in range(3)]
        bias_rows = qk_flat[:, D:4 * D]
        x_whole = carve(vt_flat, 0, [len(UP_WHOLE), B])
        a_whole = carve(vt_flat, 2 * B, [2 * len(DOWN_WHOLE), B])
        gfin = vt_flat[:, D:2 * D]
        wrt = carve(zs_flat, 0, [KD, E])
        gffn = zs_flat[:, D:2 * D]
        xg = zs_flat[:, 0:D]
        yg = zs_flat[:, D:2 * D]
        slot_hot = carve(work, 0, [NT, B])
        hT_flat = hT[:, :, :].rearrange("p a b -> p (a b)")
        xbc_flat = xbcT[:, :, :].rearrange("p a b -> p (a b)")
        p_rows = carve(vt_flat, 0, [NT, PLE])
        pT = carve(hT_flat, 3 * D, [2, T])
        w_proj_s = carve(work, 2 * D, [2, D])
        pw = carve(hT_flat, 0, [NT, D])
        gple = vt_flat[:, 0:D]
        sig_t = carve(qk_flat, D, [2, D])
        squares = carve(qk_flat, 0, [D])
        lam_prod = carve(work, 4 * D, [2, DH])
        lamv = carve(work, 4 * D + 2 * DH, [4, DH])
        iota_i = work[:, 4 * D + 6 * DH:4 * D + 6 * DH + P].bitcast(I32)
        osq = xbcT[:, 0, :]
        orow = xbcT[:, NT:2 * NT, :]
        out_row = carve(zs_flat, 0, [2, D])

        def dense(slot):
            return ring[:, slot, :].rearrange("p (k n) -> p k n", k=KD)

        ps = ctx.enter_context(nc.psum_tensor("ps", [P, 8, BANK], F32))

        x_loaded = [sem(f"x_loaded{j}") for j in range(NT)]
        gain_loaded = sem("gain_loaded")
        params_loaded = sem("params_loaded")
        late_params_loaded = sem("late_params_loaded")
        router_loaded = sem("router_loaded")
        bias_rows_loaded = sem("bias_rows_loaded")
        slot_loaded = [sem(f"slot_loaded{s}") for s in range(SLOTS)]
        up_loaded = [sem(f"up_loaded{k}") for k in range(UP_CHUNKS)]
        down_loaded = [sem(f"down_loaded{c}") for c in range(DOWN_CHUNKS)]
        consts_ready = sem("consts_ready")
        squared = sem("squared")
        scaled = sem("scaled")
        rooted = sem("rooted")
        normed = sem("normed")
        h_hi_ready = sem("h_hi_ready")
        in_hi_ready = sem("in_hi_ready")
        in_lo_ready = sem("in_lo_ready")
        wdt_hi_ready = sem("wdt_hi_ready")
        wdt_lo_ready = sem("wdt_lo_ready")
        dt_by_head = sem("dt_by_head")
        dt_rows_ready = sem("dt_rows_ready")
        norm_turned = sem("norm_turned")
        norm_copied = sem("norm_copied")
        bias_hi = sem("bias_hi")
        bias_ready = sem("bias_ready")
        projected = sem("projected")
        conv_done = sem("conv_done")
        conv_silu = sem("conv_silu")
        proj_copied = sem("proj_copied")
        dt_projected = sem("dt_projected")
        dt_pre = sem("dt_pre")
        dt_e = sem("dt_e")
        dt_u = sem("dt_u")
        dt_l = sem("dt_l")
        adt_ready = sem("adt_ready")
        cum_ready = sem("cum_ready")
        cum_args = sem("cum_args")
        cum_exp = sem("cum_exp")
        ssd_turned = sem("ssd_turned")
        ssd_read = sem("ssd_read")
        seg_ready = sem("seg_ready")
        seg_exp = sem("seg_exp")
        decay_ready = sem("decay_ready")
        ssd_summed = sem("ssd_summed")
        state_updated = sem("state_updated")
        y_gated = sem("y_gated")
        y_squared = sem("y_squared")
        y_mean = sem("y_mean")
        y_root = sem("y_root")
        y_ssd_ready = sem("y_ssd_ready")
        mix_turned = sem("mix_turned")
        mix_copied = sem("mix_copied")
        lam_dots = sem("lam_dots")
        lam_exps = sem("lam_exps")
        scored = sem("scored")
        maxed = sem("maxed")
        expd = sem("expd")
        weighed = sem("weighed")
        w_turned = sem("w_turned")
        w_copied = sem("w_copied")
        attended = sem("attended")
        o_copied = sem("o_copied")
        o_squared = sem("o_squared")
        o_mean = sem("o_mean")
        o_root = sem("o_root")
        o_ready = sem("o_ready")
        mixed = sem("mixed")
        mixed_added = sem("mixed_added")
        hn_stored = [sem(f"hn_stored{j}") for j in range(NT)]
        routed = sem("routed")
        logit_rows_ready = sem("logit_rows_ready")
        logits_turned = sem("logits_turned")
        logits_read = sem("logits_read")
        top_shifted = sem("top_shifted")
        top_exp = sem("top_exp")
        chosen_ready = sem("chosen_ready")
        placed = sem("placed")
        tables_ready = sem("tables_ready")
        dve_step = sem("dve_step")
        act_step = sem("act_step")
        hot_ready = sem("hot_ready")
        idx_summed = sem("idx_summed")
        out_idx_ready = sem("out_idx_ready")
        gather_idx_ready = sem("gather_idx_ready")
        pool_started = sem("pool_started")
        gathered = sem("gathered")
        x_turned = sem("x_turned")
        xT_hi_ready = sem("xT_hi_ready")
        xT_ready = sem("xT_ready")
        up_hot_ready = sem("up_hot_ready")
        down_hot_ready = sem("down_hot_ready")
        up_hi = sem("up_hi")
        up_lo = sem("up_lo")
        down_hi = sem("down_hi")
        down_lo = sem("down_lo")
        up_used = sem("up_used")
        down_used = sem("down_used")
        gate_clamped = sem("gate_clamped")
        up_clamped = sem("up_clamped")
        sigmoided = sem("sigmoided")
        swish = sem("swish")
        act_ready = sem("act_ready")
        a_turned = sem("a_turned")
        aT_hi_ready = sem("aT_hi_ready")
        aT_ready = sem("aT_ready")
        y_ready = sem("y_ready")
        scatter_idx_ready = sem("scatter_idx_ready")
        scattered = sem("scattered")
        p_loaded = sem("p_loaded")
        pw_done = sem("pw_done")
        pw_copied = sem("pw_copied")
        tail_loaded = sem("tail_loaded")
        p_turned = sem("p_turned")
        p_copied = sem("p_copied")
        y_loaded = [sem(f"y_loaded{b}") for b in range(Y_BUFS)]
        y_summed = sem("y_summed")
        gate_hi_ready = sem("gate_hi_ready")
        gate_lo_ready = sem("gate_lo_ready")
        gT_hi_ready = sem("gT_hi_ready")
        ple_done = sem("ple_done")
        gate_sig = sem("gate_sig")
        ple_added = sem("ple_added")
        out_ready = sem("out_ready")
        out_stored = [sem(f"out_stored{j}") for j in range(NT)]

        N_PROJ_CH = CT
        G_Z = CT
        G_QK = G_Z + NT
        G_V = G_QK + 2 * AH
        N_GROUPS = G_V + NT
        Z_CHUNKS, V_CHUNKS = (4, 5), (10, 11)
        G_IN = [2 * m + 2 for m in range(4)] + [G_QK] * 2 + [G_QK + 2 * m + 2 for m in range(4)] + [N_GROUPS] * 2
        PER_CHUNK = (N_GROUPS - G_QK) // NT
        UNITS = NT * AH

        def wait_up_free(eng, i, k):
            if k in UP_WHOLE:
                eng.wait_ge(up_used, i * UP_CHUNKS + k + 1)
            else:
                eng.wait_ge(up_lo, i * len(UP_SPLIT) + UP_SPLIT.index(k) + 1)

        def wait_down_free(eng, i, c):
            if c in DOWN_WHOLE:
                eng.wait_ge(down_used, i * DOWN_CHUNKS + c + 1)
            else:
                eng.wait_ge(down_lo, i * len(DOWN_SPLIT) + DOWN_SPLIT.index(c) + 1)

        def is_static(i, least):
            return isinstance(i, int) and i < least

        block = ctx.enter_context(nc.Block())

        @block.sync
        def _(sp):
            for j in range(NT):
                sp.dma_start(xres[:, j, :], x_v[:, j, :]).then_inc(x_loaded[j], 16)
            sp.wait_ge(gain_loaded, 16)
            sp.wait_ge(params_loaded, 16 * N_PARAMS)

            def load_dense(slot, src, col):
                sp.dma_start(dense(slot), src[:, :, col:col + WCOL]).then_inc(slot_loaded[slot], 16)

            for m in range(IN_CHUNKS):
                if m >= IN_RING:
                    sp.wait_ge(in_lo_ready, m - IN_RING + 1)
                slot = m % IN_RING
                if m in Z_CHUNKS or m in V_CHUNKS:
                    first, at = (Z_CHUNKS[0], OFF_Z) if m in Z_CHUNKS else (V_CHUNKS[0], OFF_V)
                    ks = slice((m - first) * KD // 2, (m - first + 1) * KD // 2)
                    sp.dma_start(ring[:, slot, :].rearrange("p (k n) -> p k n", n=BANK),
                                 w_in_v[:, ks, at:at + BANK]).then_inc(slot_loaded[slot], 16)
                elif m < Z_CHUNKS[0]:
                    load_dense(slot, w_in_v, OFF_XBC + WCOL * m)
                else:
                    load_dense(slot, w_in_v, OFF_Q + WCOL * (m - Z_CHUNKS[1] - 1))

            def load_up(e, k):
                sp.dma_start(ring[:, k % RING, :], w_up[0, e, k * P:(k + 1) * P, :] if isinstance(e, int)
                             else w_up[0, bass.ds(e, 1), k * P:(k + 1) * P, :].rearrange("a p n -> (a p) n")
                             ).then_inc(up_loaded[k], 16)

            def load_down(e, c):
                rows = slice(c * 2 * P, (c + 1) * 2 * P)
                src = (w_down[0, e, rows, :] if isinstance(e, int)
                       else w_down[0, bass.ds(e, 1), rows, :].rearrange("a q n -> (a q) n"))
                sp.dma_start(ring[:, 2 + c, :].rearrange("p (f n) -> p f n", f=2),
                             src.rearrange("(f p) n -> p f n", p=P)).then_inc(down_loaded[c], 16)

            for k in range(RING):
                if k < IN_RING:
                    sp.wait_ge(in_lo_ready, IN_CHUNKS - IN_RING + k + 1)
                else:
                    sp.wait_ge(projected, G_IN[9])
                load_up(0, k)
            sp.wait_ge(projected, N_GROUPS)
            for c in range(4):
                load_dense(OUT_SLOT + c, w_out_v, WCOL * c)
            sp.wait_ge(mix_turned, NT)
            sp.dma_start(wrt, w_router.rearrange("o (k p) e -> p (o k) e", p=P)).then_inc(router_loaded, 16)
            sp.dma_start(gffn, g_ffn.to_broadcast([P, D])).then_inc(gain_loaded, 16)
            sp.wait_ge(attended, UNITS)
            for q in range(2):
                rows = slice(q * E, (q + 1) * E)
                sp.dma_start(bias_rows[rows, 0:2 * D], b_up[0]).then_inc(bias_rows_loaded, 16)
                sp.dma_start(bias_rows[rows, 2 * D:3 * D], b_down[0]).then_inc(bias_rows_loaded, 16)
            sp.dma_start(p_rows, p.rearrange("o b (j p) c -> p (o b j) c", p=P)).then_inc(p_loaded, 16)
            sp.dma_start(gfin, g_final.rearrange("(a n) -> a n", a=1).to_broadcast([P, D])).then_inc(tail_loaded, 16)
            for j in range(NT):
                sp.wait_ge(normed, NT + j + 1)
                sp.dma_start(hn_v[:, j, :], hrow[:, j % 2, :]).then_inc(hn_stored[j], 16)
            def load_block(i, e, before):
                for k in range(UP_CHUNKS):
                    if k >= RING:
                        wait_up_free(sp, i, k - RING)
                    elif k + RING < UP_CHUNKS:
                        wait_up_free(sp, i - 1, k + RING)
                    elif is_static(i, 2):
                        wait_up_free(sp, 0, k)
                    else:
                        wait_down_free(sp, i - 2, k - 2)
                    load_up(e, k)
                for c in range(DOWN_CHUNKS):
                    wait_up_free(sp, i, 2 + c)
                    load_down(before, c)

            for k in range(RING, UP_CHUNKS):
                wait_up_free(sp, 0, k - RING)
                load_up(0, k)
            for i in range(1, PEELED):
                load_block(i, i, i - 1)
            sp.wait_ge(tables_ready, 1)
            sp.dma_start(w_proj_s, w_proj_v).then_inc(tail_loaded, 16)
            n = sp.value_load(extra_count[0:1, 0:1], min_val=0, max_val=EXTRA) + E
            with sp.Fori(PEELED, n) as i:
                e = sp.value_load(block_expert[0:1, bass.ds(i, 1)], min_val=0, max_val=E - 1)
                before = sp.value_load(block_expert[0:1, bass.ds(i - 1, 1)], min_val=0, max_val=E - 1)
                load_block(i, e, before)
            last = sp.value_load(block_expert[0:1, bass.ds(n - 1, 1)], min_val=0, max_val=E - 1)
            for c in range(DOWN_CHUNKS):
                wait_down_free(sp, n - 2, c)
                load_down(last, c)
            for c in range(4):
                if c < 2:
                    wait_up_free(sp, n - 1, RING + c)
                else:
                    wait_down_free(sp, n - 1, c - 2)
                sp.dma_start(ring[:, c, :].rearrange("p (f n) -> p f n", f=2),
                             w_gate_v[:, 2 * c:2 * c + 2, :]).then_inc(slot_loaded[c], 16)
            sp.wait_ge(down_used, (n - 1) * DOWN_CHUNKS + 1)
            sp.dma_start(gple, g_ple.to_broadcast([P, D])).then_inc(gain_loaded, 16)
            sp.wait_ge(scattered, n * 16)
            for j in range(NT):
                if j >= Y_BUFS:
                    sp.wait_ge(y_summed, j - Y_BUFS + 1)
                s = 4 + 2 * (j % Y_BUFS)
                sp.dma_start(ring[:, s:s + 2, :].rearrange("p a n -> p (a n)"), y_v[j]).then_inc(y_loaded[j % Y_BUFS], 16)
            for j in range(NT):
                sp.wait_ge(out_ready, j + 1)
                sp.dma_start(out_v[:, j, :], out_row[:, j % 2, :]).then_inc(out_stored[j], 16)
            for j in range(NT):
                sp.wait_ge(out_stored[j], 16)

        @block.gpsimd
        def _(pool):
            n = 0

            def link(ins):
                nonlocal n
                n += 1
                ins.then_inc(consts_ready, 1)
                pool.wait_ge(consts_ready, n)

            link(nc.gpsimd.memset(ident[:], 0.0))
            link(nc.gpsimd.affine_select(out=ident[:], in_=ident[:], compare_op=ALU.not_equal, fill=1.0,
                                         base=0, pattern=[[-1, P]], channel_multiplier=1))
            link(nc.gpsimd.memset(ones[:], 1.0))
            link(nc.gpsimd.affine_select(out=upper[:], in_=ones[:], compare_op=ALU.is_ge, fill=0.0,
                                         base=0, pattern=[[1, P]], channel_multiplier=-1))
            link(nc.gpsimd.affine_select(out=strict[:], in_=ones[:], compare_op=ALU.is_gt, fill=0.0,
                                         base=0, pattern=[[1, P]], channel_multiplier=-1))
            link(nc.gpsimd.memset(attmask[:], 0.0))
            link(nc.gpsimd.affine_select(out=attmask[:], in_=attmask[:], compare_op=ALU.is_ge, fill=MASKED,
                                         base=0, pattern=[[-1, P]], channel_multiplier=1))
            link(nc.gpsimd.iota(iota_i, pattern=[[1, P]], base=0, channel_multiplier=0))
            link(nc.gpsimd.tensor_copy(iota[:], iota_i))
            link(nc.gpsimd.iota(token4_i[:], pattern=[[TOPK * P, NT]], base=0, channel_multiplier=TOPK))
            link(nc.gpsimd.tensor_copy(token4[:], token4_i[:]))
            link(nc.gpsimd.iota(expert_i[:], pattern=[[0, 1]], base=0, channel_multiplier=1))
            link(nc.gpsimd.tensor_copy(expert_of[:], expert_i[:]))
            assert n == N_CONSTS

            last_token = pool.alloc_register("last_token")
            pool.reg_mov(last_token, T - 1)
            last_row = pool.alloc_register("last_row")
            pool.reg_mov(last_row, T * TOPK - 1)

            def gather(i):
                pool.wait_ge(gather_idx_ready, i + 1)
                if not isinstance(i, int) or i >= 1:
                    pool.wait_ge(x_turned, i)
                pool.sem_inc(pool_started, 1)
                nc.gpsimd.indirect_dma_start(
                    xg[0:B, :], None, hn_rows, bass.IndirectOffsetOnAxis(ap=gather_idx[0:B, :], axis=0),
                    bounds_check=last_token, oob_is_err=False).then_inc(gathered, 16)

            def scatter(i):
                pool.wait_ge(y_ready, i + 1)
                pool.wait_ge(scatter_idx_ready, i + 1)
                pool.sem_inc(pool_started, 1)
                nc.gpsimd.indirect_dma_start(
                    y_rows, bass.IndirectOffsetOnAxis(ap=scatter_idx[0:B, :], axis=0), yg[0:B, :], None,
                    bounds_check=last_row, oob_is_err=False).then_inc(scattered, 16)

            for j in range(NT):
                pool.wait_ge(hn_stored[j], 16)
            gather(0)
            gather(1)
            pool.wait_ge(tables_ready, 1)
            n_blocks = pool.value_load(extra_count[0:1, 0:1], min_val=0, max_val=EXTRA) + E
            gather(2)
            gather(3)
            scatter(0)
            with pool.Fori(PEELED, n_blocks) as i:
                gather(i + 1)
                scatter(i - 2)
            scatter(n_blocks - 2)
            scatter(n_blocks - 1)
            pool.wait_ge(gathered, (n_blocks + 1) * 16)
            pool.wait_ge(scattered, n_blocks * 16)

        @block.scalar
        def _(act):
            steps = 0

            def link(ins):
                nonlocal steps
                steps += 1
                ins.then_inc(act_step, 1)
                act.wait_ge(act_step, steps)

            def row(v):
                return v.to_broadcast([P, v.shape[1]])

            with nc.allow_non_contiguous_dma(reason="small parameters by partition"):
                act.dma_start(gmix, row(g_mix)).then_inc(gain_loaded, 16)
                act.dma_start(wdt[:], w_in_v[:, :, OFF_DT:OFF_DT + NH]).then_inc(params_loaded, 16)
                act.dma_start(convb_t[:], conv_b.rearrange("o (k p) -> p (o k)", p=P)).then_inc(params_loaded, 16)
                for k in range(CONV):
                    act.dma_start(convw_t[:, k, :], conv_w[0, k].rearrange("(t p) -> p t", p=P)).then_inc(params_loaded, 16)
                act.dma_start(dtb[:], row(dt_bias)).then_inc(params_loaded, 16)
                act.dma_start(alog[:], row(a_log)).then_inc(params_loaded, 16)

            def load_late_params():
                with nc.allow_non_contiguous_dma(reason="small parameters by partition"):
                    for dst, src in ((dskip[:], d_skip), (normw[:], ssd_norm_w),
                                     (lamv[:, 0, :], lam_q1), (lamv[:, 1, :], lam_k1), (lamv[:, 2, :], lam_q2),
                                     (lamv[:, 3, :], lam_k2), (subln[:], subln_w), (brt[:], b_router)):
                        act.dma_start(dst, row(src)).then_inc(late_params_loaded, 16)

            def square_of_tile(col, j):
                if col >= 1:
                    act.wait_ge(squared, col)
                nc.scalar.activation(squares, xres[:, j, :], ACT.Square,
                                     accum_out=ssq[:, col:col + 1]).then_inc(squared, 1)

            def root_of_tile(col):
                act.wait_ge(scaled, col + 1)
                nc.scalar.activation(rstd[:, col:col + 1], ssq[:, col:col + 1], ACT.Sqrt).then_inc(rooted, 1)

            def copy_h(j):
                act.wait_ge(norm_turned, j + 1)
                b = 4 + 2 * (j % 2)
                nc.scalar.activation(h_hi[:, :, j * P:(j + 1) * P], ps[:, b:b + 2, :].rearrange("p a (k t) -> p (a k) t", k=4),
                                     ACT.Copy).then_inc(h_hi_ready, 1)

            def split_in(m):
                if m >= IN_PARTS:
                    act.wait_ge(projected, G_IN[m - IN_PARTS])
                act.wait_ge(slot_loaded[m % IN_RING], 16 * (m // IN_RING + 1))
                nc.scalar.activation(in_hi[m % IN_PARTS][:], ring[:, m % IN_RING, :], ACT.Copy).then_inc(in_hi_ready, 1)

            for j in range(NT):
                act.wait_ge(x_loaded[j], 16)
                square_of_tile(j, j)
                root_of_tile(j)
                if 1 <= j < 3:
                    copy_h(j - 1)
            split_in(0)
            copy_h(2)
            copy_h(3)
            split_in(1)
            load_late_params()
            act.wait_ge(params_loaded, 16 * N_PARAMS)
            nc.scalar.activation(wdt_hi[:], wdt[:], ACT.Copy).then_inc(wdt_hi_ready, 1)
            split_in(2)
            link(nc.scalar.activation(alog[:], alog[:], ACT.Exp))
            for t in range(CT):
                act.wait_ge(conv_done, t + 1)
                nc.scalar.activation(xbcT[:, t, :], xbcT[:, t, :], ACT.Silu).then_inc(conv_silu, 1)
                if t % 2:
                    split_in(IN_PARTS + t // 2)
            act.wait_ge(dt_pre, 1)
            nc.scalar.activation(dts[:, 2, :], dts[:, 1, :], ACT.Exp).then_inc(dt_e, 1)
            act.wait_ge(dt_u, 1)
            nc.scalar.activation(dts[:, 4, :], dts[:, 3, :], ACT.Ln).then_inc(dt_l, 1)

            act.wait_ge(lam_dots, 1)
            nc.scalar.activation(lam_s[:, 2:4], lam_s[:, 0:2], ACT.Exp).then_inc(lam_exps, 1)

            def copy_group(g):
                act.wait_ge(projected, g + 1)
                bank = ps[:, g % 2, :]
                if g < G_QK:
                    ins = nc.scalar.activation(zs[:, g - G_Z, :], bank, ACT.Silu)
                elif g < G_QK + AH:
                    ins = nc.scalar.activation(qkT[:, g - G_QK, :], bank, ACT.Copy, scale=float(DH) ** -0.5)
                elif g < G_V:
                    ins = nc.scalar.activation(qkT[:, g - G_QK, :], bank, ACT.Copy)
                else:
                    ins = nc.scalar.activation(vt[:, g - G_V, :], bank, ACT.Copy)
                ins.then_inc(proj_copied, 1)

            for g in range(G_Z, G_QK):
                copy_group(g)
            split_in(7)
            split_in(8)
            act.wait_ge(cum_args, 1)
            nc.scalar.activation(dts[:, 8:11, :], dts[:, 8:11, :], ACT.Exp).then_inc(cum_exp, 1)

            g = G_QK
            for c in range(NT):
                act.wait_ge(seg_ready, c + 1)
                nc.scalar.activation(seg, seg, ACT.Exp).then_inc(seg_exp, 1)
                for _ in range(PER_CHUNK - 1):
                    copy_group(g)
                    g += 1
                if c == 1:
                    split_in(10)
                act.wait_ge(y_gated, c + 1)
                half = SSD_W // NG
                if c >= 1:
                    act.wait_ge(y_root, c)
                for q in range(NG):
                    ins = nc.scalar.activation(ysq[:, q * half:(q + 1) * half], yrow[:, q * half:(q + 1) * half],
                                               ACT.Square, accum_out=ssq[:, 16 + q:17 + q])
                    ins.then_inc(y_squared, 1)
                act.wait_ge(y_mean, c + 1)
                nc.scalar.activation(rstd[:, 16:16 + NG], ssq[:, 16:16 + NG], ACT.Sqrt).then_inc(y_root, 1)
                copy_group(g)
                g += 1
                if c == 0:
                    split_in(9)
                elif c == 1:
                    split_in(11)

            for c in range(NT):
                act.wait_ge(mix_turned, c + 1)
                nc.scalar.activation(hT[:, 0:XT, c * P:(c + 1) * P], ps[:, 6 + c % 2, :].rearrange("p (k t) -> p k t", k=XT),
                                     ACT.Copy).then_inc(mix_copied, 1)

            def exp_unit(u):
                nk = (u // AH + 1) * P
                for j in range(2):
                    s = 2 * u + j
                    act.wait_ge(maxed, s + 1)
                    if u >= 2:
                        act.wait_ge(weighed, u - 1)
                    nc.scalar.activation(probs[:, u % 2, j, 0:nk], ps[:, (u % 2) * 2 + j, 0:nk], ACT.Exp,
                                         bias=att_s[:, u % 2, j:j + 1],
                                         accum_out=att_s[:, u % 2, 2 + j:3 + j]).then_inc(expd, 1)

            def copy_w(u):
                nk = (u // AH + 1) * P
                act.wait_ge(w_turned, u + 1)
                if u >= 2:
                    act.wait_ge(attended, u - 1)
                nc.scalar.activation(wgtT[:, u % 2, 0:nk], ps[:, 4 + u % 2, 0:nk], ACT.Copy).then_inc(w_copied, 1)

            def square_o(b):
                act.wait_ge(o_copied, b + 1)
                if b >= 1:
                    act.wait_ge(o_squared, AH * b)
                for h in range(AH):
                    nc.scalar.activation(osq[:, h * VH:(h + 1) * VH], orow[:, b, h * VH:(h + 1) * VH], ACT.Square,
                                         accum_out=o_sum[:, b * AH + h:b * AH + h + 1]).then_inc(o_squared, 1)

            def copy_o(b):
                act.wait_ge(mix_turned, NT + b + 1)
                nc.scalar.activation(hT[:, XT:KD, b * P:(b + 1) * P], ps[:, 6 + b % 2, :].rearrange("p (k t) -> p k t", k=AH),
                                     ACT.Copy).then_inc(mix_copied, 1)

            exp_unit(0)
            for u in range(UNITS):
                if u + 1 < UNITS:
                    exp_unit(u + 1)
                copy_w(u)
                if u % AH == 0 and u:
                    square_o(u // AH - 1)
            square_o(NT - 1)
            act.wait_ge(o_mean, 1)
            nc.scalar.activation(o_sum[:], o_sum[:], ACT.Sqrt).then_inc(o_root, 1)
            for b in range(NT):
                copy_o(b)

            def split_hi(i, q, after_loop=False):
                chunk, b = SPLITS[q], q % PARTS
                is_up = q < len(UP_SPLIT)
                if q >= PARTS:
                    if after_loop:
                        act.wait_ge(down_used, (i - 2) * DOWN_CHUNKS + chunk + 1)
                    else:
                        act.wait_ge(up_used, i * UP_CHUNKS + SPLITS[q - PARTS] + 1)
                elif is_static(i, 1):
                    if q == 0:
                        act.wait_ge(projected, N_GROUPS)
                    elif q == 1:
                        act.wait_ge(mixed, NT)
                elif is_static(i, 2):
                    act.wait_ge(up_used, UP_SPLIT[len(UP_SPLIT) - PARTS + q] + 1)
                else:
                    act.wait_ge(down_used, (i - 2) * DOWN_CHUNKS + DOWN_SPLIT[q] + 1)
                if is_up:
                    act.wait_ge(up_loaded[chunk], 16 * (i + 1))
                    nc.scalar.activation(w_hi[b][:], ring[:, chunk % RING, :], ACT.Copy).then_inc(up_hi, 1)
                else:
                    act.wait_ge(down_loaded[chunk], 16 * i)
                    nc.scalar.activation(w_hi[b][:], ring[:, 2 + chunk, :], ACT.Copy).then_inc(down_hi, 1)

            split_hi(0, 0)
            for j in range(NT):
                act.wait_ge(mixed_added, j + 1)
                square_of_tile(NT + j, j)
                root_of_tile(NT + j)
            def sigmoid_of(i):
                act.wait_ge(gate_clamped, i + 1)
                nc.scalar.activation(sig_s, gate_s, ACT.Sigmoid, scale=SWIGLU_ALPHA).then_inc(sigmoided, 1)

            def copy_y(i):
                act.wait_ge(down_used, (i + 1) * DOWN_CHUNKS)
                if not isinstance(i, int) or i >= 1:
                    act.wait_ge(scattered, i * 16)
                nc.scalar.activation(yg.rearrange("p (a n) -> p a n", a=2), ps[:, 4:6, :], ACT.Copy).then_inc(y_ready, 1)

            turned = ps[:, 6:8, :].rearrange("p a (k n) -> p (a k) n", n=B)

            def copy_x(i):
                act.wait_ge(x_turned, i + 1)
                nc.scalar.activation(x_whole, turned[:, UP_WHOLE[0]:UP_WHOLE[1] + 1:UP_WHOLE[1] - UP_WHOLE[0], :], ACT.Copy).then_inc(xT_hi_ready, 1)
                nc.scalar.activation(xT_hi, turned, ACT.Copy).then_inc(xT_hi_ready, 1)

            def copy_a(i):
                act.wait_ge(a_turned, i + 1)
                nc.scalar.activation(a_whole, turned[:, 0:2 * len(DOWN_WHOLE), :], ACT.Copy).then_inc(aT_hi_ready, 1)
                nc.scalar.activation(aT_hi, turned, ACT.Copy).then_inc(aT_hi_ready, 1)

            def expert_step(i):
                for q in range(PARTS):
                    if not is_static(i, 1):
                        split_hi(i, q)
                if not is_static(i, 2):
                    copy_y(i - 2)
                for q in range(PARTS, len(UP_SPLIT)):
                    split_hi(i, q)
                if not is_static(i, 1):
                    copy_a(i - 1)
                    for q in range(len(UP_SPLIT), len(SPLITS)):
                        split_hi(i, q)
                sigmoid_of(i)
                copy_x(i + 1)

            act.wait_ge(bias_rows_loaded, 64)
            act.wait_ge(mixed, NT)
            nc.scalar.activation(bias_tab[0:2 * E, :], bias_rows[0:2 * E, :], ACT.Copy).then_inc(bias_hi, 1)
            for q in range(1, PARTS):
                split_hi(0, q)
            act.wait_ge(top_shifted, 1)
            nc.scalar.activation(gates[:, :, :], gates[:, :, :], ACT.Exp).then_inc(top_exp, 1)
            act.wait_ge(p_turned, 1)
            nc.scalar.activation(pT, ps[:, 2:4, :], ACT.Copy).then_inc(p_copied, 1)

            copy_x(0)
            for i in range(PEELED):
                expert_step(i)
            act.wait_ge(tables_ready, 1)
            n_blocks = act.value_load(extra_count[0:1, 0:1], min_val=0, max_val=EXTRA) + E
            with act.Fori(PEELED, n_blocks) as i:
                expert_step(i)
            copy_y(n_blocks - 2)
            copy_a(n_blocks - 1)
            for q in range(len(UP_SPLIT), len(SPLITS)):
                split_hi(n_blocks, q, after_loop=True)
            copy_y(n_blocks - 1)

            def split_gate(c):
                act.wait_ge(slot_loaded[c], 16 * (IN_CHUNKS // IN_RING + 1))
                nc.scalar.activation(gate_hi[c][:], ring[:, c, :], ACT.Copy).then_inc(gate_hi_ready, 1)

            def copy_pw(j):
                act.wait_ge(pw_done, j + 1)
                b = 2 * (j % 2)
                nc.scalar.activation(pw[:, j, :].rearrange("p (a n) -> p a n", a=2), ps[:, b:b + 2, :], ACT.Copy).then_inc(pw_copied, 1)

            split_gate(0)
            split_gate(1)
            copy_pw(0)
            split_gate(2)
            copy_pw(1)
            split_gate(3)
            copy_pw(2)
            copy_pw(3)

            def square_x2(j):
                act.wait_ge(y_summed, j + 1)
                square_of_tile(2 * NT + X2_NORM[j], j)
                root_of_tile(2 * NT + X2_NORM[j])

            def copy_gate_input(j):
                act.wait_ge(norm_turned, 2 * NT + j + 1)
                b = 4 + 2 * (j % 2)
                nc.scalar.activation(gT[j % 2][0], ps[:, b:b + 2, :].rearrange("p a (k t) -> p (a k) t", k=4),
                                     ACT.Copy).then_inc(gT_hi_ready, 1)

            def sigmoid_gate(j):
                act.wait_ge(ple_done, j + 1)
                if j >= 2:
                    act.wait_ge(ple_added, j - 1)
                b = 2 * (j % 2)
                nc.scalar.activation(sig_t[:, j % 2, :].rearrange("p (a n) -> p a n", a=2), ps[:, b:b + 2, :],
                                     ACT.Sigmoid).then_inc(gate_sig, 1)

            def square_x3(j):
                act.wait_ge(ple_added, j + 1)
                square_of_tile(2 * NT + X3_NORM[j], j)
                root_of_tile(2 * NT + X3_NORM[j])

            square_x2(0)
            copy_gate_input(0)
            square_x2(1)
            copy_gate_input(1)
            square_x2(2)
            sigmoid_gate(0)
            square_x3(0)
            copy_gate_input(2)
            square_x2(3)
            sigmoid_gate(1)
            square_x3(1)
            copy_gate_input(3)
            for j in (2, 3):
                sigmoid_gate(j)
                square_x3(j)

        @block.tensor
        def _(pe):
            mm = nc.tensor.matmul

            def turn_rows(stage, j):
                s = stage * NT + j
                pe.wait_ge(normed, s + 1)
                if s % NT >= 2:
                    pe.wait_ge(norm_copied, s - 1)
                for k in range(KD):
                    last = nc.tensor.transpose(ps[:, 4 + 2 * (j % 2) + k // 4, (k % 4) * P:(k % 4 + 1) * P],
                                               hrow[:, j % 2, k * P:(k + 1) * P], ident[:])
                last.then_inc(norm_turned, 1)

            pe.wait_ge(consts_ready, N_CONSTS)
            for j in range(NT):
                turn_rows(0, j)

            def project(g):
                if g >= 2:
                    if g - 2 < G_Z:
                        pe.wait_ge(conv_done, g - 1)
                    else:
                        pe.wait_ge(proj_copied, g - 1 - G_Z)
                bank = ps[:, g % 2, :]
                by_channel = g < G_Z or G_QK <= g < G_V
                if by_channel:
                    chunks, q = ((g if g < G_Z else g - G_QK + 12) // 2,), g % 2
                else:
                    chunks, j = (Z_CHUNKS, g - G_Z) if g < G_QK else (V_CHUNKS, g - G_V)
                pe.wait_ge(in_lo_ready, chunks[-1] + 1)
                for k in range(KD):
                    if by_channel:
                        hi, lo = [w[chunks[0] % IN_PARTS][:, k * WCOL + q * P:k * WCOL + (q + 1) * P] for w in (in_hi, in_lo)]
                        parts = ((hi, h_hi[:, k, :]), (lo, h_hi[:, k, :]), (hi, h_lo[:, k, :]))
                    else:
                        b, at = chunks[2 * k // KD] % IN_PARTS, (k % (KD // 2)) * BANK
                        hi, lo = h_hi[:, k, j * P:(j + 1) * P], h_lo[:, k, j * P:(j + 1) * P]
                        w_h, w_l = in_hi[b][:, at:at + BANK], in_lo[b][:, at:at + BANK]
                        parts = ((hi, w_h), (lo, w_h), (hi, w_l))
                    for part, (stationary, moving) in enumerate(parts):
                        last = mm(bank, stationary, moving, start=(k == 0 and part == 0), stop=(k == KD - 1 and part == 2))
                last.then_inc(projected, 1)

            pe.wait_ge(norm_copied, NT)
            for g in range(CT):
                project(g)
            pe.wait_ge(wdt_lo_ready, 1)
            for k in range(KD):
                for part, (w, h) in enumerate(((wdt_hi, h_hi), (wdt_lo, h_hi), (wdt_hi, h_lo))):
                    last = mm(ps[0:NH, 2, :], w[:, k, :], h[:, k, :], start=(k == 0 and part == 0), stop=(k == KD - 1 and part == 2))
            last.then_inc(dt_by_head, 1)
            project(G_Z)
            pe.wait_ge(dt_rows_ready, 1)
            for j in range(NT):
                last = nc.tensor.transpose(ps[:, 2, j * NH:(j + 1) * NH], dt_rows[:, j * P:(j + 1) * P], ident[0:NH, 0:NH])
            last.then_inc(dt_projected, 1)
            for g in range(G_Z + 1, G_QK):
                project(g)
            pe.wait_ge(adt_ready, 1)
            adt = dts[:, 6, :]
            mm(ps[:, 3, 0:NT * NH], upper[:], adt, start=True, stop=True)
            mm(ps[:, 3, NT * NH:2 * NT * NH], ones[:], adt, start=True, stop=True).then_inc(cum_ready, 1)

            def ssd_turn(c):
                tok = slice(c * P, (c + 1) * P)
                if c == 0:
                    pe.wait_ge(conv_silu, CT)
                    pe.wait_ge(cum_args, 1)
                else:
                    pe.wait_ge(ssd_read, c)
                    pe.wait_ge(seg_ready, c)
                    pe.wait_ge(state_updated, c)
                for t in range(XT):
                    nc.tensor.transpose(ps[:, 2, t * P:(t + 1) * P], xbcT[:, t, tok], ident[:])
                for q in range(NG):
                    nc.tensor.transpose(ps[:, 3, q * P:(q + 1) * P], xbcT[:, XT + q, tok], ident[:])
                for q in range(NG):
                    mm(ps[:, 3, (NG + q) * P:(NG + q + 1) * P], xbcT[:, XT + q, tok], xbcT[:, XT + NG + q, tok],
                       start=True, stop=True)
                for h in range(NH):
                    last = mm(ps[:, 4 + h // HG, (h % HG) * P:(h % HG + 1) * P],
                              dts[:, 6, c * NH + h:c * NH + h + 1].to_broadcast([P, P]), upper[:], start=True, stop=True)
                last.then_inc(ssd_turned, 1)

            def ssd_sum(c):
                tok = slice(c * P, (c + 1) * P)
                pe.wait_ge(decay_ready, c + 1)
                if c >= 1:
                    pe.wait_ge(y_gated, c)
                for h in range(NH):
                    mm(ps[:, 6, h * HP:(h + 1) * HP], seg[:, h, :], xdt[:, h * HP:(h + 1) * HP], start=True, stop=True)
                if c >= 1:
                    for q in range(NG):
                        mm(ps[:, 7, q * HG * HP:(q + 1) * HG * HP], xbcT[:, XT + NG + q, tok],
                           prevT[:, q * HG * HP:(q + 1) * HG * HP], start=True, stop=True)
                for q in range(NG):
                    last = mm(ps[:, 2, q * HG * HP:(q + 1) * HG * HP], b_tok[:, q * NS:(q + 1) * NS],
                              xdec[:, q * HG * HP:(q + 1) * HG * HP], start=True, stop=True)
                last.then_inc(ssd_summed, 1)

            g = G_QK
            for c in range(NT):
                ssd_turn(c)
                for _ in range(PER_CHUNK - 1):
                    project(g)
                    g += 1
                ssd_sum(c)
                project(g)
                g += 1

            for c in range(NT):
                pe.wait_ge(y_ssd_ready, c + 1)
                if c < 2:
                    pe.wait_ge(y_gated, NT)
                else:
                    pe.wait_ge(mix_copied, c - 1)
                for t in range(XT):
                    last = nc.tensor.transpose(ps[:, 6 + c % 2, t * P:(t + 1) * P], zs[:, c, t * P:(t + 1) * P], ident[:])
                last.then_inc(mix_turned, 1)

            pe.wait_ge(proj_copied, N_GROUPS - G_Z)

            def score(u):
                b, h = u // AH, u % AH
                nk = (b + 1) * P
                for j in range(2):
                    if u >= 2:
                        pe.wait_ge(expd, 2 * (u - 2) + j + 1)
                    half = slice(j * DH, (j + 1) * DH)
                    mm(ps[:, (u % 2) * 2 + j, 0:nk], qkT[half, h, b * P:(b + 1) * P], qkT[half, AH + h, 0:nk],
                       start=True, stop=True).then_inc(scored, 1)

            def turn_w(u):
                b = u // AH
                pe.wait_ge(weighed, u + 1)
                if u >= 2:
                    pe.wait_ge(w_copied, u - 1)
                for k in range(b + 1):
                    last = nc.tensor.transpose(ps[:, 4 + u % 2, k * P:(k + 1) * P], wgt[:, u % 2, k * P:(k + 1) * P], ident[:])
                last.then_inc(w_turned, 1)

            def attend(u):
                b, h = u // AH, u % AH
                pe.wait_ge(w_copied, u + 1)
                if h == 0:
                    if b < 2:
                        pe.wait_ge(mix_copied, NT)
                    else:
                        pe.wait_ge(o_copied, b - 1)
                for k in range(b + 1):
                    last = mm(ps[:, 6 + b % 2, h * VH:(h + 1) * VH], wgtT[:, u % 2, k * P:(k + 1) * P],
                              vt[:, k, h * VH:(h + 1) * VH], start=(k == 0), stop=(k == b))
                last.then_inc(attended, 1)

            def turn_o(b):
                pe.wait_ge(o_ready, b + 1)
                if b >= 2:
                    pe.wait_ge(mix_copied, NT + b - 1)
                for h in range(AH):
                    last = nc.tensor.transpose(ps[:, 6 + b % 2, h * P:(h + 1) * P], orow[:, b, h * VH:(h + 1) * VH], ident[:])
                last.then_inc(mix_turned, 1)

            score(0)
            score(1)
            for u in range(UNITS):
                if u + 2 < UNITS:
                    score(u + 2)
                turn_w(u)
                if u:
                    attend(u - 1)
            attend(UNITS - 1)

            def project_mix(j, ks):
                for c in range(4):
                    w = dense(OUT_SLOT + c)
                    for k in ks:
                        last = mm(ps[:, 2 * (j % 2) + c // 2, (c % 2) * WCOL:(c % 2 + 1) * WCOL],
                                  hT[:, k, j * P:(j + 1) * P], w[:, k, :], start=(k == 0 and c % 2 == 0),
                                  stop=(k == KD - 1), skip_group_check=True)
                return last

            for c in range(4):
                pe.wait_ge(slot_loaded[OUT_SLOT + c], 16)
            pe.wait_ge(expd, 2 * UNITS)
            project_mix(0, range(XT))
            turn_o(0)
            turn_o(1)
            for j in range(NT):
                pe.wait_ge(mix_copied, NT + j + 1)
                if j >= 2:
                    pe.wait_ge(mixed_added, j - 1)
                last = project_mix(j, range(XT if j == 0 else 0, KD))
                last.then_inc(mixed, 1)
                if j == 0:
                    turn_o(2)
                    turn_o(3)
                if j >= 1:
                    turn_rows(1, j - 1)
            def route(j):
                pe.wait_ge(norm_copied, NT + j + 1)
                for k in range(KD):
                    last = mm(ps[0:E, 0, j * P:(j + 1) * P], wrt[:, k, :], xbcT[:, k, j * P:(j + 1) * P],
                              start=(k == 0), stop=(k == KD - 1))
                return last

            pe.wait_ge(mixed_added, NT - 1)
            pe.wait_ge(router_loaded, 16)
            route(0)
            route(1)
            turn_rows(1, NT - 1)
            route(2)
            route(3).then_inc(routed, 1)
            pe.wait_ge(logit_rows_ready, 1)
            for j in range(NT):
                last = nc.tensor.transpose(ps[:, 1, j * E:(j + 1) * E], logit_rows[:, j * P:(j + 1) * P], ident[0:E, 0:E])
            last.then_inc(logits_turned, 1)
            pe.wait_ge(p_loaded, 16)
            pe.wait_ge(mixed_added, NT)
            for j in range(NT):
                for k in range(2):
                    last = nc.tensor.transpose(ps[:, 2 + k, j * P:(j + 1) * P], p_rows[:, j, k * P:(k + 1) * P], ident[:])
            last.then_inc(p_turned, 1)
            pe.wait_ge(chosen_ready, 1)
            by_tile = slice(0, NT * E)
            flat = [a.rearrange("p j e -> p (j e)") for a in (chosen, earlier)]
            mm(ps[:, 0, by_tile], strict[:], flat[0], start=True, stop=False)
            mm(ps[:, 0, by_tile], ones[:], flat[1][:, by_tile], start=False, stop=True)
            last = mm(ps[:, 0, NT * E:(NT + 1) * E], ones[:], earlier[:, NT, :], start=True, stop=True)
            last.then_inc(placed, 1)

            def sum_idx(i):
                pe.wait_ge(hot_ready, i + 1)
                if not is_static(i, 1):
                    pe.wait_ge(out_idx_ready, i)
                if not is_static(i, 2):
                    pe.wait_ge(xT_ready, i)
                for j in range(NT):
                    last = mm(ps[:, 6, 0:1], slot_hot[:, j, :], val_tab[:, j, bass.ds(i, 1)], start=(j == 0), stop=(j == NT - 1))
                last.then_inc(idx_summed, 1)

            def turn_rows_of(rows, done):
                for k in range(KD):
                    last = nc.tensor.transpose(ps[:, 6 + k // 4, (k % 4) * B:(k % 4 + 1) * B], rows[:, k * P:(k + 1) * P], ident[:])
                last.then_inc(done, 1)

            def turn_x(i):
                pe.wait_ge(gathered, 16 * (i + 1))
                pe.wait_ge(out_idx_ready, 2 if is_static(i, 1) else i + 1)
                if not is_static(i, 2):
                    pe.wait_ge(aT_ready, i - 1)
                turn_rows_of(xg, x_turned)

            def turn_a(i):
                pe.wait_ge(act_ready, i + 1)
                pe.wait_ge(xT_ready, i + 2)
                pe.wait_ge(out_idx_ready, i + 3)
                turn_rows_of(up_s, a_turned)

            def products(banks, hi, lo, w, b, stop):
                for part, (x_part, w_part) in enumerate(((hi, w_hi[b]), (lo, w_hi[b]), (hi, w_lo[b]))):
                    for a, bank in enumerate(banks):
                        last = mm(ps[:, bank, :], x_part, w_part[:, w + a * BANK:w + (a + 1) * BANK],
                                  start=False, stop=(stop and part == 2))
                return last

            def up_chunk(i, k):
                if k == 0:
                    pe.wait_ge(xT_ready, i + 1)
                    pe.wait_ge(up_hot_ready, i + 1)
                    if is_static(i, 1):
                        pe.wait_ge(bias_ready, 1)
                        pe.wait_ge(p_copied, 1)
                    else:
                        pe.wait_ge(gate_clamped, i)
                        pe.wait_ge(up_clamped, i)
                    for a in range(4):
                        mm(ps[:, a, :], up_hot[:], bias_tab[0:2 * E, a * BANK:(a + 1) * BANK], start=True, stop=False)
                if k in UP_WHOLE:
                    pe.wait_ge(up_loaded[k], 16 * (i + 1))
                    for a in range(4):
                        last = mm(ps[:, a, :], x_whole[:, UP_WHOLE.index(k), :], ring[:, k % RING, a * BANK:(a + 1) * BANK],
                                  start=False, stop=(k == KD - 1))
                else:
                    q = UP_SPLIT.index(k)
                    pe.wait_ge(up_lo, i * len(UP_SPLIT) + q + 1)
                    last = products(range(4), xT_hi[:, k, :], xT_lo[:, k, :], 0, q % PARTS, k == KD - 1)
                last.then_inc(up_used, 1)

            def down(i):
                pe.wait_ge(aT_ready, i + 1)
                pe.wait_ge(down_hot_ready, i + 1)
                if not is_static(i, 1):
                    pe.wait_ge(y_ready, i)
                for a in range(2):
                    mm(ps[:, 4 + a, :], down_hot[:], bias_tab[0:2 * E, 2 * D + a * BANK:2 * D + (a + 1) * BANK], start=True, stop=False)
                for c in range(DOWN_CHUNKS):
                    if c in DOWN_WHOLE:
                        pe.wait_ge(down_loaded[c], 16 * (i + 1))
                    else:
                        q = DOWN_SPLIT.index(c)
                        pe.wait_ge(down_lo, i * len(DOWN_SPLIT) + q + 1)
                    for f in range(2):
                        if c in DOWN_WHOLE:
                            for a in range(2):
                                last = mm(ps[:, 4 + a, :], a_whole[:, 2 * DOWN_WHOLE.index(c) + f, :],
                                          ring[:, 2 + c, f * D + a * BANK:f * D + (a + 1) * BANK], start=False, stop=False)
                        else:
                            last = products((4, 5), aT_hi[:, 2 * c + f, :], aT_lo[:, 2 * c + f, :], f * D, q,
                                            c == DOWN_CHUNKS - 1 and f == 1)
                    last.then_inc(down_used, 1)

            def expert_step(i):
                for k in range(KD // 2):
                    up_chunk(i, k)
                if not is_static(i, 1):
                    turn_a(i - 1)
                for k in range(KD // 2, KD):
                    up_chunk(i, k)
                turn_x(i + 1)
                if not is_static(i, 1):
                    down(i - 1)
                sum_idx(i + 2)

            sum_idx(0)
            sum_idx(1)
            turn_x(0)
            for i in range(PEELED):
                expert_step(i)
            pe.wait_ge(tables_ready, 1)
            n_blocks = pe.value_load(extra_count[0:1, 0:1], min_val=0, max_val=EXTRA) + E
            with pe.Fori(PEELED, n_blocks) as i:
                expert_step(i)
            turn_a(n_blocks - 1)
            down(n_blocks - 1)

            def project_p(j):
                if j >= 2:
                    pe.wait_ge(pw_copied, j - 1)
                for h in range(2):
                    for k in range(2):
                        last = mm(ps[:, 2 * (j % 2) + h, :], pT[:, k, j * P:(j + 1) * P], w_proj_s[:, k, h * BANK:(h + 1) * BANK],
                                  start=(k == 0), stop=(k == 1))
                last.then_inc(pw_done, 1)

            def project_gate(j, chunks):
                if chunks[0] == 0:
                    pe.wait_ge(norm_copied, 2 * NT + j + 1)
                    if j >= 2:
                        pe.wait_ge(gate_sig, j - 1)
                    else:
                        pe.wait_ge(pw_copied, NT)
                hi, lo = gT[j % 2]
                for c in chunks:
                    if j == 0:
                        pe.wait_ge(gate_lo_ready, c + 1)
                    for f in range(2):
                        k = 2 * c + f
                        for part, (x_part, w_part) in enumerate(((hi, gate_hi[c]), (lo, gate_hi[c]), (hi, gate_lo[c]))):
                            for h in range(2):
                                last = mm(ps[:, 2 * (j % 2) + h, :], x_part[:, k, :], w_part[:, f * D + h * BANK:f * D + (h + 1) * BANK],
                                          start=(k == 0 and part == 0), stop=(k == KD - 1 and part == 2))
                return last

            pe.wait_ge(tail_loaded, 32)
            pe.wait_ge(p_copied, 1)
            for j in range(NT):
                project_p(j)
            turn_rows(2, 0)
            for j in range(NT):
                project_gate(j, (0, 1))
                if j + 1 < NT:
                    turn_rows(2, j + 1)
                project_gate(j, (2, 3)).then_inc(ple_done, 1)

        @block.vector
        def _(dve):
            v = nc.vector
            steps = 0

            def link(ins):
                nonlocal steps
                steps += 1
                ins.then_inc(dve_step, 1)
                dve.wait_ge(dve_step, steps)

            def heads(table):
                return table.unsqueeze(2).to_broadcast([P, NH, HP])

            def by_head(a):
                return a.rearrange("p (h e) -> p h e", h=NH)

            def rms(col, n, eps):
                dve.wait_ge(squared, col + 1)
                v.tensor_scalar(ssq[:, col:col + 1], ssq[:, col:col + 1], 1.0 / n, eps, ALU.mult, ALU.add).then_inc(scaled, 1)
                dve.wait_ge(rooted, col + 1)
                link(v.reciprocal(rstd[:, col:col + 1], rstd[:, col:col + 1]))

            def norm_rows(stage, j, col=None):
                s = stage * NT + j
                col = s if col is None else col
                rms(col, D, NORM_EPS)
                if j >= 2:
                    dve.wait_ge(norm_turned, s - 1)
                if stage == 1 and j >= 2:
                    dve.wait_ge(hn_stored[j - 2], 16)
                v.scalar_tensor_tensor(hrow[:, j % 2, :], xres[:, j, :], rstd[:, col:col + 1], (gmix, gffn, gple)[stage],
                                       ALU.mult, ALU.mult).then_inc(normed, 1)

            def split_h(j):
                dve.wait_ge(h_hi_ready, j + 1)
                b = 4 + 2 * (j % 2)
                v.tensor_tensor(h_lo[:, :, j * P:(j + 1) * P], ps[:, b:b + 2, :].rearrange("p a (k t) -> p (a k) t", k=4),
                                h_hi[:, :, j * P:(j + 1) * P], ALU.subtract).then_inc(norm_copied, 1)

            def split_in(m):
                dve.wait_ge(in_hi_ready, m + 1)
                v.tensor_tensor(in_lo[m % IN_PARTS][:], ring[:, m % IN_RING, :], in_hi[m % IN_PARTS][:], ALU.subtract).then_inc(in_lo_ready, 1)

            def norm_copy(j):
                dve.wait_ge(norm_turned, NT + j + 1)
                b = 4 + 2 * (j % 2)
                v.tensor_copy(xbcT[:, :, j * P:(j + 1) * P],
                              ps[:, b:b + 2, :].rearrange("p a (k t) -> p (a k) t", k=4)).then_inc(norm_copied, 1)

            dve.wait_ge(gain_loaded, 16)
            norm_rows(0, 0)
            norm_rows(0, 1)
            for j in range(2):
                split_h(j)
                norm_rows(0, j + 2)
            split_in(0)
            split_h(2)
            split_h(3)
            split_in(1)
            split_in(2)

            dve.wait_ge(wdt_hi_ready, 1)
            v.tensor_tensor(wdt_lo[:], wdt[:], wdt_hi[:], ALU.subtract).then_inc(wdt_lo_ready, 1)
            for t in range(CT):
                dve.wait_ge(projected, t + 1)
                u = ps[:, t % 2, :]
                link(v.tensor_scalar(xbcT[:, t, :], u, convw_t[:, CONV - 1, t:t + 1], convb_t[:, t:t + 1], ALU.mult, ALU.add))
                for k in range(CONV - 1):
                    back = CONV - 1 - k
                    ins = v.scalar_tensor_tensor(xbcT[:, t, back:T], u[:, 0:T - back], convw_t[:, k, t:t + 1],
                                                 xbcT[:, t, back:T], ALU.mult, ALU.add)
                    if k < CONV - 2:
                        link(ins)
                ins.then_inc(conv_done, 1)
                if t % 2:
                    split_in(IN_PARTS + t // 2)

            NHT = NT * NH
            d = [dts[:, i, :] for i in range(12)]
            dve.wait_ge(dt_by_head, 1)
            v.tensor_copy(dt_rows, ps[0:NH, 2, :]).then_inc(dt_rows_ready, 1)
            dve.wait_ge(dt_projected, 1)
            link(v.tensor_tensor(d[0].rearrange("p (j h) -> p j h", h=NH),
                                 ps[:, 2, 0:NHT].rearrange("p (j h) -> p j h", h=NH),
                                 dtb[:].unsqueeze(1).to_broadcast([P, NT, NH]), ALU.add))
            link(v.tensor_scalar(d[2], d[0], -1.0, None, ALU.mult))
            v.tensor_tensor(d[1], d[0], d[2], ALU.min).then_inc(dt_pre, 1)
            dve.wait_ge(dt_e, 1)
            v.tensor_scalar(d[3], d[2], 1.0, None, ALU.add).then_inc(dt_u, 1)
            dve.wait_ge(dt_u, 1)
            link(v.tensor_scalar(d[5], d[3], -1.0, None, ALU.add))
            link(v.tensor_scalar(d[7], d[5], 0.0, None, ALU.is_equal))
            link(v.tensor_tensor(d[5], d[5], d[7], ALU.add))
            link(v.reciprocal(d[5], d[5]))
            link(v.tensor_tensor(d[5], d[5], d[2], ALU.mult))
            dve.wait_ge(dt_l, 1)
            link(v.tensor_tensor(d[4], d[4], d[7], ALU.add))
            link(v.tensor_tensor(d[4], d[4], d[5], ALU.mult))
            link(v.tensor_scalar(d[0], d[0], 0.0, None, ALU.max))
            link(v.tensor_tensor(d[0], d[0], d[4], ALU.add))
            link(v.tensor_scalar(alog[:], alog[:], -1.0, None, ALU.mult))
            v.tensor_tensor(d[6].rearrange("p (j h) -> p j h", h=NH), d[0].rearrange("p (j h) -> p j h", h=NH),
                            alog[:].unsqueeze(1).to_broadcast([P, NT, NH]), ALU.mult).then_inc(adt_ready, 1)
            dve.wait_ge(late_params_loaded, 16 * N_LATE_PARAMS)
            for i in range(2):
                ins = v.tensor_tensor_reduce(out=lam_prod[:, i, :], in0=lamv[:, 2 * i, :], in1=lamv[:, 2 * i + 1, :],
                                             scale=1.0, scalar=0.0, op0=ALU.mult, op1=ALU.add,
                                             accum_out=lam_s[:, i:i + 1])
                if i == 0:
                    link(ins)
            ins.then_inc(lam_dots, 1)
            dve.wait_ge(lam_exps, 1)
            link(v.tensor_tensor(lam_s[:, 0:1], lam_s[:, 2:3], lam_s[:, 3:4], ALU.subtract))
            link(v.tensor_scalar(lam_s[:, 0:1], lam_s[:, 0:1], LAM_INIT, None, ALU.add))
            link(v.tensor_scalar(subln[:], subln[:], 1.0 - LAM_INIT, None, ALU.mult))

            dve.wait_ge(cum_ready, 1)
            link(v.tensor_copy(dts[:, 8, :], ps[:, 3, 0:NHT]))
            link(v.tensor_copy(dts[:, 10, :], ps[:, 3, NHT:2 * NHT]))
            link(v.tensor_scalar(dts[:, 11, :], d[8], -1.0, None, ALU.mult))
            v.tensor_tensor(dts[:, 9, :], d[10], d[8], ALU.subtract).then_inc(cum_args, 1)
            dve.wait_ge(cum_exp, 1)
            split_in(7)
            split_in(8)

            def hcol(i, c):
                return dts[:, i, c * NH:(c + 1) * NH]

            half = SSD_W // NG
            for c in range(NT):
                dve.wait_ge(ssd_turned, c + 1)
                link(v.tensor_copy(xs_tok, ps[:, 2, :]))
                link(v.tensor_copy(b_tok, ps[:, 3, 0:NG * NS]))
                v.tensor_tensor(cb_mask, ps[:, 3, NG * NS:].rearrange("p (q l) -> p q l", q=NG),
                                upper[:].unsqueeze(1).to_broadcast([P, NG, P]), ALU.mult).then_inc(ssd_read, 1)
                dve.wait_ge(ssd_read, c + 1)
                for h in range(NH):
                    ins = v.tensor_scalar(seg[:, h, :], ps[:, 4 + h // HG, (h % HG) * P:(h % HG + 1) * P],
                                          dts[:, 11, c * NH + h:c * NH + h + 1], 0.0, ALU.add, ALU.min)
                    if h < NH - 1:
                        link(ins)
                ins.then_inc(seg_ready, 1)
                link(v.tensor_tensor(by_head(xdt), by_head(xs_tok), heads(hcol(0, c)), ALU.mult))
                link(v.tensor_tensor(by_head(xdec), by_head(xdt), heads(hcol(9, c)), ALU.mult))
                link(v.tensor_tensor(by_head(xs_tok), by_head(xs_tok), heads(dskip[:]), ALU.mult))
                dve.wait_ge(seg_exp, c + 1)
                for q in range(NG):
                    ins = v.tensor_tensor(seg[:, q * HG:(q + 1) * HG, :], seg[:, q * HG:(q + 1) * HG, :],
                                          cb_mask[:, q:q + 1, :].to_broadcast([P, HG, P]), ALU.mult)
                    if q < NG - 1:
                        link(ins)
                ins.then_inc(decay_ready, 1)
                dve.wait_ge(ssd_summed, c + 1)
                dve.wait_ge(proj_copied, NT)
                if c >= 1:
                    link(v.tensor_tensor(by_head(yrow), by_head(ps[:, 7, :]), heads(hcol(8, c)), ALU.mult))
                    link(v.tensor_tensor(yrow, yrow, xs_tok, ALU.add))
                    link(v.tensor_tensor(yrow, ps[:, 6, :], yrow, ALU.add))
                else:
                    link(v.tensor_tensor(yrow, ps[:, 6, :], xs_tok, ALU.add))
                v.tensor_tensor(yrow, yrow, zs[:, c, :], ALU.mult).then_inc(y_gated, 1)
                if c == 0:
                    v.tensor_copy(prevT, ps[:, 2, :]).then_inc(state_updated, 1)
                else:
                    link(v.tensor_tensor(by_head(prevT), by_head(prevT), heads(hcol(10, c)), ALU.mult))
                    v.tensor_tensor(prevT, ps[:, 2, :], prevT, ALU.add).then_inc(state_updated, 1)
                dve.wait_ge(state_updated, c + 1)
                dve.wait_ge(y_squared, NG * (c + 1))
                v.tensor_scalar(ssq[:, 16:16 + NG], ssq[:, 16:16 + NG], 1.0 / half, SSD_NORM_EPS, ALU.mult, ALU.add).then_inc(y_mean, 1)
                dve.wait_ge(y_root, c + 1)
                link(v.reciprocal(att_s[:, 0, 0:NG], rstd[:, 16:16 + NG]))
                for q in range(NG):
                    cols = slice(q * half, (q + 1) * half)
                    ins = v.scalar_tensor_tensor(zs[:, c, cols], yrow[:, cols], att_s[:, 0, q:q + 1], normw[:, cols],
                                                 ALU.mult, ALU.mult)
                    if q < NG - 1:
                        link(ins)
                ins.then_inc(y_ssd_ready, 1)
                if c == 0:
                    split_in(9)
                elif c == 1:
                    split_in(10)
                    split_in(11)
                dve.wait_ge(y_ssd_ready, c + 1)

            def max_unit(u):
                b = u // AH
                nk = (b + 1) * P
                for j in range(2):
                    dve.wait_ge(scored, 2 * u + j + 1)
                    s = ps[:, (u % 2) * 2 + j, :]
                    link(v.tensor_tensor(s[:, b * P:nk], s[:, b * P:nk], attmask[:], ALU.add))
                    v.tensor_reduce(out=att_s[:, u % 2, j:j + 1], in_=s[:, 0:nk], axis=AX, op=ALU.max,
                                    negate=True).then_inc(maxed, 1)

            def weigh(u):
                nk = (u // AH + 1) * P
                a = att_s[:, u % 2, :]
                dve.wait_ge(expd, 2 * u + 2)
                link(v.reciprocal(a[:, 4:6], a[:, 2:4]))
                link(v.tensor_tensor(a[:, 5:6], a[:, 5:6], lam_s[:, 0:1], ALU.mult))
                if u >= 2:
                    dve.wait_ge(w_turned, u - 1)
                link(v.tensor_scalar(wgt[:, u % 2, 0:nk], probs[:, u % 2, 1, 0:nk], a[:, 5:6], None, ALU.mult))
                v.scalar_tensor_tensor(wgt[:, u % 2, 0:nk], probs[:, u % 2, 0, 0:nk], a[:, 4:5], wgt[:, u % 2, 0:nk],
                                       ALU.mult, ALU.subtract).then_inc(weighed, 1)

            def keep_o(b):
                dve.wait_ge(attended, AH * (b + 1))
                v.tensor_copy(orow[:, b, :], ps[:, 6 + b % 2, :]).then_inc(o_copied, 1)

            def norm_o(b):
                for h in range(AH):
                    cols = slice(h * VH, (h + 1) * VH)
                    ins = v.scalar_tensor_tensor(orow[:, b, cols], orow[:, b, cols], o_inv[:, b * AH + h:b * AH + h + 1],
                                                 subln[:], ALU.mult, ALU.mult)
                    if h < AH - 1:
                        link(ins)
                ins.then_inc(o_ready, 1)

            max_unit(0)
            for u in range(UNITS):
                if u + 1 < UNITS:
                    max_unit(u + 1)
                weigh(u)
                if u % AH == 0 and u:
                    keep_o(u // AH - 1)
            keep_o(NT - 1)
            dve.wait_ge(o_squared, UNITS)
            v.tensor_scalar(o_sum[:], o_sum[:], 1.0 / VH, SUBLN_EPS, ALU.mult, ALU.add).then_inc(o_mean, 1)
            dve.wait_ge(o_root, 1)
            link(v.reciprocal(o_inv[:], o_sum[:]))
            for b in range(NT):
                norm_o(b)

            def hot(i):
                if not isinstance(i, int) or i >= 1:
                    dve.wait_ge(idx_summed, i)
                for j in range(NT):
                    ins = v.tensor_scalar(slot_hot[:, j, :], iota[:, 0:B], pos_tab[:, j, bass.ds(i, 1)], None, ALU.is_equal)
                ins.then_inc(hot_ready, 1)

            def indices(i):
                dve.wait_ge(idx_summed, i + 1)
                v.tensor_scalar(out_idx[0:B, bass.ds(i, 1)], ps[0:B, 6, 0:1],
                                float(EMPTY), None, ALU.add).then_inc(out_idx_ready, 1)
                dve.wait_ge(out_idx_ready, i + 1)
                if not isinstance(i, int) or i >= 1:
                    dve.wait_ge(gathered, 16 * i)
                v.tensor_scalar(gather_idx[0:B, :], out_idx[0:B, bass.ds(i, 1)], 2, None,
                                ALU.arith_shift_right).then_inc(gather_idx_ready, 1)

            turned = ps[:, 6:8, :].rearrange("p a (k n) -> p (a k) n", n=B)

            def copy_x(i):
                dve.wait_ge(xT_hi_ready, 2 * (i + 1))
                v.tensor_tensor(xT_lo, turned, xT_hi, ALU.subtract).then_inc(xT_ready, 1)

            def copy_a(i):
                dve.wait_ge(aT_hi_ready, 2 * (i + 1))
                v.tensor_tensor(aT_lo, turned, aT_hi, ALU.subtract).then_inc(aT_ready, 1)

            def split_lo(i, q):
                chunk, b = SPLITS[q], q % PARTS
                if q < len(UP_SPLIT):
                    dve.wait_ge(up_hi, i * len(UP_SPLIT) + q + 1)
                    v.tensor_tensor(w_lo[b][:], ring[:, chunk % RING, :], w_hi[b][:], ALU.subtract).then_inc(up_lo, 1)
                else:
                    q -= len(UP_SPLIT)
                    dve.wait_ge(down_hi, (i - 1) * len(DOWN_SPLIT) + q + 1)
                    v.tensor_tensor(w_lo[b][:], ring[:, 2 + chunk, :], w_hi[b][:], ALU.subtract).then_inc(down_lo, 1)

            def mark_expert(i, dst, done):
                expert = float(i) if isinstance(i, int) else block_expert_f[0:2 * E, bass.ds(i, 1)]
                v.tensor_scalar(dst[:], expert_of[0:2 * E, :].to_broadcast([2 * E, B]), expert, None, ALU.is_equal).then_inc(done, 1)

            def up_expert(i):
                if not is_static(i, 1):
                    dve.wait_ge(up_used, (i - 1) * UP_CHUNKS + 1)
                mark_expert(i, up_hot, up_hot_ready)

            def down_expert(i):
                if not is_static(i, 1):
                    dve.wait_ge(down_used, (i - 1) * DOWN_CHUNKS + 1)
                mark_expert(i, down_hot, down_hot_ready)

            def clamp(i):
                dve.wait_ge(up_used, UP_CHUNKS * (i + 1))
                four = [g_or_u.rearrange("p (a n) -> p a n", a=4) for g_or_u in (gate_s, up_s)]
                v.tensor_scalar(four[0], ps[:, 0:4, 0:BANK:2], SWIGLU_LIMIT, None, ALU.min).then_inc(gate_clamped, 1)
                v.tensor_scalar(four[1], ps[:, 0:4, 1:BANK:2], -SWIGLU_LIMIT, SWIGLU_LIMIT, ALU.max, ALU.min).then_inc(up_clamped, 1)

            def activate(i):
                dve.wait_ge(gate_clamped, i + 1)
                dve.wait_ge(up_clamped, i + 1)
                v.scalar_tensor_tensor(up_s, up_s, 1.0, gate_s, ALU.add, ALU.mult).then_inc(swish, 1)
                dve.wait_ge(swish, i + 1)
                dve.wait_ge(sigmoided, i + 1)
                v.tensor_tensor(up_s, up_s, sig_s, ALU.mult).then_inc(act_ready, 1)

            def place_scatter(i):
                if not is_static(i, 1):
                    dve.wait_ge(scattered, 16 * i)
                v.tensor_copy(scatter_idx[:], out_idx[:, bass.ds(i, 1)]).then_inc(scatter_idx_ready, 1)

            wide = [P, EXTRA, E]

            def make_gates():
                dve.wait_ge(top_exp, 1)
                link(v.tensor_reduce(out=small[:, 0:NT], in_=gates[:], axis=AX, op=ALU.add))
                link(v.reciprocal(small[:, 0:NT], small[:, 0:NT]))
                link(v.tensor_tensor(gates[:], gates[:], small[:, 0:NT].unsqueeze(2).to_broadcast([P, NT, TOPK]), ALU.mult))

            def count_extra():
                link(v.tensor_scalar(extra, counts, float(B), None, ALU.is_gt))
                for m in range(2, -(-T // B)):
                    link(v.tensor_scalar(cum, counts, float(m * B), None, ALU.is_gt))
                    link(v.tensor_tensor(extra, extra, cum, ALU.add))
                link(v.tensor_copy(cum, extra))
                for s in (1, 2, 4, 8, 16):
                    link(v.tensor_copy(counts, cum))
                    link(v.tensor_tensor(cum[:, s:E], counts[:, s:E], counts[:, 0:E - s], ALU.add))
                link(v.tensor_tensor(sel, cum.unsqueeze(1).to_broadcast(wide), iota[:, 0:EXTRA].unsqueeze(2).to_broadcast(wide), ALU.is_le))
                link(v.tensor_reduce(out=blk_e, in_=sel, axis=AX, op=ALU.add))
                link(v.tensor_tensor(sel, sel, extra.unsqueeze(1).to_broadcast(wide), ALU.mult))
                link(v.tensor_reduce(out=blk_b, in_=sel, axis=AX, op=ALU.add))
                link(v.tensor_tensor(blk_b, iota[:, 0:EXTRA], blk_b, ALU.subtract))
                link(v.tensor_scalar(blk_b, blk_b, 1.0, float(B), ALU.add, ALU.mult))
                link(v.tensor_tensor(sel, iota[:, 0:E].unsqueeze(1).to_broadcast(wide), blk_e.unsqueeze(2).to_broadcast(wide), ALU.is_equal))

            def extra_tables(j):
                for src, dst in ((pos_tab, pos_tab), (val_tab, val_tab)):
                    link(v.tensor_tensor(sel2, sel, src[:, j, 0:E].unsqueeze(1).to_broadcast(wide), ALU.mult))
                    link(v.tensor_reduce(out=dst[:, j, E:NB], in_=sel2, axis=AX, op=ALU.add))
                link(v.tensor_tensor(pos_tab[:, j, E:NB], pos_tab[:, j, E:NB], blk_b, ALU.subtract))

            def finish_tables():
                link(v.memset(pos_tab[:, :, NB:NCOL], -1.0))
                link(v.memset(val_tab[:, :, NB:NCOL], 0.0))
                link(v.tensor_copy(block_expert[:, 0:E], iota[:, 0:E]))
                link(v.tensor_scalar(blk_e, blk_e, float(E - 1), None, ALU.min))
                link(v.tensor_copy(block_expert[:, E:NB], blk_e))
                link(v.tensor_copy(block_expert_f[:, 0:E], iota[:, 0:E]))
                link(v.tensor_copy(block_expert_f[:, E:NB], blk_e))
                link(v.memset(block_expert_f[:, NB:NCOL], 0.0))
                v.tensor_copy(extra_count[:], cum[:, E - 1:E]).then_inc(tables_ready, 1)
                dve.wait_ge(tables_ready, 1)

            def expert_step(i):
                if not is_static(i, 1):
                    for q in range(PARTS):
                        split_lo(i, q)
                    indices(i + 1)
                hot(i + 2)
                if not is_static(i, 2):
                    place_scatter(i - 2)
                if not is_static(i, 1):
                    down_expert(i - 1)
                if is_static(i, 1):
                    make_gates()
                    count_extra()
                for q in range(PARTS, len(UP_SPLIT)):
                    split_lo(i, q)
                if is_static(i, 1):
                    extra_tables(0)
                    extra_tables(1)
                elif is_static(i, 2):
                    extra_tables(2)
                    extra_tables(3)
                    finish_tables()
                if not is_static(i, 1):
                    copy_a(i - 1)
                    for q in range(len(UP_SPLIT), len(SPLITS)):
                        split_lo(i, q)
                clamp(i)
                copy_x(i + 1)
                up_expert(i + 1)
                activate(i)

            link(v.tensor_scalar(expert_tmp[:], expert_of[:], float(E), -float(E), ALU.is_ge, ALU.mult))
            link(v.tensor_tensor(expert_of[:], expert_of[:], expert_tmp[:], ALU.add))
            up_expert(0)
            split_lo(0, 0)
            dve.wait_ge(mix_turned, NT)
            link(v.memset(xg[:, KD * E:], 0.0))

            dve.wait_ge(gain_loaded, 32)
            for j in range(NT):
                dve.wait_ge(mixed, j + 1)
                xj = xres[:, j, :].rearrange("p (a n) -> p a n", a=2)
                v.tensor_tensor(xj, ps[:, 2 * (j % 2):2 * (j % 2) + 2, :], xj, ALU.add).then_inc(mixed_added, 1)
                norm_rows(1, j)
                if j >= 1:
                    norm_copy(j - 1)
            norm_copy(NT - 1)

            dve.wait_ge(routed, 1)
            v.tensor_copy(logit_rows, ps[0:E, 0, :]).then_inc(logit_rows_ready, 1)
            link(v.memset(xg[:, 0:KD * E], 0.0))
            link(v.memset(earlier[:, 0, :], 0.0))
            dve.wait_ge(logits_turned, 1)
            v.tensor_tensor(logits, ps[:, 1, 0:NT * E].rearrange("p (j e) -> p j e", e=E),
                            brt[:].unsqueeze(1).to_broadcast([P, NT, E]), ALU.add).then_inc(logits_read, 1)
            dve.wait_ge(logits_read, 1)
            for j in range(NT):
                link(v.max(top8[:, j, :], logits[:, j, :]))
            for j in range(NT):
                link(v.max_index(topi_u[:, j, :], top8[:, j, :], logits[:, j, :]))
            v.tensor_tensor(gates[:], top8[:, :, 0:TOPK], top8[:, :, 0:1].to_broadcast([P, NT, TOPK]),
                            ALU.subtract).then_inc(top_shifted, 1)
            link(v.tensor_copy(topi, topi_u))
            for r in range(TOPK):
                dst = chosen if r == 0 else onehot
                link(v.tensor_tensor(dst, iota[:, 0:E].unsqueeze(1).to_broadcast([P, NT, E]),
                                     topi[:, :, r:r + 1].to_broadcast([P, NT, E]), ALU.is_equal))
                if r == 1:
                    link(v.tensor_scalar(rankv, onehot, float(r), None, ALU.mult))
                elif r > 1:
                    link(v.scalar_tensor_tensor(rankv, onehot, float(r), rankv, ALU.mult, ALU.add))
                if r:
                    ins = v.tensor_tensor(chosen, chosen, onehot, ALU.add)
                    link(ins)
            for j in range(NT):
                ins = v.tensor_tensor(earlier[:, j + 1, :], earlier[:, j, :], chosen[:, j, :], ALU.add)
                if j < NT - 1:
                    link(ins)
            ins.then_inc(chosen_ready, 1)
            link(v.tensor_tensor(rankv, rankv, token4[:].unsqueeze(2).to_broadcast([P, NT, E]), ALU.add))
            link(v.tensor_scalar(val_tab[:, :, 0:E], rankv, -float(EMPTY), None, ALU.add))
            dve.wait_ge(placed, 1)
            link(v.tensor_copy(counts, ps[:, 0, NT * E:(NT + 1) * E]))
            link(v.tensor_copy(onehot, ps[:, 0, 0:NT * E].rearrange("p (j e) -> p j e", e=E)))
            link(v.tensor_scalar(onehot, onehot, 1.0, None, ALU.add))
            link(v.tensor_tensor(onehot, onehot, chosen, ALU.mult))
            link(v.tensor_scalar(pos_tab[:, :, 0:E], onehot, -1.0, None, ALU.add))

            dve.wait_ge(norm_turned, 2 * NT)
            for j in range(NT):
                dve.wait_ge(hn_stored[j], 16)
            hot(0)
            indices(0)
            hot(1)
            dve.wait_ge(bias_hi, 1)
            v.tensor_tensor(bias_tab[E:2 * E, :], bias_rows[E:2 * E, :], bias_tab[E:2 * E, :], ALU.subtract).then_inc(bias_ready, 1)
            indices(1)
            split_lo(0, 1)

            copy_x(0)
            split_lo(0, 2)
            for i in range(PEELED):
                expert_step(i)
            n_blocks = dve.value_load(extra_count[0:1, 0:1], min_val=0, max_val=EXTRA) + E
            with dve.Fori(PEELED, n_blocks) as i:
                expert_step(i)
            indices(n_blocks + 1)
            place_scatter(n_blocks - 2)
            down_expert(n_blocks - 1)
            copy_a(n_blocks - 1)
            for q in range(len(UP_SPLIT), len(SPLITS)):
                split_lo(n_blocks, q)
            place_scatter(n_blocks - 1)
            dve.wait_ge(gathered, 16 * (n_blocks + 1))
            def split_gate(c):
                dve.wait_ge(gate_hi_ready, c + 1)
                v.tensor_tensor(gate_lo[c][:], ring[:, c, :], gate_hi[c][:], ALU.subtract).then_inc(gate_lo_ready, 1)

            for c in range(3):
                split_gate(c)
            dve.wait_ge(gain_loaded, 48)

            def sum_experts(j):
                b = j % Y_BUFS
                dve.wait_ge(y_loaded[b], 16 * (j // Y_BUFS + 1))
                ys = ring[:, 4 + 2 * b:6 + 2 * b, :].rearrange("p a (r d) -> p (a r) d", d=D)
                for r in range(TOPK):
                    ins = v.scalar_tensor_tensor(xres[:, j, :], ys[:, r, :], gates[:, j, r:r + 1], xres[:, j, :], ALU.mult, ALU.add)
                    if r < TOPK - 1:
                        link(ins)
                ins.then_inc(y_summed, 1)

            def norm_x2(j):
                norm_rows(2, j, 2 * NT + X2_NORM[j])

            def copy_gate_input(j):
                dve.wait_ge(gT_hi_ready, j + 1)
                b = 4 + 2 * (j % 2)
                v.tensor_tensor(gT[j % 2][1], ps[:, b:b + 2, :].rearrange("p a (k t) -> p (a k) t", k=4), gT[j % 2][0],
                                ALU.subtract).then_inc(norm_copied, 1)

            def add_ple(j):
                dve.wait_ge(gate_sig, j + 1)
                link(v.tensor_tensor(sig_t[:, j % 2, :], pw[:, j, :], sig_t[:, j % 2, :], ALU.mult))
                v.tensor_tensor(xres[:, j, :], xres[:, j, :], sig_t[:, j % 2, :], ALU.add).then_inc(ple_added, 1)

            def norm_x3(j):
                s = 2 * NT + X3_NORM[j]
                rms(s, D, NORM_EPS)
                if j >= 2:
                    dve.wait_ge(out_stored[j - 2], 16)
                v.scalar_tensor_tensor(out_row[:, j % 2, :], xres[:, j, :], rstd[:, s:s + 1], gfin, ALU.mult, ALU.mult).then_inc(out_ready, 1)

            sum_experts(0)
            norm_x2(0)
            split_gate(3)
            sum_experts(1)
            copy_gate_input(0)
            norm_x2(1)
            sum_experts(2)
            copy_gate_input(1)
            norm_x2(2)
            add_ple(0)
            sum_experts(3)
            norm_x3(0)
            copy_gate_input(2)
            norm_x2(3)
            add_ple(1)
            norm_x3(1)
            copy_gate_input(3)
            for j in (2, 3):
                add_ple(j)
                norm_x3(j)


_INS = ['x', 'p', 'g_mix', 'w_in', 'conv_w', 'conv_b', 'dt_bias', 'a_log', 'd_skip', 'ssd_norm_w',
        'lam_q1', 'lam_k1', 'lam_q2', 'lam_k2', 'subln_w', 'w_out', 'g_ffn', 'w_router', 'b_router',
        'w_up', 'b_up', 'w_down', 'b_down', 'g_ple', 'w_ple_gate', 'w_ple_proj', 'g_final']


def kernel(**inputs):
    import numpy as _np
    import concourse.bacc as _bacc
    from concourse import mybir as _mybir
    from concourse.bass_utils import run_bass_kernel_spmd as _run

    nc = _bacc.Bacc("TRN2", target_bir_lowering=False, num_devices=1)
    arrays, args = {}, []
    for name in _INS:
        a = _np.ascontiguousarray(inputs[name])
        arrays[f"in_{name}_dram"] = a
        args.append(nc.dram_tensor(f"in_{name}_dram", a.shape, _mybir.dt.from_np(a.dtype), kind="ExternalInput").ap())
    shape = tuple(inputs["x"].shape)
    args.append(nc.dram_tensor("out_0_dram", shape, _mybir.dt.float32, kind="ExternalOutput").ap())
    hybrid_ssd_diffattn_moe_ple_kernel(nc, *args)
    r = _run(nc, [arrays], core_ids=[0])
    return r.results[0]["out_0_dram"]
```
